# Optimizing a Trainium2 kernel written in Bass

```python
import jax, jax.numpy as jnp
from jax import lax
import numpy as np

D_MODEL = 1024
BATCH = 1
SEQ = 128
DEPTH = 2
DEC_BATCH = 1
DEC_SEQ = 256
PAST_LEN = 128

GRID_W = 64
BLOCK = 128
ROPE_THETA = 10000.0
EPS = 1e-6
N_ATT = (DEPTH + 1) // 2
N_SSD = DEPTH // 2
H_A = 8
KVH_A = 2
HD_A = 64
WINDOW = 128
H_B = 8
Q_RANK = 256
KV_RANK = 128
NOPE_B = 64
ROPE_B = 32
V_B = 64
QK_B = NOPE_B + ROPE_B
IN_ATT = H_A * HD_A + 2 * KVH_A * HD_A + Q_RANK + KV_RANK + ROPE_B
OUT_ATT = H_A * HD_A + H_B * V_B
D_INNER = 2 * D_MODEL
P_C = 64
H_C = D_INNER // P_C
G_C = 8
N_C = 128
D_CONV = 5
CHUNK = 128
CONV_CH = D_INNER + 2 * G_C * N_C
IN_SSD = D_INNER + CONV_CH + 2 * H_C
N_GROUPS_E = 4
EXPERTS_PER_GROUP = 8
N_EXPERTS = N_GROUPS_E * EXPERTS_PER_GROUP
TOP_K_E = 2
D_EXPERT = 256

kernel_name = "hybrid_diffusion_prefix_trunk_step"

def rmsnorm(x, g):
    xf = x.astype(jnp.float32)
    y = xf * lax.rsqrt(jnp.mean(xf * xf, axis=-1, keepdims=True) + EPS)
    return (y * g.astype(jnp.float32)).astype(x.dtype)

def adaln(cond, w, b):
    mod = jax.nn.silu(cond) @ w + b
    return jnp.split(mod[:, None, :], 6, axis=-1)

def modulate(x, g, shift, scale):
    return rmsnorm(x, g) * (1 + scale) + shift

def axial_rope(n_tokens, rot_dim):
    rows = n_tokens // GRID_W
    t = jnp.arange(rows * GRID_W)
    row = (t // GRID_W).astype(jnp.float32)
    col = (t % GRID_W).astype(jnp.float32)
    quarter = rot_dim // 4
    inv = ROPE_THETA ** (-jnp.arange(quarter, dtype=jnp.float32) / quarter)
    ar = row[:, None] * inv[None, :]
    ac = col[:, None] * inv[None, :]
    ang = jnp.concatenate([ar, ar, ac, ac], axis=-1)
    return jnp.cos(ang), jnp.sin(ang)

def _rot_half(u):
    u1, u2 = jnp.split(u, 2, axis=-1)
    return jnp.concatenate([-u2, u1], axis=-1)

def apply_axial_rope(x, cos, sin):
    half = x.shape[-1] // 2
    rotated = jnp.concatenate([_rot_half(x[..., :half]), _rot_half(x[..., half:])], axis=-1)
    c = cos[:, None, :].astype(x.dtype)
    s = sin[:, None, :].astype(x.dtype)
    return x * c + rotated * s

def ab_project(h, w_in, a_qnorm, a_knorm, b_qa_norm, b_wuq, b_kva_norm, b_qnorm):
    bsz, L, _ = h.shape
    proj = h @ w_in
    q_a, k_a, v_a, q_lat, ckv, krope = jnp.split(
        proj, [H_A * HD_A, H_A * HD_A + KVH_A * HD_A, H_A * HD_A + 2 * KVH_A * HD_A,
               H_A * HD_A + 2 * KVH_A * HD_A + Q_RANK,
               H_A * HD_A + 2 * KVH_A * HD_A + Q_RANK + KV_RANK], axis=-1)
    q_a = rmsnorm(q_a.reshape(bsz, L, H_A, HD_A), a_qnorm)
    k_a = rmsnorm(k_a.reshape(bsz, L, KVH_A, HD_A), a_knorm)
    v_a = v_a.reshape(bsz, L, KVH_A, HD_A)
    q_b = (rmsnorm(q_lat, b_qa_norm) @ b_wuq).reshape(bsz, L, H_B, QK_B)
    q_b = rmsnorm(q_b, b_qnorm)
    ckv = rmsnorm(ckv, b_kva_norm)
    return q_a, k_a, v_a, q_b, ckv, krope

def mla_keys(ckv, krope, b_wukv, b_knorm):
    bsz, L, _ = ckv.shape
    kv = (ckv @ b_wukv).reshape(bsz, L, H_B, NOPE_B + V_B)
    k_nope, v = kv[..., :NOPE_B], kv[..., NOPE_B:]
    k = jnp.concatenate([k_nope, jnp.broadcast_to(krope[:, :, None, :], (bsz, L, H_B, ROPE_B))], axis=-1)
    return rmsnorm(k, b_knorm), v

def ctx_sink_attention(q, k, v, sink):
    bsz, L, _, _ = q.shape
    grp = H_A // KVH_A
    qg = q.reshape(bsz, L, KVH_A, grp, HD_A)
    s = jnp.einsum('bqkgd,bskd->bkgqs', qg, k).astype(jnp.float32) * HD_A ** -0.5
    sink_col = jnp.broadcast_to(sink.astype(jnp.float32).reshape(1, KVH_A, grp, 1, 1), (bsz, KVH_A, grp, L, 1))
    p = jax.nn.softmax(jnp.concatenate([s, sink_col], axis=-1), axis=-1)[..., :-1].astype(v.dtype)
    o = jnp.einsum('bkgqs,bskd->bqkgd', p, v)
    return o.reshape(bsz, L, H_A * HD_A)

def window_sink_attention(q, k, v, k_ctx, v_ctx, sink):
    bsz, L, _, _ = q.shape
    grp = H_A // KVH_A
    nb = L // BLOCK
    lc = k_ctx.shape[1]
    qb = q.reshape(bsz, nb, BLOCK, KVH_A, grp, HD_A)
    pad = ((0, 0), (BLOCK, BLOCK), (0, 0), (0, 0))
    kp = jnp.pad(k, pad).reshape(bsz, nb + 2, BLOCK, KVH_A, HD_A)
    vp = jnp.pad(v, pad).reshape(bsz, nb + 2, BLOCK, KVH_A, HD_A)
    kband = jnp.concatenate([kp[:, :-2], kp[:, 1:-1], kp[:, 2:]], axis=2)
    vband = jnp.concatenate([vp[:, :-2], vp[:, 1:-1], vp[:, 2:]], axis=2)
    qi = jnp.arange(BLOCK)
    kj = jnp.arange(3 * BLOCK)
    blk = jnp.arange(nb)
    key_pos = blk[:, None] * BLOCK - BLOCK + kj[None, :]
    rel = kj[None, :] - BLOCK - qi[:, None]
    mask = (jnp.abs(rel) <= WINDOW)[None] & ((key_pos >= 0) & (key_pos < L))[:, None, :]
    scale = HD_A ** -0.5
    s_loc = jnp.einsum('bnqkgd,bnskd->bnkgqs', qb, kband).astype(jnp.float32) * scale
    s_loc = jnp.where(mask[None, :, None, None], s_loc, -jnp.inf)
    s_ctx = jnp.einsum('bnqkgd,bskd->bnkgqs', qb, k_ctx).astype(jnp.float32) * scale
    sink_col = jnp.broadcast_to(sink.astype(jnp.float32).reshape(1, 1, KVH_A, grp, 1, 1), (bsz, nb, KVH_A, grp, BLOCK, 1))
    p = jax.nn.softmax(jnp.concatenate([s_ctx, s_loc, sink_col], axis=-1), axis=-1).astype(v.dtype)
    p_ctx = p[..., :lc]
    p_loc = p[..., lc:lc + 3 * BLOCK]
    o = jnp.einsum('bnkgqs,bskd->bnqkgd', p_ctx, v_ctx) + jnp.einsum('bnkgqs,bnskd->bnqkgd', p_loc, vband)
    return o.reshape(bsz, L, H_A * HD_A)

def dense_attention(q, k, v):
    bsz, L, _, _ = q.shape
    s = jnp.einsum('bqhd,bshd->bhqs', q, k).astype(jnp.float32) * QK_B ** -0.5
    p = jax.nn.softmax(s, axis=-1).astype(v.dtype)
    return jnp.einsum('bhqs,bshe->bqhe', p, v).reshape(bsz, L, H_B * V_B)

def mla_latent_attention(q, k, v, k_ctx, v_ctx):
    bsz, L, _, _ = q.shape
    nb = L // BLOCK
    k_all = jnp.concatenate([k_ctx, k], axis=1)
    v_all = jnp.concatenate([v_ctx, v], axis=1)
    qb = jnp.moveaxis(q.reshape(bsz, nb, BLOCK, H_B, QK_B), 1, 0)

    def one_block(qblk):
        s = jnp.einsum('bqhd,bshd->bhqs', qblk, k_all).astype(jnp.float32) * QK_B ** -0.5
        p = jax.nn.softmax(s, axis=-1).astype(v_all.dtype)
        return jnp.einsum('bhqs,bshe->bqhe', p, v_all)

    o = lax.map(one_block, qb)
    return jnp.moveaxis(o, 0, 1).reshape(bsz, L, H_B * V_B)

def att_mixer_context(h, w_in, a_qnorm, a_knorm, a_sink, b_qa_norm, b_wuq, b_kva_norm, b_wukv, b_qnorm, b_knorm, w_out):
    q_a, k_a, v_a, q_b, ckv, krope = ab_project(h, w_in, a_qnorm, a_knorm, b_qa_norm, b_wuq, b_kva_norm, b_qnorm)
    o_a = ctx_sink_attention(q_a, k_a, v_a, a_sink)
    k_b, v_b = mla_keys(ckv, krope, b_wukv, b_knorm)
    o_b = dense_attention(q_b, k_b, v_b)
    out = jnp.concatenate([o_a, o_b], axis=-1) @ w_out
    return out, k_a, v_a, ckv, krope

def att_mixer_latent(h, ka_ctx, va_ctx, ckv_ctx, krope_ctx, w_in, a_qnorm, a_knorm, a_sink, b_qa_norm, b_wuq,
                     b_kva_norm, b_wukv, b_qnorm, b_knorm, w_out):
    L = h.shape[1]
    cos_a, sin_a = axial_rope(L, HD_A)
    cos_b, sin_b = axial_rope(L, ROPE_B)
    q_a, k_a, v_a, q_b, ckv, krope = ab_project(h, w_in, a_qnorm, a_knorm, b_qa_norm, b_wuq, b_kva_norm, b_qnorm)
    q_a = apply_axial_rope(q_a, cos_a, sin_a)
    k_a = apply_axial_rope(k_a, cos_a, sin_a)
    o_a = window_sink_attention(q_a, k_a, v_a, ka_ctx, va_ctx, a_sink)
    k_b, v_b = mla_keys(ckv, krope, b_wukv, b_knorm)
    k_bc, v_bc = mla_keys(ckv_ctx, krope_ctx, b_wukv, b_knorm)
    q_b = jnp.concatenate([q_b[..., :NOPE_B], apply_axial_rope(q_b[..., NOPE_B:], cos_b, sin_b)], axis=-1)
    k_b = jnp.concatenate([k_b[..., :NOPE_B], apply_axial_rope(k_b[..., NOPE_B:], cos_b, sin_b)], axis=-1)
    o_b = mla_latent_attention(q_b, k_b, v_b, k_bc, v_bc)
    return jnp.concatenate([o_a, o_b], axis=-1) @ w_out

def centred_dwconv(u, w, bias):
    ch = u.shape[-1]
    k = w.shape[0]
    out = lax.conv_general_dilated(u, w[:, None, :].astype(u.dtype), window_strides=(1,),
                                   padding=[(k // 2, k // 2)], dimension_numbers=('NWC', 'WIO', 'NWC'),
                                   feature_group_count=ch)
    return out + bias

def ssd_scan(x, dt, a_neg, bm, cm, s0):
    f32 = jnp.float32
    bsz, L, H, P = x.shape
    G, N = bm.shape[2], bm.shape[3]
    R = H // G
    nc = L // CHUNK
    xc = x.astype(f32).reshape(bsz, nc, CHUNK, G, R, P)
    dtc = dt.astype(f32).reshape(bsz, nc, CHUNK, G, R)
    bc = bm.astype(f32).reshape(bsz, nc, CHUNK, G, N)
    cc = cm.astype(f32).reshape(bsz, nc, CHUNK, G, N)
    acs = jnp.cumsum(dtc * a_neg.astype(f32).reshape(G, R), axis=2)
    tri = jnp.tril(jnp.ones((CHUNK, CHUNK), dtype=bool))
    seg = acs[:, :, :, None] - acs[:, :, None, :]
    decay = jnp.exp(jnp.where(tri[:, :, None, None], seg, -jnp.inf))
    cb = jnp.einsum('bcign,bcjgn->bcijg', cc, bc)
    y_intra = jnp.einsum('bcijgr,bcjgrp->bcigrp', cb[..., None] * decay * dtc[:, :, None], xc)
    to_end = jnp.exp(acs[:, :, -1:] - acs) * dtc
    chunk_states = jnp.einsum('bcjgn,bcjgrp->bcgrpn', bc, to_end[..., None] * xc)
    chunk_decay = jnp.exp(acs[:, :, -1])

    def step(s, inp):
        dec, st = inp
        return dec[..., None, None] * s + st, s

    s_fin, s_prev = lax.scan(step, s0.astype(f32).reshape(bsz, G, R, P, N),
                             (jnp.moveaxis(chunk_decay, 1, 0), jnp.moveaxis(chunk_states, 1, 0)))
    s_prev = jnp.moveaxis(s_prev, 0, 1)
    y_inter = jnp.einsum('bcign,bcgrpn->bcigrp', cc, s_prev) * jnp.exp(acs)[..., None]
    y = (y_intra + y_inter).reshape(bsz, L, H, P)
    return y, s_fin.reshape(bsz, H, P, N)

def ssd_mixer(h, s0_f, s0_b, w_in, conv_w, conv_b, alog_f, alog_b, dtb_f, dtb_b, d_skip, norm_w, w_out):
    f32 = jnp.float32
    bsz, L, _ = h.shape
    proj = h @ w_in
    z, xbc, dt_f, dt_b = jnp.split(proj, [D_INNER, D_INNER + CONV_CH, D_INNER + CONV_CH + H_C], axis=-1)
    xbc = jax.nn.silu(centred_dwconv(xbc, conv_w, conv_b))
    xs, bm, cm = jnp.split(xbc, [D_INNER, D_INNER + G_C * N_C], axis=-1)
    xs = xs.reshape(bsz, L, H_C, P_C)
    bm = bm.reshape(bsz, L, G_C, N_C)
    cm = cm.reshape(bsz, L, G_C, N_C)
    dtf = jax.nn.softplus((dt_f + dtb_f).astype(f32))
    dtbk = jax.nn.softplus((dt_b + dtb_b).astype(f32))
    y_f, s_f = ssd_scan(xs, dtf, -jnp.exp(alog_f.astype(f32)), bm, cm, s0_f)
    flip = lambda t: jnp.flip(t, axis=1)
    y_b, s_b = ssd_scan(flip(xs), flip(dtbk), -jnp.exp(alog_b.astype(f32)), flip(bm), flip(cm), s0_b)
    y = y_f + flip(y_b) + d_skip.astype(f32)[:, None] * xs.astype(f32)
    y = y.reshape(bsz, L, D_INNER) * jax.nn.silu(z.astype(f32))
    yg = y.reshape(bsz, L, G_C, D_INNER // G_C)
    yg = yg * lax.rsqrt(jnp.mean(yg * yg, axis=-1, keepdims=True) + EPS)
    y = yg.reshape(bsz, L, D_INNER) * norm_w.astype(f32)
    return y.astype(h.dtype) @ w_out, s_f.astype(h.dtype), s_b.astype(h.dtype)

def hier_moe(h, wg, bg, we, be, w1, w3, w2):
    bsz, L, d = h.shape
    t = h.reshape(-1, d)
    n = t.shape[0]
    p_grp = jax.nn.softmax((t @ wg + bg).astype(jnp.float32), axis=-1)
    p_top, g_idx = lax.top_k(p_grp, 1)
    e_logits = (t @ we + be).astype(jnp.float32).reshape(n, N_GROUPS_E, EXPERTS_PER_GROUP)
    e_in = jnp.take_along_axis(e_logits, g_idx[:, :, None], axis=1)[:, 0]
    w_top, e_idx = lax.top_k(jax.nn.softmax(e_in, axis=-1), TOP_K_E)
    w_top = w_top / jnp.sum(w_top, axis=-1, keepdims=True)
    gate_k = p_top * w_top
    expert_id = g_idx * EXPERTS_PER_GROUP + e_idx
    gates = jnp.sum(jax.nn.one_hot(expert_id, N_EXPERTS, dtype=jnp.float32) * gate_k[..., None], axis=1).astype(h.dtype)
    hid = jax.nn.silu(jnp.einsum('nd,edf->nef', t, w1)) * jnp.einsum('nd,edf->nef', t, w3)
    out = jnp.einsum('nef,efd->nd', hid * gates[:, :, None], w2)
    return out.reshape(bsz, L, d)

def setup_inputs(seed: int = 0) -> dict:
    key = jax.random.key(seed)
    ks = iter(jax.random.split(key, 64))
    f32 = jnp.float32

    def nrm(shape, scale):
        return jax.random.normal(next(ks), shape, f32) * scale

    def gain(shape):
        return 1.0 + nrm(shape, 0.02)

    def dt_bias(shape):
        dt = jnp.exp(jax.random.uniform(next(ks), shape, f32, np.log(1e-3), np.log(1e-1)))
        return dt + jnp.log(-jnp.expm1(-dt))

    inp = {}
    inp["x_prompt"] = nrm((BATCH, SEQ, D_MODEL), 1.0)
    inp["x_sample"] = nrm((DEC_BATCH, DEC_SEQ, D_MODEL), 1.0)
    inp["cache_a_k"] = nrm((DEC_BATCH, N_ATT, PAST_LEN, KVH_A, HD_A), 1.0)
    inp["cache_a_v"] = nrm((DEC_BATCH, N_ATT, PAST_LEN, KVH_A, HD_A), 1.0)
    inp["cache_b_ckv"] = nrm((DEC_BATCH, N_ATT, PAST_LEN, KV_RANK), 1.0)
    inp["cache_b_krope"] = nrm((DEC_BATCH, N_ATT, PAST_LEN, ROPE_B), 1.0)
    inp["state_c_fwd"] = nrm((DEC_BATCH, N_SSD, H_C, P_C, N_C), 0.1)
    inp["state_c_bwd"] = nrm((DEC_BATCH, N_SSD, H_C, P_C, N_C), 0.1)
    inp["c"] = nrm((DEC_BATCH, D_MODEL), 1.0)
    inp["c_ctx"] = nrm((D_MODEL,), 1.0)
    inp["ada_w"] = nrm((DEPTH, D_MODEL, 6 * D_MODEL), 0.5 * D_MODEL ** -0.5)
    inp["ada_b"] = nrm((DEPTH, 6 * D_MODEL), 0.02)
    inp["norm_mix"] = gain((DEPTH, D_MODEL))
    inp["norm_ffn"] = gain((DEPTH, D_MODEL))
    inp["att_w_in"] = nrm((N_ATT, D_MODEL, IN_ATT), D_MODEL ** -0.5)
    inp["att_a_qnorm"] = gain((N_ATT, HD_A))
    inp["att_a_knorm"] = gain((N_ATT, HD_A))
    inp["att_a_sink"] = nrm((N_ATT, H_A), 0.5)
    inp["att_b_qa_norm"] = gain((N_ATT, Q_RANK))
    inp["att_b_wuq"] = nrm((N_ATT, Q_RANK, H_B * QK_B), Q_RANK ** -0.5)
    inp["att_b_kva_norm"] = gain((N_ATT, KV_RANK))
    inp["att_b_wukv"] = nrm((N_ATT, KV_RANK, H_B * (NOPE_B + V_B)), KV_RANK ** -0.5)
    inp["att_b_qnorm"] = gain((N_ATT, QK_B))
    inp["att_b_knorm"] = gain((N_ATT, QK_B))
    inp["att_w_out"] = nrm((N_ATT, OUT_ATT, D_MODEL), OUT_ATT ** -0.5)
    inp["ssd_w_in"] = nrm((N_SSD, D_MODEL, IN_SSD), D_MODEL ** -0.5)
    inp["ssd_conv_w"] = nrm((N_SSD, D_CONV, CONV_CH), D_CONV ** -0.5)
    inp["ssd_conv_b"] = nrm((N_SSD, CONV_CH), 0.02)
    inp["ssd_alog_fwd"] = jnp.log(jax.random.uniform(next(ks), (N_SSD, H_C), f32, 1.0, 16.0))
    inp["ssd_alog_bwd"] = jnp.log(jax.random.uniform(next(ks), (N_SSD, H_C), f32, 1.0, 16.0))
    inp["ssd_dtb_fwd"] = dt_bias((N_SSD, H_C))
    inp["ssd_dtb_bwd"] = dt_bias((N_SSD, H_C))
    inp["ssd_d"] = 1.0 + nrm((N_SSD, H_C), 0.1)
    inp["ssd_norm"] = gain((N_SSD, D_INNER))
    inp["ssd_w_out"] = nrm((N_SSD, D_INNER, D_MODEL), D_INNER ** -0.5)
    inp["moe_wg"] = nrm((DEPTH, D_MODEL, N_GROUPS_E), D_MODEL ** -0.5)
    inp["moe_bg"] = nrm((DEPTH, N_GROUPS_E), 0.01)
    inp["moe_we"] = nrm((DEPTH, D_MODEL, N_EXPERTS), D_MODEL ** -0.5)
    inp["moe_be"] = nrm((DEPTH, N_EXPERTS), 0.01)
    inp["moe_w1"] = nrm((DEPTH, N_EXPERTS, D_MODEL, D_EXPERT), D_MODEL ** -0.5)
    inp["moe_w3"] = nrm((DEPTH, N_EXPERTS, D_MODEL, D_EXPERT), D_MODEL ** -0.5)
    inp["moe_w2"] = nrm((DEPTH, N_EXPERTS, D_EXPERT, D_MODEL), D_EXPERT ** -0.5)
    return inp

def reference(x_prompt, x_sample, cache_a_k, cache_a_v, cache_b_ckv, cache_b_krope, state_c_fwd, state_c_bwd,
              c, c_ctx, ada_w, ada_b, norm_mix, norm_ffn,
              att_w_in, att_a_qnorm, att_a_knorm, att_a_sink, att_b_qa_norm, att_b_wuq, att_b_kva_norm,
              att_b_wukv, att_b_qnorm, att_b_knorm, att_w_out,
              ssd_w_in, ssd_conv_w, ssd_conv_b, ssd_alog_fwd, ssd_alog_bwd, ssd_dtb_fwd, ssd_dtb_bwd, ssd_d,
              ssd_norm, ssd_w_out,
              moe_wg, moe_bg, moe_we, moe_be, moe_w1, moe_w3, moe_w2):
    yp = x_prompt
    ys = x_sample
    new_ak, new_av, new_ckv, new_kr, new_sf, new_sb = [], [], [], [], [], []
    for layer in range(DEPTH):
        sh1_p, sc1_p, g1_p, sh2_p, sc2_p, g2_p = adaln(c_ctx[None, :], ada_w[layer], ada_b[layer])
        sh1_s, sc1_s, g1_s, sh2_s, sc2_s, g2_s = adaln(c, ada_w[layer], ada_b[layer])
        hp = modulate(yp, norm_mix[layer], sh1_p, sc1_p)
        hs = modulate(ys, norm_mix[layer], sh1_s, sc1_s)
        if layer % 2 == 0:
            i = layer // 2
            ap = (att_w_in[i], att_a_qnorm[i], att_a_knorm[i], att_a_sink[i], att_b_qa_norm[i], att_b_wuq[i],
                  att_b_kva_norm[i], att_b_wukv[i], att_b_qnorm[i], att_b_knorm[i], att_w_out[i])
            op, ka, va, ckv, kr = att_mixer_context(hp, *ap)
            os_ = att_mixer_latent(hs, cache_a_k[:, i], cache_a_v[:, i], cache_b_ckv[:, i], cache_b_krope[:, i], *ap)
            new_ak.append(ka)
            new_av.append(va)
            new_ckv.append(ckv)
            new_kr.append(kr)
        else:
            j = layer // 2
            sp = (ssd_w_in[j], ssd_conv_w[j], ssd_conv_b[j], ssd_alog_fwd[j], ssd_alog_bwd[j], ssd_dtb_fwd[j],
                  ssd_dtb_bwd[j], ssd_d[j], ssd_norm[j], ssd_w_out[j])
            zeros = jnp.zeros((yp.shape[0], H_C, P_C, N_C), yp.dtype)
            op, sf, sb = ssd_mixer(hp, zeros, zeros, *sp)
            os_, _, _ = ssd_mixer(hs, state_c_fwd[:, j], state_c_bwd[:, j], *sp)
            new_sf.append(sf)
            new_sb.append(sb)
        yp = yp + g1_p * op
        ys = ys + g1_s * os_
        mp = (moe_wg[layer], moe_bg[layer], moe_we[layer], moe_be[layer], moe_w1[layer], moe_w3[layer], moe_w2[layer])
        yp = yp + g2_p * hier_moe(modulate(yp, norm_ffn[layer], sh2_p, sc2_p), *mp)
        ys = ys + g2_s * hier_moe(modulate(ys, norm_ffn[layer], sh2_s, sc2_s), *mp)
    new_a_k = jnp.stack(new_ak, axis=1)
    new_a_v = jnp.stack(new_av, axis=1)
    new_b_ckv = jnp.stack(new_ckv, axis=1)
    new_b_krope = jnp.stack(new_kr, axis=1)
    new_state_fwd = jnp.stack(new_sf, axis=1)
    new_state_bwd = jnp.stack(new_sb, axis=1)
    return (yp, ys, new_a_k, new_a_v, new_b_ckv, new_b_krope, new_state_fwd, new_state_bwd)


_drawn_inputs = setup_inputs


def setup_inputs(seed=0):
    import zlib

    import numpy as np

    out = dict(_drawn_inputs(seed))
    spreads = {}
    factors = {'cache_a_k': 3.788,
     'cache_a_v': 3.293,
     'cache_b_ckv': 3.886,
     'cache_b_krope': 7.554,
     'att_a_qnorm': 8.0,
     'att_a_sink': 64.0,
     'att_b_qa_norm': 8.0,
     'att_b_kva_norm': 2.992,
     'att_b_qnorm': 8.0,
     'att_b_knorm': 8.0,
     'ssd_d': 3.795,
     'ssd_norm': 68.436,
     'moe_bg': 17.012,
     'moe_be': 21.447,
     'norm_ffn': 5.498}
    for name, (base, spread) in spreads.items():
        noise = np.random.default_rng([zlib.crc32(name.encode()), seed]).standard_normal(out[name].shape)
        drawn = base * np.exp(spread * noise) if base else spread * noise
        out[name] = __import__('jax').numpy.asarray(drawn.astype(out[name].dtype))
    for name, factor in factors.items():
        out[name] = (out[name] * factor).astype(out[name].dtype)
    return out
```

```python
from contextlib import ExitStack

import numpy as np
import concourse.bass as bass
from concourse import mybir

P = 128
D = 1024
KD = D // P
T = 3
NTOK = T * P
F32 = mybir.dt.float32
I32 = mybir.dt.int32
F32R = mybir.dt.float32r
BF16 = mybir.dt.bfloat16
ALU = mybir.AluOpType
ACT = mybir.ActivationFunctionType
AX = mybir.AxisListType
EPS = 1e-6
BIG = 1e30
BANK = 512

HD_A, HD_B, NOPE, ROPE, V_B = 64, 96, 64, 32, 64
IN_ATT = 1184
H_C, P_C, G_C, N_C, D_INNER = 32, 64, 8, 128, 2048
CONV_CH = 4096
R_C = H_C // G_C
NE, NG, PER, FE = 32, 4, 8, 256
SLOTS = 64
PAIRS = NE // 2
ROUNDS = NTOK // SLOTS

SLOT_RING = 4
MIX, FFN = 0, 1


def const_table():
    i = np.arange(P)
    low = (i[None, :] <= i[:, None])
    high = (i[None, :] >= i[:, None])
    cols, at = [], {}

    def put(name, a):
        a = np.broadcast_to(np.asarray(a, np.float32), (P, a.shape[1]))
        at[name] = (sum(c.shape[1] for c in cols), a.shape[1])
        cols.append(a)

    put("ident", np.eye(P))
    put("ones", np.ones((P, P)))
    put("upto", high)
    put("from_", low)
    put("before", i[None, :] > i[:, None])
    put("mask_high", np.where(high, 0.0, -BIG))
    put("mask_low", np.where(low, 0.0, -BIG))
    put("slot_no", np.arange(SLOTS)[None, :])
    put("rank32", np.arange(NE, 0, -1)[None, :])
    put("rank4", np.arange(NG, 0, -1)[None, :])
    pick = np.zeros((P, 2 * P), np.float32)
    pick[0, 0:P] = 1
    pick[1, P:] = 1
    put("pick", pick)
    put("sum4", np.stack([(i % 32 == g) for g in range(2)], axis=1))
    tok = np.arange(2 * P)
    for name, rot in (("a", HD_A), ("b", ROPE)):
        quarter = rot // 4
        inv = np.float32(10000.0) ** (-np.arange(quarter, dtype=np.float32) / np.float32(quarter))
        ar = (tok // 64).astype(np.float32)[:, None] * inv[None, :]
        ac = (tok % 64).astype(np.float32)[:, None] * inv[None, :]
        ang = np.concatenate([ar, ar, ac, ac], axis=1).astype(np.float32)
        sign = np.repeat(np.array([-1, 1, -1, 1], np.float32), quarter)
        cos, sin = np.cos(ang), np.sin(ang) * sign[None, :]
        put("cos_" + name, cos.reshape(2, P, rot).transpose(1, 0, 2).reshape(P, 2 * rot))
        put("sin_" + name, sin.reshape(2, P, rot).transpose(1, 0, 2).reshape(P, 2 * rot))
    return np.ascontiguousarray(np.concatenate(cols, axis=1)), at


class Shared:
    pass


def stream_plan(w):
    plan, at = [], {}

    def add(stage, key, *moves):
        at[stage, key] = len(plan)
        plan.append(moves)

    def cols(a, c0, n, k0=0):
        return (lambda slot: slot[:, :, 0:n] if n == BANK else slot[:, :, 0:n],
                a[:, k0:k0 + KD, c0:c0 + n])

    for l in range(2):
        ada = w["ada_w"][l].rearrange("(p k) n -> p k n", k=KD)
        for j in range(12):
            add(("ada", l), j, cols(ada, j * BANK, BANK))
        if l == 0:
            win = w["att_w_in"][0].rearrange("(p k) n -> p k n", k=KD)
            for j, n in enumerate((512, 512, 160)):
                add("att_in", j, cols(win, j * BANK, n))
            wuq = w["att_b_wuq"][0].rearrange("(k p) n -> p k n", p=P)
            wukv = w["att_b_wukv"][0]
            add("att_up", 0,
                (lambda s: s.rearrange("p k n -> p (k n)")[:, 0:1536].rearrange("p (k n) -> p k n", k=2), wuq),
                (lambda s: s.rearrange("p k n -> p (k n)")[:, 1536:2560], wukv))
            wout = w["att_w_out"][0].rearrange("(p k) n -> p k n", k=KD)
            for j in range(2):
                add("att_out", j, cols(wout, j * BANK, BANK))
        else:
            win = w["ssd_w_in"][0].rearrange("(p k) n -> p k n", k=KD)
            for j in range(8):
                add("ssd_xbc", j, cols(win, D_INNER + j * BANK, BANK))
            add("ssd_dt", 0, cols(win, D_INNER + CONV_CH, 2 * H_C))
            for j in range(4):
                add("ssd_z", j, cols(win, j * BANK, BANK))
            wout = w["ssd_w_out"][0].rearrange("(k p) n -> p k n", p=P)
            for j in range(2):
                for kh in range(2):
                    add("ssd_out", (j, kh), cols(wout, j * BANK, BANK, kh * KD))
        at["moe", l] = len(plan)
        for e in range(SLOT_RING):
            plan.append(tuple((lambda slot, c=c: slot[:, :, c:c + FE], w[name][l, e].rearrange("(p k) f -> p k f", k=KD))
                              for name, c in (("moe_w1", 0), ("moe_w3", FE))))
        plan.extend([None] * (NE - SLOT_RING))
    return plan, at


def build(nc, w, out):
    ctx = ExitStack()
    s = Shared()
    with ctx:
        def sb(name, shape, dt=F32):
            return ctx.enter_context(nc.sbuf_tensor(name, shape, dt))

        def sem(name):
            return ctx.enter_context(nc.semaphore(name))

        s.nc, s.w, s.out = nc, w, out
        s.ps = ctx.enter_context(nc.psum_tensor("ps", [P, 8, BANK], F32))
        s.y = sb("y", [P, T, D])
        s.hT = sb("hT", [P, KD, NTOK])
        s.ring = sb("ring", [P, SLOT_RING, KD, BANK])
        s.gates = sb("gates", [2, 2, D])
        s.shift = sb("shift", [P, 2, KD, 2])
        s.gain = sb("gain", [P, 2, KD, 2])
        _, s.cat = const_table()
        s.consts = sb("consts", [P, w["consts"].shape[1]])
        s.cid = lambda name: s.consts[:, s.cat[name][0]:s.cat[name][0] + s.cat[name][1]]
        s.ident = s.cid("ident")
        s.ring_full = [sem(f"ring_full{n}") for n in range(SLOT_RING)]
        s.ring_free = sem("ring_free")
        s.plan, s.at = stream_plan(w)
        s.fill_of = fill_counts(s)
        s.issued = 0
        s.loads = sem("loads")
        s.loaded = 0
        s.stores = sem("stores")
        s.stored = 0
        s.chain = {e: sem(f"chain_{e}") for e in ("dve", "act")}
        s.chained = {"dve": 0, "act": 0}

        for l in range(2):
            layer = ctx.enter_context(ExitStack())
            own = []

            def layer_sem(name, layer=layer, own=own):
                own.append(layer.enter_context(nc.semaphore(name)))
                return own[-1]

            s.sem = layer_sem
            with ExitStack() as st:
                ada_stage(s, l, st)
            with ExitStack() as st:
                norm_stage(s, l, MIX, st)
            if l == 0:
                with ExitStack() as st:
                    attention(s, st)
            else:
                with ExitStack() as st:
                    ssd(s, st)
            with ExitStack() as st:
                moe(s, l, st)
            if l == 0:
                with nc.Block() as block:
                    @block.gpsimd
                    def _(pool):
                        for one in own:
                            pool.sem_clear(one)
                layer.close()
        store_y(s)


def link(s, name, eng, ins):
    s.chained[name] += 1
    ins.then_inc(s.chain[name], 1)
    eng.wait_ge(s.chain[name], s.chained[name])


def ring_loads(s, sp, upto):
    while s.issued < min(upto, len(s.plan)):
        n = s.issued
        if s.plan[n] is None:
            break
        if n >= SLOT_RING:
            sp.wait_ge(s.ring_free, n - SLOT_RING + 1)
        slot = s.ring[:, n % SLOT_RING]
        for part, src in s.plan[n]:
            sp.dma_start(part(slot), src).then_inc(s.ring_full[n % SLOT_RING], 16)
        s.issued += 1


def fill_counts(s):
    total, out = [0] * SLOT_RING, []
    for n, moves in enumerate(s.plan):
        total[n % SLOT_RING] += 16 * (2 if moves is None else len(moves))
        out.append(total[n % SLOT_RING])
    return out


def ring_wait(s, pe, n):
    pe.wait_ge(s.ring_full[n % SLOT_RING], s.fill_of[n])


def stage_buffers(s, st, prefix):
    def sb(name, shape, dt=F32):
        return st.enter_context(s.nc.sbuf_tensor(prefix + name, shape, dt))
    return sb


def ada_stage(s, l, st):
    nc, w, ps = s.nc, s.w, s.ps
    sb = stage_buffers(s, st, f"ada{l}_")
    cond = sb("cond", [P, 2, KD])
    silu_c = sb("silu_c", [P, KD, 32])
    part = sb("part", [P, 2, BANK])
    bias = sb("bias", [2, 6 * D])
    row = sb("row", [2, 6 * D])
    norm_g = sb("norm_g", [P, 2, KD])
    mod_t = sb("mod_t", [P, 4, KD, 2])
    silu_ready, col_ps, col_done, t_ps = (s.sem(f"ada{l}_{x}") for x in ("silu", "col_ps", "col_done", "t_ps"))
    zero, part_ev, sum_ps = (s.sem(f"ada{l}_{x}") for x in ("zero", "part_ev", "sum_ps"))
    base = s.at[("ada", l), 0]
    block = st.enter_context(nc.Block())

    @block.sync
    def _(sp):
        n = 0
        loads = [(cond[:, 0, :], w["c_ctx"].rearrange("(p k) -> p k", k=KD)),
                 (cond[:, 1, :], w["c"][0].rearrange("(p k) -> p k", k=KD)),
                 (norm_g[:, 0, :], w["norm_mix"][l].rearrange("(p k) -> p k", k=KD)),
                 (norm_g[:, 1, :], w["norm_ffn"][l].rearrange("(p k) -> p k", k=KD)),
                 (bias[0:1, :], w["ada_b"][l:l + 1, :]),
                 (bias[1:2, :], w["ada_b"][l:l + 1, :])]
        if l == 0:
            loads += [(s.consts[:, :], w["consts"]),
                      (s.y[:, 0, :], w["x_prompt"][0]),
                      (s.y[:, 1:3, :], w["x_sample"][0].rearrange("(t p) d -> p t d", p=P))]
        for dst, src in loads:
            sp.dma_start(dst, src).then_inc(s.loads, 16)
            n += 16
        s.loaded += n
        ring_loads(s, sp, base + 12 + SLOT_RING)

    @block.scalar
    def _(act):
        act.wait_ge(zero, 1)
        act.wait_ge(s.loads, s.loaded)
        nc.scalar.activation(silu_c[:, :, 0:2].rearrange("p k g -> p g k"), cond[:, :, :], ACT.Silu).then_inc(silu_ready, 1)
        for j in range(12):
            act.wait_ge(s.ring_free, base + j + 1)
            if j >= 2:
                act.wait_ge(sum_ps, j - 1)
            nc.scalar.copy(part[:, j % 2, :], ps[:, j % 2, :]).then_inc(part_ev, 1)

    @block.tensor
    def _(pe):
        pe.wait_ge(silu_ready, 1)

        def add_up(j):
            pe.wait_ge(part_ev, j + 1)
            if j >= 2:
                pe.wait_ge(col_done, j - 1)
            pe.matmul(ps[0:2, 3 + j % 2, :], s.cid("sum4"), part[:, j % 2, :], start=True, stop=True).then_inc(sum_ps, 1)

        for j in range(12):
            ring_wait(s, pe, base + j)
            if j >= 2:
                pe.wait_ge(part_ev, j - 1)
            for k in range(KD):
                c = 32 * (k % 4)
                mm = pe.matmul(ps[c:c + 32, j % 2, :], silu_c[:, k, :], s.ring[:, (base + j) % SLOT_RING, k, :],
                               start=(k < 4), stop=(k >= 4))
            mm.then_inc(s.ring_free, 1)
            if j:
                add_up(j - 1)
        add_up(11)
        pe.wait_ge(col_done, 12)
        pe.wait_ge(s.loads, s.loaded)
        for qi, q in enumerate((0, 1, 3, 4)):
            for k in range(KD):
                c = (qi * KD + k) * 2
                mm = pe.transpose(ps[:, 2, c:c + 2], row[0:2, q * D + k:(q + 1) * D:KD], s.ident[0:2, 0:2])
        mm.then_inc(t_ps, 1)

    @block.vector
    def _(dve):
        nc.vector.memset(silu_c[:, :, :], 0.0).then_inc(zero, 1)
        dve.wait_ge(s.loads, s.loaded)
        for j in range(12):
            dve.wait_ge(sum_ps, j + 1)
            q, h = divmod(j, 2)
            dst = s.gates[:, q // 3, h * BANK:(h + 1) * BANK] if q in (2, 5) else row[:, j * BANK:(j + 1) * BANK]
            nc.vector.tensor_tensor(dst, ps[0:2, 3 + j % 2, :], bias[:, j * BANK:(j + 1) * BANK], ALU.add).then_inc(col_done, 1)
        dve.wait_ge(t_ps, 1)
        link(s, "dve", dve, nc.vector.tensor_copy(mod_t[:, :, :, :].rearrange("p q k g -> p (q k g)"), ps[:, 2, 0:4 * KD * 2]))
        for m in (MIX, FFN):
            link(s, "dve", dve, nc.vector.tensor_copy(s.shift[:, m, :, :], mod_t[:, 2 * m, :, :]))
            g = norm_g[:, m, :].unsqueeze(2).broadcast_to([P, KD, 2])
            link(s, "dve", dve, nc.vector.scalar_tensor_tensor(
                out=s.gain[:, m, :, :], in0=mod_t[:, 2 * m + 1, :, :], scalar=1.0, in1=g, op0=ALU.add, op1=ALU.mult))


def rsqrt_act(s, act, x, r0, x_ready, x_count, r0_ready):
    act.wait_ge(x_ready, x_count)
    link(s, "act", act, s.nc.scalar.activation(r0, x, ACT.Ln))
    s.nc.scalar.activation(r0, r0, ACT.Exp, scale=-0.5).then_inc(r0_ready, 1)


def rsqrt_dve(s, dve, x, r0, tmp, r0_ready, count):
    v = s.nc.vector
    dve.wait_ge(r0_ready, count)
    link(s, "dve", dve, v.tensor_tensor(tmp, r0, r0, ALU.mult))
    link(s, "dve", dve, v.tensor_tensor(tmp, tmp, x, ALU.mult))
    link(s, "dve", dve, v.tensor_scalar(tmp, tmp, -0.5, 1.5, ALU.mult, ALU.add))
    link(s, "dve", dve, v.tensor_tensor(r0, r0, tmp, ALU.mult))


def norm_stage(s, l, m, st, hp=None):
    nc, ps = s.nc, s.ps
    pre = f"n{l}{m}_"
    sb = stage_buffers(s, st, pre)
    sq = sb("sq", [P, D])
    ss = sb("ss", [P, T])
    x = sb("x", [P, T])
    r = sb("r", [P, T])
    tmp = sb("tmp", [P, T])
    hn = hp if hp is not None else sb("hn", [P, T, KD, P])
    ss_ready, x_ready, r_ready, hn_ready, t_ps, ev_a, ev_d, b_ps = (
        s.sem(pre + n) for n in ("ss", "x", "r", "hn", "t_ps", "ev_a", "ev_d", "b_ps"))
    block = st.enter_context(nc.Block())

    @block.scalar
    def _(act):
        for t in range(T):
            if t:
                act.wait_ge(ss_ready, t)
            nc.scalar.activation(sq[:, :], s.y[:, t, :], ACT.Square, accum_out=ss[:, t:t + 1]).then_inc(ss_ready, 1)
        rsqrt_act(s, act, x[:, :], r[:, :], x_ready, 1, r_ready)
        for t in range(T):
            act.wait_ge(t_ps, t + 1)
            for k in range(4, KD):
                nc.scalar.activation(s.hT[:, k, t * P:(t + 1) * P], ps[:, 2 * t + 1, (k - 4) * P:(k - 3) * P], ACT.Identity,
                                     scale=s.gain[:, m, k, min(t, 1):min(t, 1) + 1],
                                     bias=s.shift[:, m, k, min(t, 1):min(t, 1) + 1]).then_inc(ev_a, 1)

    @block.vector
    def _(dve):
        dve.wait_ge(ss_ready, T)
        nc.vector.tensor_scalar(x[:, :], ss[:, :], 1.0 / D, EPS, ALU.mult, ALU.add).then_inc(x_ready, 1)
        rsqrt_dve(s, dve, x[:, :], r[:, :], tmp[:, :], r_ready, 1)
        for t in range(T):
            nc.vector.tensor_scalar(hn[:, t, :, :], s.y[:, t, :].rearrange("n (p k) -> n k p", k=KD),
                                    r[:, t:t + 1], None, ALU.mult).then_inc(hn_ready, 1)
        for t in range(T):
            dve.wait_ge(t_ps, t + 1)
            for k in range(4):
                g = min(t, 1)
                nc.vector.tensor_scalar(s.hT[:, k, t * P:(t + 1) * P], ps[:, 2 * t, k * P:(k + 1) * P],
                                        s.gain[:, m, k, g:g + 1], s.shift[:, m, k, g:g + 1],
                                        ALU.mult, ALU.add).then_inc(ev_d, 1)
        if hp is not None:
            for t in range(T):
                dve.wait_ge(b_ps, t + 1)
                nc.vector.tensor_copy(hp[:, t, :, :].rearrange("n k p -> n (k p)"),
                                      ps[:, 2 * t:2 * t + 2, :].rearrange("n b c -> n (b c)")).then_inc(hn_ready, 1)

    @block.tensor
    def _(pe):
        for t in range(T):
            pe.wait_ge(hn_ready, t + 1)
            for k in range(KD):
                mm = pe.transpose(ps[:, 2 * t + k // 4, (k % 4) * P:(k % 4 + 1) * P], hn[:, t, k, :], s.ident)
            mm.then_inc(t_ps, 1)
        if hp is not None:
            for t in range(T):
                pe.wait_ge(ev_a, 4 * (t + 1))
                pe.wait_ge(ev_d, 4 * (t + 1))
                for k in range(KD):
                    mm = pe.transpose(ps[:, 2 * t + k // 4, (k % 4) * P:(k % 4 + 1) * P],
                                      s.hT[:, k, t * P:(t + 1) * P], s.ident)
                mm.then_inc(b_ps, 1)


def store_y(s):
    nc = s.nc
    with nc.Block() as block:
        @block.sync
        def _(sp):
            sp.dma_start(s.out["y_prompt"][0], s.y[:, 0, :]).then_inc(s.stores, 16)
            sp.dma_start(s.out["y_sample"][0].rearrange("(t p) d -> p t d", p=P), s.y[:, 1:3, :]).then_inc(s.stores, 16)
            s.stored += 32
            sp.wait_ge(s.stores, s.stored)


NTB = 7


def attention(s, st):
    att_tiles = ExitStack()
    sb = stage_buffers(s, st, "att_")
    qk_t = sb("qk_t", [P, T, 4, P])
    k_t = sb("k_t", [P, 4, P])
    v_a = sb("v_a", [P, 4, P])
    qkb_t = sb("qkb_t", [HD_B, 8, NTB, P])
    v_b = sb("v_b", [P, 4, 8, V_B])
    small = sb("small", [P, 8])
    with att_tiles:
        att_project(s, att_tiles, qk_t, k_t, v_a, qkb_t, v_b, small)
    with ExitStack() as st2:
        att_scores(s, st2, qk_t, k_t, v_a, qkb_t, v_b, small)


def att_project(s, st, qk_t, k_t, v_a, qkb_t, v_b, sink):
    nc, w, ps, out = s.nc, s.w, s.ps, s.out
    sb = stage_buffers(s, st, "prj_")
    proj = sb("proj", [P, T, IN_ATT])
    heads = sb("heads", [P, T, 10, 64])
    cache_k = sb("cache_k", [P, P])
    cache_c = sb("cache_c", [P, P])
    cache_r = sb("cache_r", [P, ROPE])
    q_gain, k_gain = sb("q_gain", [P, 64]), sb("k_gain", [P, 64])
    qa_gain, kva_gain = sb("qa_gain", [P, 256]), sb("kva_gain", [P, P])
    b_gain = sb("b_gain", [P, 2, HD_B])
    lat_t = sb("lat_t", [P, 2, NTOK])
    ckv_t = sb("ckv_t", [P, 4 * P])
    qkb = sb("qkb", [P, NTB, 8, HD_B])
    ss = sb("ss", [P, T, 12])
    x, r, tmp = sb("x", [P, T * 12]), sb("r", [P, T * 12]), sb("tmp", [P, T * 12])
    ssb = sb("ssb", [P, NTB * 8])
    xb, rb, tmpb = sb("xb", [P, NTB * 8]), sb("rb", [P, NTB * 8]), sb("tmpb", [P, NTB * 8])
    sq = s.hT[:, :, :].rearrange("p k n -> p (k n)")
    rot = sb("rot", [P, 8, 64])
    names = ("in_ps", "in_a", "in_d", "norm_x", "norm_r", "heads_ready", "lat_ready", "ta_ps", "ta_ev",
             "tl_ps", "tl_ev", "up_ps", "up_a", "up_d", "b_x", "b_r", "b_ready", "tb_ps", "tb_ev", "sq_a")
    S = {n: s.sem("prj_" + n) for n in names}
    in0, up0 = s.at["att_in", 0], s.at["att_up", 0]
    widths = (512, 512, 160)
    slot = [s.ring[:, (in0 + j) % SLOT_RING] for j in range(3)]
    up = s.ring[:, up0 % SLOT_RING].rearrange("p k n -> p (k n)")
    wuq = up[:, 0:1536].rearrange("p (k n) -> p k n", k=2)
    wukv = up[:, 1536:2560]
    block = st.enter_context(nc.Block())

    @block.sync
    def _(sp):
        loads = [(cache_k[:, :], w["cache_a_k"][0, 0].rearrange("n h d -> n (h d)")),
                 (v_a[:, 3, :], w["cache_a_v"][0, 0].rearrange("n h d -> n (h d)")),
                 (cache_c[:, :], w["cache_b_ckv"][0, 0]),
                 (cache_r[:, :], w["cache_b_krope"][0, 0]),
                 (q_gain[:, :], w["att_a_qnorm"][0].partition_broadcast(P)),
                 (k_gain[:, :], w["att_a_knorm"][0].partition_broadcast(P)),
                 (qa_gain[:, :], w["att_b_qa_norm"][0].partition_broadcast(P)),
                 (kva_gain[:, :], w["att_b_kva_norm"][0].partition_broadcast(P)),
                 (b_gain[:, 0, :], w["att_b_qnorm"][0].partition_broadcast(P)),
                 (b_gain[:, 1, :], w["att_b_knorm"][0].partition_broadcast(P)),
                 (sink[:, :], w["att_a_sink"][0].partition_broadcast(P))]
        for dst, src in loads:
            sp.dma_start(dst, src).then_inc(s.loads, 16)
        s.loaded += 16 * len(loads)
        ring_loads(s, sp, up0 + 1 + SLOT_RING)
        sp.wait_ge(S["in_a"], 5)
        sp.wait_ge(S["in_d"], 4)
        sp.dma_start(out["new_a_v"][0, 0].rearrange("n h d -> n (h d)"), proj[:, 0, 640:768]).then_inc(s.stores, 16)
        sp.dma_start(out["new_b_krope"][0, 0], proj[:, 0, 1152:1184]).then_inc(s.stores, 16)
        sp.wait_ge(S["heads_ready"], 1)
        sp.dma_start(out["new_a_k"][0, 0], heads[:, 0, 8:10, :]).then_inc(s.stores, 16)
        sp.wait_ge(S["lat_ready"], 1)
        sp.dma_start(out["new_b_ckv"][0, 0], proj[:, 0, 1024:1152]).then_inc(s.stores, 16)
        s.stored += 64
        sp.wait_ge(s.stores, s.stored)

    units = [(c, t) for c in range(3) for t in range(T)]

    @block.tensor
    def _(pe):
        for n, (c, t) in enumerate(units):
            if t == 0:
                ring_wait(s, pe, in0 + c)
            if n >= 8:
                pe.wait_ge(S["in_a"], 1)
            for k in range(KD):
                mm = pe.matmul(ps[:, n % 8, 0:widths[c]], s.hT[:, k, t * P:(t + 1) * P], slot[c][:, k, 0:widths[c]],
                               start=(k == 0), stop=(k == KD - 1))
            mm.then_inc(S["in_ps"], 1)
            if t == T - 1:
                pe.wait_ge(S["in_ps"], n + 1)
                pe.sem_inc(s.ring_free, 1)
        pe.wait_ge(S["in_a"], 5)
        pe.wait_ge(S["in_d"], 4)
        pe.wait_ge(S["lat_ready"], 1)
        pe.wait_ge(s.loads, s.loaded)
        for t in range(T):
            for c in range(2):
                mm = pe.transpose(ps[:, c, t * P:(t + 1) * P], proj[:, t, 768 + c * P:768 + (c + 1) * P], s.ident)
            mm = pe.transpose(ps[:, 2, t * P:(t + 1) * P], proj[:, t, 1024:1152], s.ident)
        mm = pe.transpose(ps[:, 2, 3 * P:4 * P], cache_c[:, :], s.ident)
        mm.then_inc(S["tl_ps"], 1)
        pe.wait_ge(S["tl_ev"], 1)
        ring_wait(s, pe, up0)
        for n in range(NTB):
            b = 4 + 2 * (n % 2)
            if n >= 2:
                pe.wait_ge(S["up_d"], n - 1)
            if n < T:
                for h in range(2):
                    for k in range(2):
                        mm = pe.matmul(ps[:, b + h, 0:384], lat_t[:, k, n * P:(n + 1) * P], wuq[:, k, h * 384:(h + 1) * 384],
                                       start=(k == 0), stop=(k == 1))
            else:
                for h in range(2):
                    mm = pe.matmul(ps[:, b + h, :], ckv_t[:, (n - T) * P:(n - T + 1) * P], wukv[:, h * BANK:(h + 1) * BANK],
                                   start=True, stop=True)
            mm.then_inc(S["up_ps"], 1)
        pe.wait_ge(S["up_ps"], NTB)
        pe.sem_inc(s.ring_free, 1)
        pe.wait_ge(S["heads_ready"], 2)
        for t in range(T):
            for j in range(4):
                pe.transpose(ps[:, t, j * P:(j + 1) * P], heads[:, t, 2 * j:2 * j + 2, :].rearrange("n a d -> n (a d)"), s.ident)
            mm = pe.transpose(ps[:, 3, t * P:(t + 1) * P], heads[:, t, 8:10, :].rearrange("n a d -> n (a d)"), s.ident)
        mm = pe.transpose(ps[:, 3, 3 * P:4 * P], cache_k[:, :], s.ident)
        mm.then_inc(S["ta_ps"], 1)
        pe.wait_ge(S["up_d"], NTB)
        for n in range(NTB):
            b = 4 + 2 * (n % 2)
            if n >= 2:
                pe.wait_ge(S["tb_ev"], n - 1)
            if n == 0:
                pe.wait_ge(S["b_ready"], 1)
            for h in range(8):
                mm = pe.transpose(ps[0:HD_B, b + h // 4, (h % 4) * P:(h % 4 + 1) * P], qkb[:, n, h, :], s.ident)
            mm.then_inc(S["tb_ps"], 1)

    @block.scalar
    def _(act):
        for n, (c, t) in enumerate(units):
            if n % 2 == 0:
                act.wait_ge(S["in_ps"], n + 1)
                nc.scalar.copy(proj[:, t, c * BANK:c * BANK + widths[c]], ps[:, n % 8, 0:widths[c]]).then_inc(S["in_a"], 1)
        rsqrt_act(s, act, x[:, :], r[:, :], S["norm_x"], 1, S["norm_r"])
        act.wait_ge(S["tl_ps"], 1)
        link(s, "act", act, nc.scalar.copy(lat_t[:, :, :], ps[:, 0:2, 0:NTOK]))
        nc.scalar.copy(ckv_t[:, :], ps[:, 2, :]).then_inc(S["tl_ev"], 1)
        act.wait_ge(S["ta_ps"], 1)
        nc.scalar.copy(qk_t[:, :, :, :].rearrange("p t j n -> p (t j n)"), ps[:, 0:3, :].rearrange("p b n -> p (b n)")).then_inc(S["ta_ev"], 1)
        nc.scalar.copy(k_t[:, :, :].rearrange("p t n -> p (t n)"), ps[:, 3, :]).then_inc(S["ta_ev"], 1)
        rsqrt_act(s, act, xb[:, :], rb[:, :], S["b_x"], 1, S["b_r"])
        for n in range(NTB):
            b = 4 + 2 * (n % 2)
            act.wait_ge(S["tb_ps"], n + 1)
            nc.scalar.copy(qkb_t[:, :, n, :], ps[0:HD_B, b:b + 2, :].rearrange("p b (h n) -> p (b h) n", h=4)).then_inc(S["tb_ev"], 1)

    @block.vector
    def _(dve):
        v = nc.vector
        for n, (c, t) in enumerate(units):
            if n % 2 == 1:
                dve.wait_ge(S["in_ps"], n + 1)
                v.tensor_copy(proj[:, t, c * BANK:c * BANK + widths[c]], ps[:, n % 8, 0:widths[c]]).then_inc(S["in_d"], 1)
        dve.wait_ge(S["in_a"], 5)
        dve.wait_ge(S["in_d"], 4)
        dve.wait_ge(s.loads, s.loaded)
        for t in range(T):
            link(s, "dve", dve, v.tensor_tensor(sq[:, 0:640], proj[:, t, 0:640], proj[:, t, 0:640], ALU.mult))
            link(s, "dve", dve, v.tensor_tensor(sq[:, 640:1024], proj[:, t, 768:1152], proj[:, t, 768:1152], ALU.mult))
            link(s, "dve", dve, v.tensor_reduce(ss[:, t, 0:10], sq[:, 0:640].rearrange("p (h d) -> p h d", d=64), AX.X, ALU.add))
            link(s, "dve", dve, v.tensor_reduce(ss[:, t, 10:11], sq[:, 640:896], AX.X, ALU.add))
            link(s, "dve", dve, v.tensor_reduce(ss[:, t, 11:12], sq[:, 896:1024], AX.X, ALU.add))
        x3 = x[:, :].rearrange("p (t h) -> p t h", t=T)
        link(s, "dve", dve, v.tensor_scalar(x3[:, :, 0:10], ss[:, :, 0:10], 1.0 / 64, EPS, ALU.mult, ALU.add))
        link(s, "dve", dve, v.tensor_scalar(x3[:, :, 10:11], ss[:, :, 10:11], 1.0 / 256, EPS, ALU.mult, ALU.add))
        v.tensor_scalar(x3[:, :, 11:12], ss[:, :, 11:12], 1.0 / P, EPS, ALU.mult, ALU.add).then_inc(S["norm_x"], 1)
        rsqrt_dve(s, dve, x[:, :], r[:, :], tmp[:, :], S["norm_r"], 1)
        r3 = r[:, :].rearrange("p (t h) -> p t h", t=T)
        for t in range(T):
            link(s, "dve", dve, v.scalar_tensor_tensor(out=proj[:, t, 768:1024], in0=proj[:, t, 768:1024], scalar=r3[:, t, 10:11],
                                                       in1=qa_gain[:, :], op0=ALU.mult, op1=ALU.mult))
            ins = v.scalar_tensor_tensor(out=proj[:, t, 1024:1152], in0=proj[:, t, 1024:1152], scalar=r3[:, t, 11:12],
                                         in1=kva_gain[:, :], op0=ALU.mult, op1=ALU.mult)
        ins.then_inc(S["lat_ready"], 1)
        for t in range(T):
            q_in = proj[:, t, 0:512].rearrange("p (v j d) -> p j v d", v=2, j=4)
            q_out = heads[:, t, 0:8, :].rearrange("p (j v) d -> p j v d", j=4)
            for kv in range(2):
                rr = r3[:, t, 4 * kv:4 * kv + 4].unsqueeze(2).broadcast_to([P, 4, 64])
                link(s, "dve", dve, v.tensor_tensor(q_out[:, :, kv, :], q_in[:, :, kv, :], rr, ALU.mult))
            rk = r3[:, t, 8:10].unsqueeze(2).broadcast_to([P, 2, 64])
            link(s, "dve", dve, v.tensor_tensor(heads[:, t, 8:10, :], proj[:, t, 512:640].rearrange("p (v d) -> p v d", v=2), rk, ALU.mult))
            link(s, "dve", dve, v.tensor_copy(v_a[:, t, :], proj[:, t, 640:768]))
            link(s, "dve", dve, v.tensor_tensor(heads[:, t, 0:8, :], heads[:, t, 0:8, :], q_gain[:, :].unsqueeze(1).broadcast_to([P, 8, 64]), ALU.mult))
            ins = v.tensor_tensor(heads[:, t, 8:10, :], heads[:, t, 8:10, :], k_gain[:, :].unsqueeze(1).broadcast_to([P, 2, 64]), ALU.mult)
            if t == 0:
                ins.then_inc(S["heads_ready"], 1)
            else:
                link(s, "dve", dve, ins)
                ins = rope(s, dve, heads[:, t], "a", t - 1, 10, rot_pool(sq, 640))
                if t == T - 1:
                    ins.then_inc(S["heads_ready"], 1)
                else:
                    link(s, "dve", dve, ins)
        dve.wait_ge(S["tl_ps"], 1)
        for n in range(NTB):
            b = 4 + 2 * (n % 2)
            dve.wait_ge(S["up_ps"], n + 1)
            if n < T:
                ins = v.tensor_copy(qkb[:, n, :, :].rearrange("p (b h) d -> p b (h d)", b=2), ps[:, b:b + 2, 0:384])
            else:
                kv = ps[:, b:b + 2, :].rearrange("p b (h d) -> p (b h) d", h=4)
                link(s, "dve", dve, v.tensor_copy(v_b[:, n - T, :, :], kv[:, :, 64:128]))
                rope_src = (proj[:, n - T, 1152:1184] if n < NTB - 1 else cache_r[:, :]).unsqueeze(1).broadcast_to([P, 8, ROPE])
                link(s, "dve", dve, v.tensor_copy(qkb[:, n, :, 64:96], rope_src))
                ins = v.tensor_copy(qkb[:, n, :, 0:64], kv[:, :, 0:64])
            ins.then_inc(S["up_d"], 1)
            dve.wait_ge(S["up_d"], n + 1)
            sqn = sq[:, 0:768]
            flat = qkb[:, n, :, :].rearrange("p h d -> p (h d)")
            link(s, "dve", dve, v.tensor_tensor(sqn, flat, flat, ALU.mult))
            link(s, "dve", dve, v.tensor_reduce(ssb[:, 8 * n:8 * n + 8], sqn.rearrange("p (h d) -> p h d", h=8), AX.X, ALU.add))
        v.tensor_scalar(xb[:, :], ssb[:, :], 1.0 / HD_B, EPS, ALU.mult, ALU.add).then_inc(S["b_x"], 1)
        rsqrt_dve(s, dve, xb[:, :], rb[:, :], tmpb[:, :], S["b_r"], 1)
        for n in range(NTB):
            rr = rb[:, 8 * n:8 * n + 8].unsqueeze(2).broadcast_to([P, 8, HD_B])
            g = b_gain[:, 0 if n < T else 1, :].unsqueeze(1).broadcast_to([P, 8, HD_B])
            link(s, "dve", dve, v.tensor_tensor(qkb[:, n, :, :], qkb[:, n, :, :], rr, ALU.mult))
            ins = v.tensor_tensor(qkb[:, n, :, :], qkb[:, n, :, :], g, ALU.mult)
            if n in (1, 2, 4, 5):
                link(s, "dve", dve, ins)
                ins = rope(s, dve, qkb[:, n, :, 64:96], "b", (n % 3) - 1, 8, rot_pool(sq, 256))
            if n < NTB - 1:
                link(s, "dve", dve, ins)
        ins.then_inc(S["b_ready"], 1)


def rot_pool(sq, n):
    return sq[:, 1024:1024 + n]


def rope(s, dve, x, which, tile, nh, scratch):
    v = s.nc.vector
    rot = HD_A if which == "a" else ROPE
    qtr = rot // 4
    cos = s.cid("cos_" + which)[:, tile * rot:(tile + 1) * rot].unsqueeze(1).broadcast_to([P, nh, rot])
    sin = s.cid("sin_" + which)[:, tile * rot:(tile + 1) * rot]
    tmp = scratch.rearrange("p (h d) -> p h d", h=nh)
    for blk in range(2):
        for u in range(2):
            a, b = blk * 2 * qtr + u * qtr, blk * 2 * qtr + (1 - u) * qtr
            link(s, "dve", dve, v.tensor_tensor(tmp[:, :, a:a + qtr], x[:, :, b:b + qtr],
                                                sin[:, a:a + qtr].unsqueeze(1).broadcast_to([P, nh, qtr]), ALU.mult))
    link(s, "dve", dve, v.tensor_tensor(x, x, cos, ALU.mult))
    return v.tensor_tensor(x, x, tmp, ALU.add)


def att_scores(s, st, qk_t, k_t, v_a, qkb_t, v_b, sink):
    nc, ps = s.nc, s.ps
    sb = stage_buffers(s, st, "sc_")
    prob = sb("prob", [P, 2, 4, 3 * P])
    prob_t = sb("prob_t", [P, 2, 12, P])
    o = sb("o", [P, T, D])
    mx, nb, den, rec, e_sink = (sb(n, [P, 2, 4]) for n in ("mx", "nb", "den", "rec", "e_sink"))
    names = ("s_ps", "nb", "exp", "den", "t_ps", "t_ev", "o_ps", "o_ev", "ot_ps", "ot_ev")
    S = {n: s.sem("sc_" + n) for n in names}
    units = [(kind, t, g) for t in range(T) for kind in "AB" for g in range(2)]
    NU = len(units)
    block = st.enter_context(nc.Block())

    def keys(t):
        return 1 if t == 0 else 3

    @block.sync
    def _(sp):
        ring_loads(s, sp, s.at["att_out", 0] + 2)

    @block.tensor
    def _(pe):
        def scores(n):
            kind, t, g = units[n]
            nk = keys(t)
            if n >= 1:
                pe.wait_ge(S["exp"], 4 * n)
            for j in range(4):
                if kind == "A":
                    lhs = qk_t[64 * g:64 * g + 64, t, j, :]
                    rhs = k_t[64 * g:64 * g + 64, 0, :] if nk == 1 else k_t[64 * g:64 * g + 64, 1:4, :].rearrange("p t n -> p (t n)")
                else:
                    h = 4 * g + j
                    lhs = qkb_t[:, h, t, :]
                    rhs = qkb_t[:, h, 3, :] if nk == 1 else qkb_t[:, h, 4:7, :].rearrange("p t n -> p (t n)")
                masked = kind == "A" and nk == 3
                mm = pe.matmul(ps[:, j, 0:nk * P], lhs, rhs, start=True, stop=True)
                if masked:
                    c = 0 if t == 2 else P
                    mask = s.cid("mask_high") if t == 2 else s.cid("mask_low")
                    mm = pe.matmul(ps[:, j, c:c + P], s.ident, mask, start=False, stop=True, skip_group_check=True)
            mm.then_inc(S["s_ps"], 1)

        def turn(n):
            nk = keys(units[n][1])
            pe.wait_ge(S["exp"], 4 * n + 4)
            if n >= 1:
                pe.wait_ge(S["t_ev"], n)
            for j in range(4):
                for c in range(nk):
                    i = j * nk + c
                    mm = pe.transpose(ps[:, 4 + i // 4, (i % 4) * P:(i % 4 + 1) * P], prob[:, n % 2, j, c * P:(c + 1) * P], s.ident)
            mm.then_inc(S["t_ps"], 1)

        def weigh(n):
            kind, t, g = units[n]
            nk = keys(t)
            pe.wait_ge(S["t_ev"], n + 1)
            if n >= 1:
                pe.wait_ge(S["o_ev"], n)
            for j in range(4):
                for c in range(nk):
                    kt = 0 if nk == 1 else 1 + c
                    rhs = v_a[:, kt, 64 * g:64 * g + 64] if kind == "A" else v_b[:, kt, 4 * g + j, :]
                    mm = pe.matmul(ps[:, 7, j * 64:(j + 1) * 64], prob_t[:, n % 2, j * nk + c, :], rhs,
                                   start=(c == 0), stop=(c == nk - 1))
            mm.then_inc(S["o_ps"], 1)

        scores(0)
        for n in range(NU):
            turn(n)
            if n + 1 < NU:
                scores(n + 1)
            weigh(n)
        for t in range(T):
            pe.wait_ge(S["o_ev"], NU)
            b = 2 * t
            for k in range(KD):
                mm = pe.transpose(ps[:, b + k // 4, (k % 4) * P:(k % 4 + 1) * P], o[:, t, k::KD], s.ident)
            mm.then_inc(S["ot_ps"], 1)

    @block.scalar
    def _(act):
        for n in range(NU):
            kind, t, g = units[n]
            nk = keys(t)
            scale = HD_A ** -0.5 if kind == "A" else HD_B ** -0.5
            act.wait_ge(S["nb"], n + 1)
            if n >= 2:
                act.wait_ge(S["t_ps"], n - 1)
            for j in range(4):
                nc.scalar.activation(prob[:, n % 2, j, 0:nk * P], ps[:, j, 0:nk * P], ACT.Exp, scale=scale,
                                     bias=nb[:, n % 2, j:j + 1], accum_out=den[:, n % 2, j:j + 1]).then_inc(S["exp"], 1)
            if kind == "A":
                for j in range(4):
                    nc.scalar.activation(e_sink[:, n % 2, j:j + 1], sink[:, 4 * g + j:4 * g + j + 1], ACT.Exp,
                                         bias=nb[:, n % 2, j:j + 1]).then_inc(S["den"], 1)
            act.wait_ge(S["t_ps"], n + 1)
            nc.scalar.copy(prob_t[:, n % 2, 0:4 * nk, :].rearrange("p i n -> p (i n)"),
                           ps[:, 4:4 + nk, :].rearrange("p b n -> p (b n)")).then_inc(S["t_ev"], 1)

    @block.vector
    def _(dve):
        v = nc.vector

        def bias(n):
            kind, t, g = units[n]
            nk, b = keys(t), n % 2
            scale = HD_A ** -0.5 if kind == "A" else HD_B ** -0.5
            dve.wait_ge(S["s_ps"], n + 1)
            link(s, "dve", dve, v.tensor_reduce(mx[:, b, :], ps[:, 0:4, 0:nk * P], AX.X, ALU.max))
            if kind == "A":
                link(s, "dve", dve, v.scalar_tensor_tensor(out=mx[:, b, :], in0=mx[:, b, :], scalar=scale,
                                                           in1=sink[:, 4 * g:4 * g + 4], op0=ALU.mult, op1=ALU.max))
                v.tensor_scalar(nb[:, b, :], mx[:, b, :], -1.0, None, ALU.mult).then_inc(S["nb"], 1)
            else:
                v.tensor_scalar(nb[:, b, :], mx[:, b, :], -scale, None, ALU.mult).then_inc(S["nb"], 1)

        sinks = 0
        bias(0)
        for n in range(NU):
            kind, t, g = units[n]
            b = n % 2
            dve.wait_ge(S["exp"], 4 * n + 4)
            if kind == "A":
                sinks += 4
                dve.wait_ge(S["den"], sinks)
                link(s, "dve", dve, v.tensor_tensor(den[:, b, :], den[:, b, :], e_sink[:, b, :], ALU.add))
            link(s, "dve", dve, v.reciprocal(rec[:, b, :], den[:, b, :]))
            if n + 1 < NU:
                bias(n + 1)
            dve.wait_ge(S["o_ps"], n + 1)
            c0 = (0 if kind == "A" else 512) + 256 * g
            v.tensor_tensor(o[:, t, c0:c0 + 256].rearrange("p (h d) -> p h d", h=4),
                            ps[:, 7, 0:256].rearrange("p (h d) -> p h d", h=4),
                            rec[:, b, :].unsqueeze(2).broadcast_to([P, 4, 64]), ALU.mult).then_inc(S["o_ev"], 1)
        for t in range(T):
            dve.wait_ge(S["ot_ps"], t + 1)
            v.tensor_copy(s.hT[:, :, t * P:(t + 1) * P], ps[:, 2 * t:2 * t + 2, :].rearrange("p b (k n) -> p (b k) n", k=4)).then_inc(S["ot_ev"], 1)

    st.close()
    with ExitStack() as st3:
        project_out(s, st3, "ao_", s.hT, KD, [("att_out", 0), ("att_out", 1)], MIX)


def project_out(s, st, pre, src, nk, keys, m):
    nc, ps = s.nc, s.ps
    sb = stage_buffers(s, st, pre)
    gate = sb("gate", [P, 2, D])
    tmp = sb("tmp", [P, 2, BANK])
    g_ps, g_ev, o_ps, o_ev = (s.sem(pre + n) for n in ("g_ps", "g_ev", "o_ps", "o_ev"))
    per = nk // KD
    block = st.enter_context(nc.Block())
    last = s.at[keys[-1]]

    @block.sync
    def _(sp):
        ring_loads(s, sp, last + 1 + SLOT_RING)

    @block.tensor
    def _(pe):
        for g in range(2):
            for h in range(2):
                mm = pe.matmul(ps[:, 2 * g + h, :], s.cid("pick")[0:2, g * P:(g + 1) * P], s.gates[0:2, m, h * BANK:(h + 1) * BANK],
                               start=True, stop=True)
        mm.then_inc(g_ps, 1)
        for h in range(2):
            for kh in range(per):
                ring_wait(s, pe, s.at[keys[h * per + kh]])
            if h:
                pe.wait_ge(o_ev, 3)
            for t in range(T):
                for k in range(nk):
                    n = s.at[keys[h * per + k // KD]]
                    mm = pe.matmul(ps[:, 4 + t, :], src[:, k, t * P:(t + 1) * P], s.ring[:, n % SLOT_RING, k % KD, :],
                                   start=(k == 0), stop=(k == nk - 1))
                mm.then_inc(o_ps, 1)
            pe.wait_ge(o_ps, 3 * (h + 1))
            pe.sem_inc(s.ring_free, per)

    @block.vector
    def _(dve):
        v = nc.vector
        dve.wait_ge(g_ps, 1)
        link(s, "dve", dve, v.tensor_copy(gate[:, :, :].rearrange("p g n -> p (g n)"), ps[:, 0:4, :].rearrange("p b n -> p (b n)")))
        for h in range(2):
            for t in range(T):
                n = 3 * h + t
                dve.wait_ge(o_ps, n + 1)
                v.tensor_tensor(tmp[:, n % 2, :], ps[:, 4 + t, :], gate[:, min(t, 1), h * BANK:(h + 1) * BANK], ALU.mult).then_inc(o_ev, 1)
                dve.wait_ge(o_ev, n + 1)
                ys = s.y[:, t, h * BANK:(h + 1) * BANK]
                v.tensor_tensor(ys, ys, tmp[:, n % 2, :], ALU.add)


def ssd(s, st):
    sb = stage_buffers(s, st, "ssd_")
    xs = sb("xs", [P, T, D_INNER])
    with ExitStack() as st2:
        sb2 = stage_buffers(s, st2, "ssd_")
        g = Shared()
        g.b_t, g.c_t = sb2("b_t", [P, G_C, NTOK]), sb2("c_t", [P, G_C, NTOK])
        g.b_n = sb2("b_n", [P, T, G_C, N_C])
        g.state = sb2("state", [P, 2, D_INNER])
        g.dt, g.dta = sb2("dt", [P, T, 64]), sb2("dta", [P, T, 64])
        g.nacs, g.eacs, g.etot, g.toend = (sb2(n, [P, T, 64]) for n in ("nacs", "eacs", "etot", "toend"))
        with ExitStack() as st3:
            ssd_conv(s, st3, xs, g)
        with ExitStack() as st3:
            ssd_scan(s, st3, xs, g)
    y_t = sb("y_t", [P, 2 * KD, NTOK])
    with ExitStack() as st2:
        ssd_gate(s, st2, xs, y_t)
    with ExitStack() as st2:
        project_out(s, st2, "so_", y_t, 2 * KD, [("ssd_out", (j, kh)) for j in range(2) for kh in range(2)], MIX)


def ssd_conv(s, st, xs, g):
    nc, w, ps = s.nc, s.w, s.ps
    sb = stage_buffers(s, st, "cv_")
    taps_in, taps = sb("taps_in", [32, 6, P]), sb("taps", [P, 6, 32])
    PAD = NTOK + 8
    xp, cv, x_t = sb("xp", [P, 2, PAD]), sb("cv", [P, 2, PAD - 4]), sb("x_t", [P, 2, NTOK])
    dtb, alog, ea = sb("dtb", [P, 64]), sb("alog", [P, 64]), sb("ea", [P, 64])
    v1, v2, v3, v4 = (sb(n, [P, T * 64]) for n in ("v1", "v2", "v3", "v4"))
    names = ("turn_ps", "turn_ev", "mm_ps", "xp", "cv", "silu", "tr_ps", "tr_ev", "dt_ps", "dt_x", "dt_e", "dta", "acs_ps",
             "acs_x", "acs_e", "zero")
    S = {n: s.sem("cv_" + n) for n in names}
    s0 = xs[:, :, :].rearrange("p t n -> p (t n)")[:, 0:4096].rearrange("p (d c n) -> p d c n", d=2, c=16)
    u0, dt0 = s.at["ssd_xbc", 0], s.at["ssd_dt", 0]
    NT = 32
    block = st.enter_context(nc.Block())

    def turned(n):
        return n < 24

    @block.sync
    def _(sp):
        loads = [(taps_in[:, 0:5, :], w["ssd_conv_w"][0].rearrange("k (c p) -> c k p", p=P)),
                 (taps_in[:, 5, :], w["ssd_conv_b"][0].rearrange("(c p) -> c p", p=P)),
                 (dtb[:, 0:32], w["ssd_dtb_fwd"][0].partition_broadcast(P)),
                 (dtb[:, 32:64], w["ssd_dtb_bwd"][0].partition_broadcast(P)),
                 (alog[:, 0:32], w["ssd_alog_fwd"][0].partition_broadcast(P)),
                 (alog[:, 32:64], w["ssd_alog_bwd"][0].partition_broadcast(P)),
                 (s0[:, 0], w["state_c_fwd"][0, 0].rearrange("h p n -> (h p) n").rearrange("(c q) n -> q c n", q=P)),
                 (s0[:, 1], w["state_c_bwd"][0, 0].rearrange("h p n -> (h p) n").rearrange("(c q) n -> q c n", q=P))]
        for dst, src in loads:
            sp.dma_start(dst, src).then_inc(s.loads, 16)
        s.loaded += 16 * len(loads)
        ring_loads(s, sp, dt0 + 1 + SLOT_RING)

    @block.tensor
    def _(pe):
        pe.wait_ge(s.loads, s.loaded)
        for k in range(6):
            mm = pe.transpose(ps[:, 4, k * 32:(k + 1) * 32], taps_in[:, k, :], s.ident[0:32, 0:32])
        mm.then_inc(S["turn_ps"], 1)
        for q in range(4):
            if q >= 2:
                pe.wait_ge(S["turn_ev"], q)
            for c in range(8):
                mm = pe.transpose(ps[:, 2 * (q % 2) + c // 4, (c % 4) * P:(c % 4 + 1) * P], s0[:, q // 2, 8 * (q % 2) + c, :], s.ident)
            mm.then_inc(S["turn_ps"], 1)

        def turn(n):
            pe.wait_ge(S["silu"], 2 * (n + 1))
            if n >= 2:
                pe.wait_ge(S["tr_ev"], n - 1)
            src = x_t[:, n % 2, :] if n < 16 else g.b_t[:, n - 16, :]
            for t in range(T):
                mm = pe.transpose(ps[:, 2 + n % 2, t * P:(t + 1) * P], src[:, t * P:(t + 1) * P], s.ident)
            mm.then_inc(S["tr_ps"], 1)

        pe.wait_ge(S["turn_ev"], 5)
        for n in range(NT):
            c, i = divmod(n, 4)
            if i == 0:
                ring_wait(s, pe, u0 + c)
            if n >= 2:
                pe.wait_ge(S["xp"], 2 * (n - 1))
            for k in range(KD):
                mm = pe.matmul(ps[:, n % 2, 0:NTOK], s.ring[:, (u0 + c) % SLOT_RING, k, i * P:(i + 1) * P], s.hT[:, k, :],
                               start=(k == 0), stop=(k == KD - 1))
            mm.then_inc(S["mm_ps"], 1)
            if n >= 2 and turned(n - 2):
                turn(n - 2)
            if i == 0 and c >= 1:
                pe.wait_ge(S["mm_ps"], n)
                pe.sem_inc(s.ring_free, 1)
        pe.wait_ge(S["mm_ps"], NT)
        pe.sem_inc(s.ring_free, 1)
        ring_wait(s, pe, dt0)
        for t in range(T):
            for k in range(KD):
                mm = pe.matmul(ps[:, 4, t * 64:(t + 1) * 64], s.hT[:, k, t * P:(t + 1) * P], s.ring[:, dt0 % SLOT_RING, k, 0:64],
                               start=(k == 0), stop=(k == KD - 1))
        mm.then_inc(S["dt_ps"], 1)
        pe.wait_ge(S["dt_ps"], 1)
        pe.sem_inc(s.ring_free, 1)
        pe.wait_ge(S["dta"], 1)
        for t in range(T):
            for d in range(2):
                pe.matmul(ps[:, 5, t * 64 + 32 * d:t * 64 + 32 * d + 32], s.cid("from_" if d else "upto"),
                          g.dta[:, t, 32 * d:32 * d + 32], start=True, stop=True)
            mm = pe.matmul(ps[:, 6, t * 64:(t + 1) * 64], s.cid("ones"), g.dta[:, t, :], start=True, stop=True)
        mm.then_inc(S["acs_ps"], 1)

    @block.scalar
    def _(act):
        a = nc.scalar

        def silu(n):
            act.wait_ge(S["cv"], n + 1)
            if n < 16 and n >= 2:
                act.wait_ge(S["tr_ps"], n - 1)
            dst = x_t[:, n % 2, :] if n < 16 else (g.b_t[:, n - 16, :] if n < 24 else g.c_t[:, n - 24, :])
            bias = taps[:, 5, n:n + 1]
            a.activation(dst[:, 0:P], cv[:, n % 2, 0:P], ACT.Silu, bias=bias).then_inc(S["silu"], 1)
            a.activation(dst[:, P:NTOK], cv[:, n % 2, P + 4:NTOK + 4], ACT.Silu, bias=bias).then_inc(S["silu"], 1)

        def turned_out(n):
            act.wait_ge(S["tr_ps"], n + 1)
            dst = xs[:, :, n * P:(n + 1) * P] if n < 16 else g.b_n[:, :, n - 16, :]
            a.copy(dst, ps[:, 2 + n % 2, 0:NTOK].rearrange("p (t n) -> p t n", t=T)).then_inc(S["tr_ev"], 1)

        act.wait_ge(s.loads, s.loaded)
        act.wait_ge(S["turn_ps"], 1)
        a.copy(taps[:, :, :].rearrange("p k c -> p (k c)"), ps[:, 4, 0:192]).then_inc(S["turn_ev"], 1)
        for q in range(4):
            act.wait_ge(S["turn_ps"], q + 2)
            a.copy(g.state[:, q // 2, (q % 2) * D:(q % 2 + 1) * D], ps[:, 2 * (q % 2):2 * (q % 2) + 2, :].rearrange("p b n -> p (b n)")).then_inc(S["turn_ev"], 1)
        act.wait_ge(S["zero"], 1)
        for n in range(NT + 3):
            if n < NT:
                act.wait_ge(S["mm_ps"], n + 1)
                if n >= 2:
                    act.wait_ge(S["cv"], n - 1)
                a.copy(xp[:, n % 2, 2:P + 2], ps[:, n % 2, 0:P]).then_inc(S["xp"], 1)
                a.copy(xp[:, n % 2, P + 6:NTOK + 6], ps[:, n % 2, P:NTOK]).then_inc(S["xp"], 1)
            if 1 <= n <= NT:
                silu(n - 1)
            if n >= 3 and turned(n - 3):
                turned_out(n - 3)
        a.activation(ea[:, :], alog[:, :], ACT.Exp).then_inc(S["dt_e"], 1)
        act.wait_ge(S["dt_x"], 1)
        a.activation(v2[:, :], v2[:, :], ACT.Exp, scale=-1.0).then_inc(S["dt_e"], 1)
        act.wait_ge(S["acs_x"], 1)
        a.activation(flat3(g.toend), flat3(g.toend), ACT.Exp).then_inc(S["acs_e"], 1)
        a.activation(flat3(g.eacs), flat3(g.nacs), ACT.Exp, scale=-1.0).then_inc(S["acs_e"], 1)
        a.activation(flat3(g.etot), flat3(g.etot), ACT.Exp).then_inc(S["acs_e"], 1)

    @block.vector
    def _(dve):
        v = nc.vector
        v.memset(xp[:, :, :], 0.0).then_inc(S["zero"], 1)
        dve.wait_ge(S["turn_ev"], 1)
        for n in range(NT):
            dve.wait_ge(S["xp"], 2 * (n + 1))
            if n >= 2:
                dve.wait_ge(S["silu"], 2 * (n - 1))
            o = cv[:, n % 2, :]
            link(s, "dve", dve, v.tensor_scalar(o, xp[:, n % 2, 0:PAD - 4], taps[:, 0, n:n + 1], None, ALU.mult))
            for k in range(1, 5):
                ins = v.scalar_tensor_tensor(out=o, in0=xp[:, n % 2, k:k + PAD - 4], scalar=taps[:, k, n:n + 1], in1=o,
                                             op0=ALU.mult, op1=ALU.add)
                if k < 4:
                    link(s, "dve", dve, ins)
            ins.then_inc(S["cv"], 1)
        dve.wait_ge(s.loads, s.loaded)
        dve.wait_ge(S["dt_ps"], 1)
        link(s, "dve", dve, v.tensor_tensor(v1[:, :].rearrange("p (t h) -> p t h", t=T), ps[:, 4, 0:T * 64].rearrange("p (t h) -> p t h", t=T),
                                            dtb[:, :].unsqueeze(1).broadcast_to([P, T, 64]), ALU.add))
        v.scalar_tensor_tensor(out=v2[:, :], in0=v1[:, :], scalar=-1.0, in1=v1[:, :], op0=ALU.mult, op1=ALU.max).then_inc(S["dt_x"], 1)
        dve.wait_ge(S["dt_e"], 2)
        link(s, "dve", dve, v.tensor_scalar(v3[:, :], v2[:, :], 2.0, None, ALU.add))
        link(s, "dve", dve, v.reciprocal(v3[:, :], v3[:, :]))
        link(s, "dve", dve, v.tensor_tensor(v2[:, :], v2[:, :], v3[:, :], ALU.mult))
        link(s, "dve", dve, v.tensor_tensor(v3[:, :], v2[:, :], v2[:, :], ALU.mult))
        link(s, "dve", dve, v.tensor_scalar(v4[:, :], v3[:, :], 1.0 / 13, None, ALU.mult))
        for odd in (11, 9, 7, 5, 3):
            link(s, "dve", dve, v.scalar_tensor_tensor(out=v4[:, :], in0=v4[:, :], scalar=1.0 / odd, in1=v3[:, :], op0=ALU.add, op1=ALU.mult))
        link(s, "dve", dve, v.scalar_tensor_tensor(out=v4[:, :], in0=v4[:, :], scalar=1.0, in1=v2[:, :], op0=ALU.add, op1=ALU.mult))
        link(s, "dve", dve, v.tensor_scalar(v4[:, :], v4[:, :], 2.0, None, ALU.mult))
        link(s, "dve", dve, v.scalar_tensor_tensor(out=flat3(g.dt), in0=v1[:, :], scalar=0.0, in1=v4[:, :], op0=ALU.max, op1=ALU.add))
        v.scalar_tensor_tensor(out=g.dta[:, :, :], in0=g.dt[:, :, :], scalar=-1.0, in1=ea[:, :].unsqueeze(1).broadcast_to([P, T, 64]),
                               op0=ALU.mult, op1=ALU.mult).then_inc(S["dta"], 1)
        dve.wait_ge(S["acs_ps"], 1)
        link(s, "dve", dve, v.tensor_scalar(flat3(g.nacs), ps[:, 5, 0:T * 64], -1.0, None, ALU.mult))
        link(s, "dve", dve, v.tensor_tensor(flat3(g.toend), flat3(g.nacs), ps[:, 6, 0:T * 64], ALU.add))
        v.tensor_copy(flat3(g.etot), ps[:, 6, 0:T * 64]).then_inc(S["acs_x"], 1)
        dve.wait_ge(S["acs_e"], 3)
        link(s, "dve", dve, v.tensor_tensor(flat3(g.toend), flat3(g.toend), flat3(g.dt), ALU.mult))


def flat3(t):
    return t[:, :, :].rearrange("p a b -> p (a b)")


def ssd_scan(s, st, xs, g):
    nc, w, ps, out = s.nc, s.w, s.ps, s.out
    sb = stage_buffers(s, st, "scan_")
    W = R_C * P_C
    e = sb("e", [P, 2, 2, R_C, P])
    cb = sb("cb", [P, T, P])
    xdt = sb("xdt", [P, T, 2, R_C, P_C])
    xe = sb("xe", [P, 4, R_C, P_C])
    inter = sb("inter", [P, 2, W])
    stage = sb("stage", [P, BANK])
    skip = sb("skip", [P, H_C])
    ident_h = sb("ident_h", [P, P], BF16)
    mask_h = sb("mask_h", [P, 2, P], BF16)
    names = ("cb_ps", "cb_ev", "a_ps", "exp", "m", "pool", "y_ps", "y_ev", "i_ps", "i_ev", "sp_ps", "sp_ev", "s1_ps", "upd", "init", "stage")
    S = {n: s.sem("scan_" + n) for n in names}
    EX = ((0, 0), (0, 1), (1, 0), (2, 1))
    block = st.enter_context(nc.Block())

    @block.sync
    def _(sp):
        sp.dma_start(skip[:, :], w["ssd_d"][0].partition_broadcast(P)).then_inc(s.loads, 16)
        s.loaded += 16
        for q in range(G_C):
            sp.wait_ge(S["sp_ev"], q + 1)
            for d in range(2):
                dst = out["new_state_bwd" if d else "new_state_fwd"][0, 0, 4 * q:4 * q + 4].rearrange("(a b) p n -> (b p) a n", a=2)
                sp.dma_start(dst, stage[:, d * 256:(d + 1) * 256].rearrange("p (a n) -> p a n", a=2)).then_inc(S["stage"], 16)
        sp.wait_ge(S["stage"], 32 * G_C)

    @block.gpsimd
    def _(pool):
        pool.wait_ge(s.loads, s.loaded)

        def scaled(dst, t, src, col):
            return nc.gpsimd.tensor_tensor(dst, xs[:, t, q * W:(q + 1) * W].rearrange("p (h d) -> p h d", h=R_C),
                                           src[:, col:col + R_C].unsqueeze(2).broadcast_to([P, R_C, P_C]), ALU.mult)
        for q in range(G_C):
            if q:
                pool.wait_ge(S["y_ps"], 3 * q)
                pool.wait_ge(S["y_ev"], 3 * q)
                pool.wait_ge(S["s1_ps"], q)
            for t in range(T):
                for d in range(2):
                    scaled(xdt[:, t, d], t, g.dt[:, t, :], 32 * d + 4 * q)
                for i, (tt, d) in enumerate(EX):
                    if tt == t:
                        scaled(xe[:, i], t, g.toend[:, t, :], 32 * d + 4 * q)
                scaled(xs[:, t, q * W:(q + 1) * W].rearrange("p (h d) -> p h d", h=R_C), t, skip, 4 * q).then_inc(S["pool"], 1)

    @block.tensor
    def _(pe):
        pe.wait_ge(S["init"], 3)

        def decay(q, t):
            u = 3 * q + t
            if u >= 2:
                pe.wait_ge(S["exp"], 8 * (u - 1))
            for d in range(2):
                b = 1 + 2 * (u % 2) + d
                for r in range(R_C):
                    c = 32 * d + 4 * q + r
                    pe.matmul(ps[:, b, r * P:(r + 1) * P], g.dta[:, t, c:c + 1].broadcast_to([P, P]),
                              s.cid("from_" if d else "upto"), start=(r == 0), stop=False, skip_group_check=True)
                mm = pe.matmul(ps[:, b, :].rearrange("p (r i) -> p r i", r=R_C), ident_h[:, :],
                               mask_h[:, d, :].unsqueeze(1).broadcast_to([P, R_C, P]), start=False, stop=True, skip_group_check=True)
            mm.then_inc(S["a_ps"], 1)

        def give(q, t):
            u = 3 * q + t
            pe.wait_ge(S["m"], u + 1)
            pe.wait_ge(S["pool"], u + 1)
            if u:
                pe.wait_ge(S["y_ev"], u)
            for r in range(R_C):
                for d in range(2):
                    mm = pe.matmul(ps[:, 5, r * P_C:(r + 1) * P_C], e[:, u % 2, d, r, :], xdt[:, t, d, r, :],
                                   start=(d == 0), stop=(d == 1))
            mm.then_inc(S["y_ps"], 1)

        def from_state(q, rnd):
            n = 2 * q + rnd
            if n:
                pe.wait_ge(S["i_ev"], n)
            if rnd:
                pe.wait_ge(S["upd"], 2 * (q + 1))
            for d in range(2):
                t = (1, 2)[d] if rnd == 0 else (2, 1)[d]
                mm = pe.matmul(ps[:, 7, d * W:(d + 1) * W], g.c_t[:, q, t * P:(t + 1) * P], g.state[:, d, q * W:(q + 1) * W],
                               start=True, stop=True)
            mm.then_inc(S["i_ps"], 1)

        for q in range(G_C):
            if q:
                pe.wait_ge(S["cb_ev"], q)
            for t in range(T):
                mm = pe.matmul(ps[:, 0, t * P:(t + 1) * P], g.b_t[:, q, t * P:(t + 1) * P], g.c_t[:, q, t * P:(t + 1) * P],
                               start=True, stop=True)
            mm.then_inc(S["cb_ps"], 1)
            decay(q, 0)
            decay(q, 1)
            from_state(q, 0)
            pe.wait_ge(S["pool"], 3 * q + 1)
            if q:
                pe.wait_ge(S["upd"], 2 * q)
            for d in range(2):
                for a in range(2):
                    mm = pe.matmul(ps[:, 6, (2 * d + a) * P:(2 * d + a + 1) * P], xe[:, d, 2 * a:2 * a + 2, :].rearrange("p h d -> p (h d)"),
                                   g.b_n[:, 0, q, :], start=True, stop=True)
            mm.then_inc(S["sp_ps"], 1)
            give(q, 0)
            decay(q, 2)
            pe.wait_ge(S["pool"], 3 * q + 3)
            pe.wait_ge(S["sp_ev"], q + 1)
            for d in range(2):
                mm = pe.matmul(ps[:, 6, d * W:(d + 1) * W], g.b_n[:, 1 + d, q, :], xe[:, 2 + d, :, :].rearrange("p h d -> p (h d)"),
                               start=True, stop=True)
            mm.then_inc(S["s1_ps"], 1)
            give(q, 1)
            from_state(q, 1)
            give(q, 2)

    @block.scalar
    def _(act):
        a = nc.scalar
        for u in range(3 * G_C):
            q, t = divmod(u, T)
            act.wait_ge(S["a_ps"], u + 1)
            if u >= 2:
                act.wait_ge(S["y_ps"], u - 1)
            for d in range(2):
                for r in range(R_C):
                    c = 32 * d + 4 * q + r
                    a.activation(e[:, u % 2, d, r, :], ps[:, 1 + 2 * (u % 2) + d, r * P:(r + 1) * P], ACT.Exp,
                                 bias=g.nacs[:, t, c:c + 1]).then_inc(S["exp"], 1)
            if t == 1:
                act.wait_ge(S["sp_ps"], q + 1)
                if q >= 1:
                    act.wait_ge(S["stage"], 32 * q)
                a.copy(stage[:, :], ps[:, 6, :]).then_inc(S["sp_ev"], 1)

    @block.vector
    def _(dve):
        v = nc.vector
        v.tensor_copy(ident_h[:, :], s.ident).then_inc(S["init"], 1)
        v.tensor_copy(mask_h[:, 0, :], s.cid("mask_high")).then_inc(S["init"], 1)
        v.tensor_copy(mask_h[:, 1, :], s.cid("mask_low")).then_inc(S["init"], 1)

        def weigh(q, t):
            u = 3 * q + t
            dve.wait_ge(S["exp"], 8 * (u + 1))
            m = e[:, u % 2].rearrange("p d r i -> p (d r) i")
            v.tensor_tensor(m, m, cb[:, t, :].unsqueeze(1).broadcast_to([P, 2 * R_C, P]), ALU.mult).then_inc(S["m"], 1)

        def take(q, t):
            u = 3 * q + t
            dve.wait_ge(S["y_ps"], u + 1)
            dve.wait_ge(S["pool"], u + 1)
            v.tensor_tensor(xs[:, t, q * W:(q + 1) * W], ps[:, 5, 0:W], xs[:, t, q * W:(q + 1) * W], ALU.add).then_inc(S["y_ev"], 1)
            dve.wait_ge(S["y_ev"], u + 1)

        def add_inter(q, rnd, d):
            t = (1, 2)[d] if rnd == 0 else (2, 1)[d]
            yq = xs[:, t, q * W:(q + 1) * W]
            link(s, "dve", dve, v.tensor_tensor(yq, yq, inter[:, d, :], ALU.add))

        def scale_inter(q, rnd):
            dve.wait_ge(S["i_ps"], 2 * q + rnd + 1)
            for d in range(2):
                t = (1, 2)[d] if rnd == 0 else (2, 1)[d]
                c = 32 * d + 4 * q
                ins = v.tensor_tensor(inter[:, d, :].rearrange("p (h d) -> p h d", h=R_C), ps[:, 7, d * W:(d + 1) * W].rearrange("p (h d) -> p h d", h=R_C),
                                      g.eacs[:, t, c:c + 4].unsqueeze(2).broadcast_to([P, R_C, P_C]), ALU.mult)
                if d == 0:
                    link(s, "dve", dve, ins)
            ins.then_inc(S["i_ev"], 1)
            dve.wait_ge(S["i_ev"], 2 * q + rnd + 1)

        for q in range(G_C):
            dve.wait_ge(S["cb_ps"], q + 1)
            v.tensor_copy(cb[:, :, :].rearrange("p t i -> p (t i)"), ps[:, 0, 0:NTOK]).then_inc(S["cb_ev"], 1)
            dve.wait_ge(S["cb_ev"], q + 1)
            weigh(q, 0)
            weigh(q, 1)
            scale_inter(q, 0)
            for d in range(2):
                c, tt = 32 * d + 4 * q, 1 + d
                sq = g.state[:, d, q * W:(q + 1) * W].rearrange("p (h d) -> p h d", h=R_C)
                link(s, "dve", dve, v.tensor_tensor(sq, sq, g.etot[:, tt, c:c + 4].unsqueeze(2).broadcast_to([P, R_C, P_C]), ALU.mult))
            take(q, 0)
            weigh(q, 2)
            dve.wait_ge(S["s1_ps"], q + 1)
            for d in range(2):
                sq = g.state[:, d, q * W:(q + 1) * W]
                v.tensor_tensor(sq, sq, ps[:, 6, d * W:(d + 1) * W], ALU.add).then_inc(S["upd"], 1)
            take(q, 1)
            add_inter(q, 0, 0)
            take(q, 2)
            add_inter(q, 0, 1)
            scale_inter(q, 1)
            add_inter(q, 1, 0)
            add_inter(q, 1, 1)


def ssd_gate(s, st, xs, y_t):
    nc, w, ps = s.nc, s.w, s.ps
    sb = stage_buffers(s, st, "gate_")
    z = sb("z", [P, 2, BANK])
    gw_in, gw = sb("gw_in", [16, P]), sb("gw", [P, 16])
    sq = sb("sq", [P, 256])
    ss, x, r, tmp = (sb(n, [P, T * G_C]) for n in ("ss", "x", "r", "tmp"))
    names = ("z_ps", "z", "y", "ss", "x", "r", "yn", "gw_ps", "gw", "t_ps", "t_ev")
    S = {n: s.sem("gate_" + n) for n in names}
    z0 = s.at["ssd_z", 0]
    block = st.enter_context(nc.Block())

    @block.sync
    def _(sp):
        sp.dma_start(gw_in[:, :], w["ssd_norm"][0].rearrange("(k p) -> k p", p=P)).then_inc(s.loads, 16)
        s.loaded += 16
        ring_loads(s, sp, z0 + 4 + SLOT_RING)

    @block.tensor
    def _(pe):
        for j in range(4):
            ring_wait(s, pe, z0 + j)
            for t in range(T):
                n = 3 * j + t
                if n >= 4:
                    pe.wait_ge(S["z"], n - 3)
                for k in range(KD):
                    mm = pe.matmul(ps[:, n % 4, :], s.hT[:, k, t * P:(t + 1) * P], s.ring[:, (z0 + j) % SLOT_RING, k, :],
                                   start=(k == 0), stop=(k == KD - 1))
                mm.then_inc(S["z_ps"], 1)
            pe.wait_ge(S["z_ps"], 3 * j + 3)
            pe.sem_inc(s.ring_free, 1)
        pe.wait_ge(s.loads, s.loaded)
        pe.wait_ge(S["z"], 12)
        pe.transpose(ps[:, 0, 0:16], gw_in[:, :], s.ident[0:16, 0:16]).then_inc(S["gw_ps"], 1)
        pe.wait_ge(S["gw"], 1)
        for t in range(T):
            pe.wait_ge(S["yn"], t + 1)
            if t >= 2:
                pe.wait_ge(S["t_ev"], 4 * (t - 1))
            for k in range(16):
                mm = pe.transpose(ps[:, 4 * (t % 2) + k // 4, (k % 4) * P:(k % 4 + 1) * P], xs[:, t, k * P:(k + 1) * P], s.ident)
            mm.then_inc(S["t_ps"], 1)

    @block.scalar
    def _(act):
        a = nc.scalar
        for n in range(12):
            act.wait_ge(S["z_ps"], n + 1)
            if n >= 2:
                act.wait_ge(S["y"], n - 1)
            a.activation(z[:, n % 2, :], ps[:, n % 4, :], ACT.Silu).then_inc(S["z"], 1)
        act.wait_ge(S["y"], 12)
        for t in range(T):
            for q in range(G_C):
                i = t * G_C + q
                if i:
                    act.wait_ge(S["ss"], i)
                a.activation(sq[:, :], xs[:, t, q * 256:(q + 1) * 256], ACT.Square, accum_out=ss[:, i:i + 1]).then_inc(S["ss"], 1)
        rsqrt_act(s, act, x[:, :], r[:, :], S["x"], 1, S["r"])

    @block.vector
    def _(dve):
        v = nc.vector
        for n in range(12):
            j, t = divmod(n, T)
            dve.wait_ge(S["z"], n + 1)
            yj = xs[:, t, j * BANK:(j + 1) * BANK]
            v.tensor_tensor(yj, yj, z[:, n % 2, :], ALU.mult).then_inc(S["y"], 1)
        dve.wait_ge(S["gw_ps"], 1)
        v.tensor_copy(gw[:, :], ps[:, 0, 0:16]).then_inc(S["gw"], 1)
        dve.wait_ge(S["ss"], T * G_C)
        v.tensor_scalar(x[:, :], ss[:, :], 1.0 / 256, EPS, ALU.mult, ALU.add).then_inc(S["x"], 1)
        rsqrt_dve(s, dve, x[:, :], r[:, :], tmp[:, :], S["r"], 1)
        for t in range(T):
            yt = xs[:, t, :].rearrange("p (q c) -> p q c", q=G_C)
            v.tensor_tensor(yt, yt, r[:, t * G_C:(t + 1) * G_C].unsqueeze(2).broadcast_to([P, G_C, 256]), ALU.mult).then_inc(S["yn"], 1)
        for t in range(T):
            dve.wait_ge(S["t_ps"], t + 1)
            for b in range(4):
                v.tensor_tensor(y_t[:, 4 * b:4 * b + 4, t * P:(t + 1) * P], ps[:, 4 * (t % 2) + b, :].rearrange("p (k n) -> p k n", k=4),
                                gw[:, 4 * b:4 * b + 4].unsqueeze(2).broadcast_to([P, 4, P]), ALU.mult).then_inc(S["t_ev"], 1)


def moe(s, l, st):
    sb = stage_buffers(s, st, f"moe{l}_")
    m = Shared()
    m.hp = sb("hp", [P, T, KD, P])
    m.acc = s.hT[:, :, :].rearrange("p k n -> p (k n)").rearrange("p (t d) -> p t d", t=T)
    m.gates = sb("gates", [P, T, NE])
    m.code = sb("code", [P, T, NE])
    m.most = sb("most", [1, 1], I32)
    with ExitStack() as st2:
        norm_stage(s, l, FFN, st2, hp=m.hp)
    with ExitStack() as st2:
        route(s, l, st2, m)
    with ExitStack() as st2:
        experts(s, l, st2, m)
    with ExitStack() as st2:
        add_moe(s, l, st2, m)


def route(s, l, st, m):
    nc, w, ps = s.nc, s.w, s.ps
    sb = stage_buffers(s, st, f"rt{l}_")
    rw, rb = sb("rw", [P, KD, NG + NE]), sb("rb", [P, NG + NE])
    lg = sb("lg", [P, T, NG + NE])
    v4 = sb("v4", [P, T, NG])
    oh4 = sb("oh4", [P, T, NG])
    le, eq, oh1, oh2, sel = (sb(n, [P, T, NE]) for n in ("le", "eq", "oh1", "oh2", "sel"))
    mx, m1, m2, t1, ptop, w1, w2 = (sb(n, [P, T, 1]) for n in ("mx", "m1", "m2", "t1", "ptop", "w1", "w2"))
    top = sb("top", [P, 1])
    names = ("lg_ps", "x4", "e4", "x2", "e2", "sel", "rank_ps")
    S = {n: s.sem(f"rt{l}_" + n) for n in names}
    block = st.enter_context(nc.Block())

    @block.sync
    def _(sp):
        loads = [(rw[:, :, 0:NG], w["moe_wg"][l].rearrange("(p k) n -> p k n", k=KD)),
                 (rw[:, :, NG:NG + NE], w["moe_we"][l].rearrange("(p k) n -> p k n", k=KD)),
                 (rb[:, 0:NG], w["moe_bg"][l].partition_broadcast(P)),
                 (rb[:, NG:NG + NE], w["moe_be"][l].partition_broadcast(P))]
        for dst, src in loads:
            sp.dma_start(dst, src).then_inc(s.loads, 16)
        s.loaded += 16 * len(loads)

    @block.tensor
    def _(pe):
        pe.wait_ge(s.loads, s.loaded)
        for t in range(T):
            for k in range(KD):
                mm = pe.matmul(ps[:, 0, t * 36:(t + 1) * 36], s.hT[:, k, t * P:(t + 1) * P], rw[:, k, :],
                               start=(k == 0), stop=(k == KD - 1))
        mm.then_inc(S["lg_ps"], 1)
        pe.wait_ge(S["sel"], 1)
        for t in range(T):
            for b in range(t):
                pe.matmul(ps[:, 1, t * NE:(t + 1) * NE], s.cid("ones"), sel[:, b, :], start=(b == 0), stop=False)
            pe.matmul(ps[:, 1, t * NE:(t + 1) * NE], s.cid("before"), sel[:, t, :], start=(t == 0), stop=True)
        for t in range(T):
            mm = pe.matmul(ps[:, 1, T * NE:(T + 1) * NE], s.cid("ones"), sel[:, t, :], start=(t == 0), stop=(t == T - 1))
        mm.then_inc(S["rank_ps"], 1)

    @block.scalar
    def _(act):
        act.wait_ge(S["x4"], 1)
        nc.scalar.activation(v4[:, :, :], v4[:, :, :], ACT.Exp).then_inc(S["e4"], 1)
        act.wait_ge(S["x2"], 1)
        nc.scalar.activation(w2[:, :, :], w2[:, :, :], ACT.Exp).then_inc(S["e2"], 1)

    @block.vector
    def _(dve):
        v = nc.vector

        def do(ins):
            link(s, "dve", dve, ins)

        def wide(a, n):
            return a.broadcast_to([P, T, n])

        def first_of(dst, values, most, order, n):
            e = eq[:, :, 0:n]
            do(v.tensor_tensor(e, values, wide(most, n), ALU.is_equal))
            do(v.tensor_tensor(e, e, order.unsqueeze(1).broadcast_to([P, T, n]), ALU.mult))
            do(v.tensor_reduce(t1[:, :, :], e, AX.X, ALU.max))
            do(v.tensor_tensor(dst, e, wide(t1[:, :, :], n), ALU.is_equal))

        dve.wait_ge(s.loads, s.loaded)
        dve.wait_ge(S["lg_ps"], 1)
        do(v.tensor_tensor(lg[:, :, :], ps[:, 0, 0:T * 36].rearrange("p (t n) -> p t n", t=T), rb[:, :].unsqueeze(1).broadcast_to([P, T, 36]), ALU.add))
        grp = lg[:, :, 0:NG]
        do(v.tensor_reduce(mx[:, :, :], grp, AX.X, ALU.max))
        v.tensor_tensor(v4[:, :, :], grp, wide(mx[:, :, :], NG), ALU.subtract).then_inc(S["x4"], 1)
        first_of(oh4[:, :, :], grp, mx[:, :, :], s.cid("rank4"), NG)
        do(v.tensor_scalar(oh4[:, :, :], oh4[:, :, :], -1.0, BIG, ALU.add, ALU.mult))
        do(v.tensor_copy(le[:, :, :], lg[:, :, NG:]))
        for t in range(T):
            le_t = le[:, t, :].rearrange("p (g e) -> p g e", g=NG)
            do(v.tensor_tensor(le_t, le_t, oh4[:, t, :].unsqueeze(2).broadcast_to([P, NG, PER]), ALU.add))
        do(v.tensor_reduce(m1[:, :, :], le[:, :, :], AX.X, ALU.max))
        first_of(oh1[:, :, :], le[:, :, :], m1[:, :, :], s.cid("rank32"), NE)
        do(v.scalar_tensor_tensor(out=le[:, :, :], in0=oh1[:, :, :], scalar=-3 * BIG, in1=le[:, :, :], op0=ALU.mult, op1=ALU.add))
        do(v.tensor_reduce(m2[:, :, :], le[:, :, :], AX.X, ALU.max))
        first_of(oh2[:, :, :], le[:, :, :], m2[:, :, :], s.cid("rank32"), NE)
        v.tensor_tensor(w2[:, :, :], m2[:, :, :], m1[:, :, :], ALU.subtract).then_inc(S["x2"], 1)
        v.tensor_tensor(sel[:, :, :], oh1[:, :, :], oh2[:, :, :], ALU.add).then_inc(S["sel"], 1)
        dve.wait_ge(S["e4"], 1)
        do(v.tensor_reduce(ptop[:, :, :], v4[:, :, :], AX.X, ALU.add))
        dve.wait_ge(S["e2"], 1)
        do(v.tensor_scalar(w1[:, :, :], w2[:, :, :], 1.0, None, ALU.add))
        do(v.tensor_tensor(w1[:, :, :], w1[:, :, :], ptop[:, :, :], ALU.mult))
        do(v.reciprocal(w1[:, :, :], w1[:, :, :]))
        do(v.tensor_tensor(w2[:, :, :], w2[:, :, :], w1[:, :, :], ALU.mult))
        do(v.tensor_tensor(oh1[:, :, :], oh1[:, :, :], wide(w1[:, :, :], NE), ALU.mult))
        do(v.tensor_tensor(oh2[:, :, :], oh2[:, :, :], wide(w2[:, :, :], NE), ALU.mult))
        do(v.tensor_tensor(m.gates[:, :, :], oh1[:, :, :], oh2[:, :, :], ALU.add))
        dve.wait_ge(S["sel"], 1)
        dve.wait_ge(S["rank_ps"], 1)
        do(v.scalar_tensor_tensor(out=m.code[:, :, :], in0=ps[:, 1, 0:T * NE].rearrange("p (t n) -> p t n", t=T), scalar=1.0,
                                  in1=sel[:, :, :], op0=ALU.add, op1=ALU.mult))
        do(v.tensor_scalar(m.code[:, :, :], m.code[:, :, :], -1.0, None, ALU.add))
        do(v.tensor_reduce(top[:, :], ps[:, 1, T * NE:(T + 1) * NE], AX.X, ALU.max))
        do(v.tensor_copy(m.most[:, :], top[0:1, :]))


class PairSteps:

    NAMES = ("onehot", "gt_ps", "gt_ev", "hg_ps", "hg_ev", "h_ps", "silu", "hid", "ht_ps", "ht_ev", "o_ps", "o_ev", "lo_ev", "sc_ps", "sc_ev")

    def __init__(self, s, m, bufs, sems, deep, first_slot):
        self.s, self.m, self.b, self.S, self.deep, self.first_slot = s, m, bufs, sems, deep, first_slot

    def wait(self, eng, name, value, at_least=1):
        if at_least > 0:
            eng.wait_ge(self.S[name], value)

    def onehot(self, dve, i, n, b, n0):
        v, m = self.s.nc.vector, self.m
        self.wait(dve, "hg_ps", n + 1 - self.deep, n0 + 1 - self.deep)
        v.tensor_copy(self.b.turn[:, b, :, P:P + 2], m.gates[:, :, bass.ds(2 * i, 2)]).then_inc(self.S["onehot"], 1)
        for e in range(2):
            v.tensor_tensor(self.b.onehot[:, b, :, e * SLOTS:(e + 1) * SLOTS],
                            self.s.cid("slot_no")[:, 0:SLOTS].unsqueeze(1).broadcast_to([P, T, SLOTS]),
                            m.code[:, :, bass.ds(2 * i + e, 1)].broadcast_to([P, T, SLOTS]), ALU.is_equal).then_inc(self.S["onehot"], 1)

    def take_turned(self, dve, n, b, n0):
        v = self.s.nc.vector
        dve.wait_ge(self.S["gt_ps"], n + 1)
        self.wait(dve, "sc_ps", 6 * (n + 1 - self.deep), n0 + 1 - self.deep)
        turned = self.s.ps[:, 3, 0:T * (P + 2)].rearrange("p (t c) -> p t c", t=T)
        v.tensor_copy(self.b.onehot_t[:, b, :].rearrange("p (t n) -> p t n", t=T), turned[:, :, 0:P]).then_inc(self.S["gt_ev"], 1)
        for e in range(2):
            q = slice(e * SLOTS, (e + 1) * SLOTS)
            v.tensor_reduce(self.b.slot_gate[q, b:b + 1], turned[q, :, P + e:P + e + 1].rearrange("p t c -> p c t"), AX.X, ALU.add).then_inc(self.S["gt_ev"], 1)

    def hidden(self, dve, n, b):
        dve.wait_ge(self.S["silu"], n + 1)
        dve.wait_ge(self.S["gt_ev"], 3 * (n + 1))
        self.s.nc.vector.scalar_tensor_tensor(out=self.b.hid[:, :], in0=self.s.ps[:, 2, FE:2 * FE], scalar=self.b.slot_gate[:, b:b + 1],
                                              in1=self.b.silu[:, :], op0=ALU.mult, op1=ALU.mult).then_inc(self.S["hid"], 1)

    def take_hidden(self, dve, n, n0):
        dve.wait_ge(self.S["ht_ps"], n + 1)
        self.wait(dve, "o_ps", 2 * n, n0)
        self.s.nc.vector.tensor_copy(self.b.hid_t[:, :], self.s.ps[:, 2, 0:2 * P]).then_inc(self.S["ht_ev"], 1)

    def out_low(self, dve, n, b, n0):
        self.wait(dve, "sc_ps", 6 * (n + 1 - self.deep), n0 + 1 - self.deep)
        for h in range(2):
            c = slice(h * BANK, (h + 1) * BANK)
            dve.wait_ge(self.S["o_ev"], 2 * n + h + 1)
            self.s.nc.vector.tensor_tensor(self.b.o_lo[:, b, c], self.s.ps[:, 5 + h, :], self.b.o_hi[:, b, c].bitcast(F32),
                                           ALU.subtract).then_inc(self.S["lo_ev"], 1)

    def add_tokens(self, dve, n):
        v, acc = self.s.nc.vector, self.m.acc
        for q in range(6):
            t, h = divmod(q, 2)
            dve.wait_ge(self.S["sc_ps"], 6 * n + q + 1)
            a = acc[:, t, h * BANK:(h + 1) * BANK]
            v.tensor_tensor(a, a, self.s.ps[:, 4 if q % 2 else 7, :], ALU.add).then_inc(self.S["sc_ev"], 1)

    def take_gathered(self, act, n, b, n0):
        act.wait_ge(self.S["hg_ps"], n + 1)
        self.wait(act, "h_ps", 2 * (n + 1 - self.deep), n0 + 1 - self.deep)
        self.s.nc.scalar.copy(self.b.hg[:, b, :], self.s.ps[:, 0:2, :].rearrange("p b n -> p (b n)")).then_inc(self.S["hg_ev"], 1)

    def silu(self, act, n, n0):
        act.wait_ge(self.S["h_ps"], 2 * (n + 1))
        self.wait(act, "hid", n, n0)
        self.s.nc.scalar.activation(self.b.silu[:, :], self.s.ps[:, 2, 0:FE], ACT.Silu).then_inc(self.S["silu"], 1)

    def take_out(self, act, n, b, n0):
        act.wait_ge(self.S["o_ps"], 2 * (n + 1))
        self.wait(act, "sc_ps", 6 * (n + 1 - self.deep), n0 + 1 - self.deep)
        for h in range(2):
            self.s.nc.scalar.copy(self.b.o_hi[:, b, h * BANK:(h + 1) * BANK], self.s.ps[:, 5 + h, :]).then_inc(self.S["o_ev"], 1)

    def gather(self, pe, i, n, b, n0):
        s, ps, oh = self.s, self.s.ps, self.b.onehot
        pe.wait_ge(self.S["onehot"], 3 * (n + 1))
        self.wait(pe, "gt_ev", 3 * n, n0)
        for t in range(T):
            mm = pe.matmul(ps[:, 3, t * (P + 2):(t + 1) * (P + 2)], oh[:, b, t, :], self.b.turn[:, b, t, :], start=True, stop=True)
        mm.then_inc(self.S["gt_ps"], 1)
        self.wait(pe, "hg_ev", n, n0)
        for k in range(KD):
            for t in range(T):
                mm = pe.matmul(ps[:, k // 4, (k % 4) * P:(k % 4 + 1) * P], self.m.hp[:, t, k, :], oh[:, b, t, :], start=(t == 0), stop=(t == T - 1))
        mm.then_inc(self.S["hg_ps"], 1)

    def hidden_products(self, pe, n, b, n0, w13, ready):
        ps = self.s.ps
        pe.wait_ge(self.S["hg_ev"], n + 1)
        self.wait(pe, "ht_ev", n, n0)
        for e, k in self.order(pe, ready, range(KD)):
            mm = pe.matmul(ps[e * SLOTS:(e + 1) * SLOTS, 2, :], self.b.hg[:, b, k * P + e * SLOTS:k * P + (e + 1) * SLOTS],
                           w13(e)[:, k, :], start=(k == 0), stop=(k == KD - 1))
            if k == KD - 1:
                mm.then_inc(self.S["h_ps"], 1)

    def order(self, pe, ready, steps):
        if self.deep == 1:
            for e in range(2):
                ready(pe, e)
                for x in steps:
                    yield e, x
        else:
            ready(pe, 0)
            ready(pe, 1)
            for x in steps:
                yield 0, x
                yield 1, x

    def turn_hidden(self, pe, n):
        pe.wait_ge(self.S["hid"], n + 1)
        for c in range(2):
            mm = pe.transpose(self.s.ps[:, 2, c * P:(c + 1) * P], self.b.hid[:, c::2], self.s.ident)
        mm.then_inc(self.S["ht_ps"], 1)

    def out_products(self, pe, n, n0, w2, ready):
        pe.wait_ge(self.S["ht_ev"], n + 1)
        self.wait(pe, "lo_ev", 2 * n, n0)
        for e, (h, c) in self.order(pe, ready, [(h, c) for h in range(2) for c in range(2)]):
            mm = pe.matmul(self.s.ps[e * SLOTS:(e + 1) * SLOTS, 5 + h, :], self.b.hid_t[:, c * P + e * SLOTS:c * P + (e + 1) * SLOTS],
                           w2(e)[:, c, h * BANK:(h + 1) * BANK], start=(c == 0), stop=(c == 1))
            if (h, c) == (1, 1):
                mm.then_inc(self.S["o_ps"], 1)

    def scatter(self, pe, n, b, n0):
        pe.wait_ge(self.S["lo_ev"], 2 * (n + 1))
        pe.wait_ge(self.S["gt_ev"], 3 * (n + 1))
        for q in range(6):
            t, h = divmod(q, 2)
            if q >= 2 or n0 > 0:
                pe.wait_ge(self.S["sc_ev"], 6 * n + q - 1)
            for part in (self.b.o_hi, self.b.o_lo):
                mm = pe.matmul(self.s.ps[:, 4 if q % 2 else 7, :], self.b.onehot_t[:, b, t * P:(t + 1) * P],
                               part[:, b, h * BANK:(h + 1) * BANK], start=(part is self.b.o_hi), stop=(part is self.b.o_lo))
            mm.then_inc(self.S["sc_ps"], 1)


def experts(s, l, st, m):
    nc, w = s.nc, s.w
    sb = stage_buffers(s, st, f"ex{l}_")

    def buffers(pre, deep):
        b = Shared()
        b.onehot = sb(pre + "onehot", [P, deep, T, P])
        b.turn = sb(pre + "turn", [P, deep, T, P + 2])
        b.onehot_t = sb(pre + "onehot_t", [P, deep, NTOK], F32R)
        b.slot_gate = sb(pre + "slot_gate", [P, deep])
        b.hg = sb(pre + "hg", [P, deep, D])
        b.silu, b.hid = sb(pre + "silu", [P, FE]), sb(pre + "hid", [P, FE])
        b.hid_t = sb(pre + "hid_t", [P, 2 * P])
        b.o_hi, b.o_lo = (sb(pre + n, [P, deep, D], F32R) for n in ("o_hi", "o_lo"))
        return b

    w2_ring = sb("w2_ring", [P, 4, 2, D])
    bufs = buffers("", 2)
    over_w = sb("over_w", [P, KD, BANK])
    S = {n: s.sem(f"ex{l}_" + n) for n in PairSteps.NAMES}
    V = {n: s.sem(f"ov{l}_" + n) for n in PairSteps.NAMES}
    w2_full = [s.sem(f"ex{l}_w2_full{n}") for n in range(4)]
    zeroed, shifted, ov_w13, ov_w2 = (s.sem(f"ex{l}_" + n) for n in ("zeroed", "shifted", "ov_w13", "ov_w2"))
    base = s.at["moe", l]
    main = PairSteps(s, m, bufs, S, 2, base)
    over = PairSteps(s, m, bufs, V, 1, base)
    w1v = w["moe_w1"][l].rearrange("e (p k) f -> p e k f", k=KD)
    w3v = w["moe_w3"][l].rearrange("e (p k) f -> p e k f", k=KD)
    w2v = w["moe_w2"][l].rearrange("e (p c) d -> p e c d", c=2)
    block = st.enter_context(nc.Block())

    def engine_rounds(eng, steps, before):
        most = eng.value_load(m.most[0:1, 0:1], min_val=0, max_val=NTOK)
        with eng.If(most > SLOTS):
            eng.wait_ge(S["sc_ev"], 6 * PAIRS)
            for r in range(1, ROUNDS):
                before()
                first = PAIRS * (r - 1)
                steps(0, first, first)
                with eng.Fori(1, PAIRS) as i:
                    steps(i, first + i, first + 1)

    @block.sync
    def _(sp):
        def w13_load(dst, ex, done):
            for src, c in ((w1v, 0), (w3v, FE)):
                sp.dma_start(dst[:, :, c:c + FE], src[:, bass.ds(ex, 1)].rearrange("p e k f -> p (e k) f")).then_inc(done, 16)

        def w2_load(dst, ex, done):
            sp.dma_start(dst, w2v[:, bass.ds(ex, 1)].rearrange("p e c d -> p (e c) d")).then_inc(done, 16)

        for e in range(4):
            slot = (base + e) % SLOT_RING
            if s.issued <= base + e:
                sp.wait_ge(s.ring_free, base + e - SLOT_RING + 1)
                w13_load(s.ring[:, slot], e, s.ring_full[slot])
            w2_load(w2_ring[:, e], e, w2_full[e])
        with sp.Fori(0, NE // 4 - 1) as q:
            for e in range(4):
                slot = (base + e) % SLOT_RING
                sp.wait_ge(S["h_ps"], 4 * q + e + 1)
                w13_load(s.ring[:, slot], 4 * q + 4 + e, s.ring_full[slot])
                sp.wait_ge(S["o_ps"], 4 * q + e + 1)
                w2_load(w2_ring[:, e], 4 * q + 4 + e, w2_full[e])
        s.issued = base + NE
        ring_loads(s, sp, base + NE + SLOT_RING)
        sp.wait_ge(S["o_ps"], NE)

        def steps(i, n, n0):
            for e in range(2):
                if n0 + e > 0:
                    sp.wait_ge(V["h_ps"], 2 * n + e)
                w13_load(over_w, 2 * i + e, ov_w13)
                if n0 + e > 0:
                    sp.wait_ge(V["o_ps"], 2 * n + e)
                w2_load(w2_ring[:, 0], 2 * i + e, ov_w2)

        engine_rounds(sp, steps, lambda: None)

    @block.tensor
    def _(pe):
        def step(i, p, j):
            n0, b = p, p % 2
            def w13_ready(eng, e):
                x = 2 * p + e
                eng.wait_ge(s.ring_full[(base + x) % SLOT_RING], s.fill_of[base + x] + 32 * j)

            def w2_ready(eng, e):
                x = 2 * p + e
                eng.wait_ge(w2_full[x % 4], 16 * (x // 4 + 1) + 16 * j)

            main.hidden_products(pe, i, b, n0, lambda e: s.ring[:, (base + 2 * p + e) % SLOT_RING], w13_ready)
            if p < PAIRS - 1:
                main.gather(pe, i + 1, i + 1, 1 - b, n0 + 1)
            main.turn_hidden(pe, i)
            if p > 0:
                main.scatter(pe, i - 1, 1 - b, n0 - 1)
            main.out_products(pe, i, n0, lambda e: w2_ring[:, (2 * p + e) % 4], w2_ready)

        pe.wait_ge(zeroed, 1 + 2 * T)
        main.gather(pe, 0, 0, 0, 0)
        step(0, 0, 0)
        step(1, 1, 0)
        with pe.Fori(0, TURNS) as j:
            step(2 * j + 2, 2, j)
            step(2 * j + 3, 3, j)
        step(PAIRS - 2, PAIRS - 2, 0)
        step(PAIRS - 1, PAIRS - 1, 0)
        main.scatter(pe, PAIRS - 1, (PAIRS - 1) % 2, PAIRS - 1)
        pe.wait_ge(S["h_ps"], NE)
        pe.sem_inc(s.ring_free, NE)

        def steps(i, n, n0):
            over.gather(pe, i, n, 0, n0)
            over.hidden_products(pe, n, 0, n0, lambda e: over_w, lambda eng, e: eng.wait_ge(ov_w13, 64 * n + 32 * (e + 1)))
            over.turn_hidden(pe, n)
            over.out_products(pe, n, n0, lambda e: w2_ring[:, 0], lambda eng, e: eng.wait_ge(ov_w2, 32 * n + 16 * (e + 1)))
            over.scatter(pe, n, 0, n0)

        engine_rounds(pe, steps, lambda: None)

    @block.scalar
    def _(act):
        def step(i, p):
            main.silu(act, i, p)
            if p < PAIRS - 1:
                main.take_gathered(act, i + 1, (p + 1) % 2, p + 1)
            main.take_out(act, i, p % 2, p)

        main.take_gathered(act, 0, 0, 0)
        step(0, 0)
        step(1, 1)
        with act.Fori(0, TURNS) as j:
            step(2 * j + 2, 2)
            step(2 * j + 3, 3)
        step(PAIRS - 2, PAIRS - 2)
        step(PAIRS - 1, PAIRS - 1)

        def steps(i, n, n0):
            over.take_gathered(act, n, 0, n0)
            over.silu(act, n, n0)
            over.take_out(act, n, 0, n0)

        engine_rounds(act, steps, lambda: None)

    @block.vector
    def _(dve):
        def step(i, p):
            if p > 0:
                main.out_low(dve, i - 1, (p - 1) % 2, p - 1)
            main.hidden(dve, i, p % 2)
            main.take_hidden(dve, i, p)
            if p > 0:
                main.add_tokens(dve, i - 1)
            if p < PAIRS - 1:
                main.take_turned(dve, i + 1, (p + 1) % 2, p + 1)
            if p < PAIRS - 2:
                main.onehot(dve, i + 2, i + 2, p % 2, p + 2)

        nc.vector.memset(m.acc[:, :, :], 0.0).then_inc(zeroed, 1)
        for b in range(2):
            for t in range(T):
                nc.vector.tensor_copy(bufs.turn[:, b, t, 0:P], s.ident).then_inc(zeroed, 1)
        main.onehot(dve, 0, 0, 0, 0)
        main.onehot(dve, 1, 1, 1, 1)
        main.take_turned(dve, 0, 0, 0)
        step(0, 0)
        step(1, 1)
        with dve.Fori(0, TURNS) as j:
            step(2 * j + 2, 2)
            step(2 * j + 3, 3)
        step(PAIRS - 2, PAIRS - 2)
        step(PAIRS - 1, PAIRS - 1)
        main.out_low(dve, PAIRS - 1, (PAIRS - 1) % 2, PAIRS - 1)
        main.add_tokens(dve, PAIRS - 1)

        rounds = [0]

        def next_round():
            rounds[0] += 1
            if rounds[0] > 1:
                dve.wait_ge(V["hg_ps"], PAIRS * (rounds[0] - 1))
            nc.vector.tensor_scalar(m.code[:, :, :], m.code[:, :, :], -float(SLOTS), None, ALU.add).then_inc(shifted, 1)
            dve.wait_ge(shifted, rounds[0])

        def steps(i, n, n0):
            over.onehot(dve, i, n, 0, n0)
            over.take_turned(dve, n, 0, n0)
            over.hidden(dve, n, 0)
            over.take_hidden(dve, n, n0)
            over.out_low(dve, n, 0, n0)
            over.add_tokens(dve, n)

        engine_rounds(dve, steps, next_round)


TURNS = (PAIRS - 4) // 2


def add_moe(s, l, st, m):
    nc, ps = s.nc, s.ps
    g_ps, mul = s.sem(f"am{l}_g_ps"), s.sem(f"am{l}_mul")
    block = st.enter_context(nc.Block())

    @block.tensor
    def _(pe):
        for g in range(2):
            for h in range(2):
                mm = pe.matmul(ps[:, 2 * g + h, :], s.cid("pick")[0:2, g * P:(g + 1) * P], s.gates[0:2, FFN, h * BANK:(h + 1) * BANK],
                               start=True, stop=True)
        mm.then_inc(g_ps, 1)

    @block.vector
    def _(dve):
        v = nc.vector
        dve.wait_ge(g_ps, 1)
        for n in range(2 * T):
            t, h = divmod(n, 2)
            a = m.acc[:, t, h * BANK:(h + 1) * BANK]
            v.tensor_tensor(a, a, ps[:, 2 * min(t, 1) + h, :], ALU.mult).then_inc(mul, 1)
        for n in range(2 * T):
            t, h = divmod(n, 2)
            dve.wait_ge(mul, n + 1)
            ys = s.y[:, t, h * BANK:(h + 1) * BANK]
            v.tensor_tensor(ys, ys, m.acc[:, t, h * BANK:(h + 1) * BANK], ALU.add)


_INS = ["x_prompt", "x_sample", "cache_a_k", "cache_a_v", "cache_b_ckv", "cache_b_krope", "state_c_fwd", "state_c_bwd",
        "c", "c_ctx", "ada_w", "ada_b", "norm_mix", "norm_ffn",
        "att_w_in", "att_a_qnorm", "att_a_knorm", "att_a_sink", "att_b_qa_norm", "att_b_wuq", "att_b_kva_norm",
        "att_b_wukv", "att_b_qnorm", "att_b_knorm", "att_w_out",
        "ssd_w_in", "ssd_conv_w", "ssd_conv_b", "ssd_alog_fwd", "ssd_alog_bwd", "ssd_dtb_fwd", "ssd_dtb_bwd", "ssd_d",
        "ssd_norm", "ssd_w_out", "moe_wg", "moe_bg", "moe_we", "moe_be", "moe_w1", "moe_w3", "moe_w2"]
_OUTS = [("y_prompt", (1, 128, 1024)), ("y_sample", (1, 256, 1024)), ("new_a_k", (1, 1, 128, 2, 64)),
         ("new_a_v", (1, 1, 128, 2, 64)), ("new_b_ckv", (1, 1, 128, 128)), ("new_b_krope", (1, 1, 128, 32)),
         ("new_state_fwd", (1, 1, 32, 64, 128)), ("new_state_bwd", (1, 1, 32, 64, 128))]


def kernel(**inputs):
    import concourse.bacc as _bacc
    from concourse.bass_utils import run_bass_kernel_spmd as _run

    nc = _bacc.Bacc("TRN2", target_bir_lowering=False, num_devices=1)
    arrays, ins, outs = {}, {}, {}
    given = {name: inputs[name] for name in _INS}
    given["consts"] = const_table()[0]
    for name, value in given.items():
        a = np.ascontiguousarray(value)
        arrays[f"in_{name}_dram"] = a
        ins[name] = nc.dram_tensor(f"in_{name}_dram", a.shape, mybir.dt.from_np(a.dtype), kind="ExternalInput").ap()
    for name, shape in _OUTS:
        outs[name] = nc.dram_tensor(f"out_{name}_dram", shape, F32, kind="ExternalOutput").ap()
    build(nc, ins, outs)
    r = _run(nc, [arrays], core_ids=[0])
    return tuple(r.results[0][f"out_{name}_dram"] for name, _ in _OUTS)
```

```python
from contextlib import ExitStack

import numpy as np
import concourse.bass as bass
from concourse import mybir

P = 128
D = 1024
KD = D // P
T = 3
NTOK = T * P
F32 = mybir.dt.float32
I32 = mybir.dt.int32
F32R = mybir.dt.float32r
BF16 = mybir.dt.bfloat16
ALU = mybir.AluOpType
ACT = mybir.ActivationFunctionType
AX = mybir.AxisListType
EPS = 1e-6
BIG = 1e30
BANK = 512

HD_A, HD_B, NOPE, ROPE, V_B = 64, 96, 64, 32, 64
IN_ATT = 1184
H_C, P_C, G_C, N_C, D_INNER = 32, 64, 8, 128, 2048
CONV_CH = 4096
R_C = H_C // G_C
NE, NG, PER, FE = 32, 4, 8, 256
SLOTS = 64
PAIRS = NE // 2
ROUNDS = NTOK // SLOTS

SLOT_RING = 4
MIX, FFN = 0, 1


def const_table():
    i = np.arange(P)
    low = (i[None, :] <= i[:, None])
    high = (i[None, :] >= i[:, None])
    cols, at = [], {}

    def put(name, a):
        a = np.broadcast_to(np.asarray(a, np.float32), (P, a.shape[1]))
        at[name] = (sum(c.shape[1] for c in cols), a.shape[1])
        cols.append(a)

    put("ident", np.eye(P))
    put("ones", np.ones((P, P)))
    put("upto", high)
    put("from_", low)
    put("before", i[None, :] > i[:, None])
    put("mask_high", np.where(high, 0.0, -BIG))
    put("mask_low", np.where(low, 0.0, -BIG))
    put("slot_no", np.arange(SLOTS)[None, :])
    put("rank32", np.arange(NE, 0, -1)[None, :])
    put("rank4", np.arange(NG, 0, -1)[None, :])
    pick = np.zeros((P, 2 * P), np.float32)
    pick[[0, 32], 0:P] = 1
    pick[[1, 33], P:] = 1
    put("pick", pick)
    put("sum4", np.stack([(i % 32 == g) for g in range(2)], axis=1))
    tok = np.arange(2 * P)
    for name, rot in (("a", HD_A), ("b", ROPE)):
        quarter = rot // 4
        inv = np.float32(10000.0) ** (-np.arange(quarter, dtype=np.float32) / np.float32(quarter))
        ar = (tok // 64).astype(np.float32)[:, None] * inv[None, :]
        ac = (tok % 64).astype(np.float32)[:, None] * inv[None, :]
        ang = np.concatenate([ar, ar, ac, ac], axis=1).astype(np.float32)
        sign = np.repeat(np.array([-1, 1, -1, 1], np.float32), quarter)
        cos, sin = np.cos(ang), np.sin(ang) * sign[None, :]
        put("cos_" + name, cos.reshape(2, P, rot).transpose(1, 0, 2).reshape(P, 2 * rot))
        put("sin_" + name, sin.reshape(2, P, rot).transpose(1, 0, 2).reshape(P, 2 * rot))
    return np.ascontiguousarray(np.concatenate(cols, axis=1)), at


class Shared:
    pass


def stream_plan(w):
    plan, at = [], {}

    def add(stage, key, *moves):
        at[stage, key] = len(plan)
        plan.append(moves)

    def cols(a, c0, n, k0=0):
        return (lambda slot: slot[:, :, 0:n] if n == BANK else slot[:, :, 0:n],
                a[:, k0:k0 + KD, c0:c0 + n])

    def ada(l):
        for j in range(12):
            add(("ada", l), j, cols(w["ada_w"][l].rearrange("(p k) n -> p k n", k=KD), j * BANK, BANK))

    for l in range(2):
        if l == 0:
            ada(0)
            win = w["att_w_in"][0].rearrange("(p k) n -> p k n", k=KD)
            for j, n in enumerate((512, 512, 160)):
                add("att_in", j, cols(win, j * BANK, n))
            wuq = w["att_b_wuq"][0].rearrange("(k p) n -> p k n", p=P)
            wukv = w["att_b_wukv"][0]
            add("att_up", 0,
                (lambda s: s.rearrange("p k n -> p (k n)")[:, 0:1536].rearrange("p (k n) -> p k n", k=2), wuq),
                (lambda s: s.rearrange("p k n -> p (k n)")[:, 1536:2560], wukv))
            ada(1)
            wout = w["att_w_out"][0].rearrange("(p k) n -> p k n", k=KD)
            for j in range(2):
                add("att_out", j, cols(wout, j * BANK, BANK))
        else:
            win = w["ssd_w_in"][0].rearrange("(p k) n -> p k n", k=KD)
            for j in range(8):
                add("ssd_xbc", j, cols(win, D_INNER + j * BANK, BANK))
            add("ssd_dt", 0, cols(win, D_INNER + CONV_CH, 2 * H_C))
            for j in range(4):
                add("ssd_z", j, cols(win, j * BANK, BANK))
            wout = w["ssd_w_out"][0].rearrange("(k p) n -> p k n", p=P)
            for j in range(2):
                for kh in range(2):
                    add("ssd_out", (j, kh), cols(wout, j * BANK, BANK, kh * KD))
        at["moe", l] = len(plan)
        for e in range(SLOT_RING):
            plan.append(tuple((lambda slot, c=c: slot[:, :, c:c + FE], w[name][l, e].rearrange("(p k) f -> p k f", k=KD))
                              for name, c in (("moe_w1", 0), ("moe_w3", FE))))
        plan.extend([None] * (NE - SLOT_RING))
    return plan, at


def build(nc, w, out):
    ctx = ExitStack()
    s = Shared()
    with ctx:
        def sb(name, shape, dt=F32):
            return ctx.enter_context(nc.sbuf_tensor(name, shape, dt))

        def sem(name):
            return ctx.enter_context(nc.semaphore(name))

        s.nc, s.w, s.out = nc, w, out
        s.ps = ctx.enter_context(nc.psum_tensor("ps", [P, 8, BANK], F32))
        s.y = sb("y", [P, T, D])
        s.hT = sb("hT", [P, KD, NTOK])
        s.ring = sb("ring", [P, SLOT_RING, KD, BANK])
        s.gates = sb("gates", [34, 2, D])
        s.shift = sb("shift", [P, 2, 2, KD, 2])
        s.gain = sb("gain", [P, 2, 2, KD, 2])
        _, s.cat = const_table()
        s.consts = sb("consts", [P, w["consts"].shape[1]])
        s.cid = lambda name: s.consts[:, s.cat[name][0]:s.cat[name][0] + s.cat[name][1]]
        s.ident = s.cid("ident")
        s.ring_full = [sem(f"ring_full{n}") for n in range(SLOT_RING)]
        s.ring_free = sem("ring_free")
        s.plan, s.at = stream_plan(w)
        s.fill_of = fill_counts(s)
        s.issued = 0
        s.loads = sem("loads")
        s.loaded = 0
        s.stores = sem("stores")
        s.stored = 0
        s.chain = {e: sem(f"chain_{e}") for e in ("dve", "act")}
        s.chained = {"dve": 0, "act": 0}

        for l in range(2):
            layer = ctx.enter_context(ExitStack())
            own = []

            def layer_sem(name, layer=layer, own=own):
                own.append(layer.enter_context(nc.semaphore(name)))
                return own[-1]

            s.sem = layer_sem
            if l == 0:
                with ExitStack() as ada:
                    s.silu_c = ada.enter_context(nc.sbuf_tensor("silu_c", [P, KD, 32], F32))
                    with ExitStack() as st:
                        ada_stage(s, st)
                    with ExitStack() as st:
                        norm_stage(s, l, MIX, st)
                    with ExitStack() as st:
                        attention(s, st)
            else:
                with ExitStack() as st:
                    norm_stage(s, l, MIX, st)
                with ExitStack() as st:
                    ssd(s, st)
            with ExitStack() as st:
                moe(s, l, st)
            if l == 0:
                with nc.Block() as block:
                    @block.gpsimd
                    def _(pool):
                        for one in own:
                            pool.sem_clear(one)
                layer.close()
        store_y(s)


def narrow_matmul(pe, dst, lhs, rhs, start, stop):
    for q in (slice(0, 64), slice(64, 128)):
        mm = pe.matmul(dst[q], lhs[:, q], rhs, start=start, stop=stop)
    return mm


def link(s, name, eng, ins):
    s.chained[name] += 1
    ins.then_inc(s.chain[name], 1)
    eng.wait_ge(s.chain[name], s.chained[name])


def ring_loads(s, sp, upto):
    while s.issued < min(upto, len(s.plan)):
        n = s.issued
        if s.plan[n] is None:
            break
        if n >= SLOT_RING:
            sp.wait_ge(s.ring_free, n - SLOT_RING + 1)
        slot = s.ring[:, n % SLOT_RING]
        for part, src in s.plan[n]:
            sp.dma_start(part(slot), src).then_inc(s.ring_full[n % SLOT_RING], 16)
        s.issued += 1


def fill_counts(s):
    total, out = [0] * SLOT_RING, []
    for n, moves in enumerate(s.plan):
        total[n % SLOT_RING] += 16 * (2 if moves is None else len(moves))
        out.append(total[n % SLOT_RING])
    return out


def ring_wait(s, pe, n):
    pe.wait_ge(s.ring_full[n % SLOT_RING], s.fill_of[n])


def stage_buffers(s, st, prefix):
    def sb(name, shape, dt=F32):
        return st.enter_context(s.nc.sbuf_tensor(prefix + name, shape, dt))
    return sb


def ada_stage(s, st):
    nc, w, ps = s.nc, s.w, s.ps
    l = 0
    sb = stage_buffers(s, st, f"ada{l}_")
    cond = sb("cond", [P, 2, KD])
    silu_c = s.silu_c
    part = sb("part", [P, 2, BANK])
    bias = sb("bias", [2, 6 * D])
    row = sb("row", [2, 6 * D])
    norm_g = sb("norm_g", [P, 2, KD])
    mod_t = sb("mod_t", [P, 4, KD, 2])
    silu_ready, col_ps, col_done, t_ps = (s.sem(f"ada{l}_{x}") for x in ("silu", "col_ps", "col_done", "t_ps"))
    zero, part_ev, sum_ps = (s.sem(f"ada{l}_{x}") for x in ("zero", "part_ev", "sum_ps"))
    base = s.at[("ada", l), 0]
    block = st.enter_context(nc.Block())

    @block.sync
    def _(sp):
        n = 0
        loads = [(cond[:, 0, :], w["c_ctx"].rearrange("(p k) -> p k", k=KD)),
                 (cond[:, 1, :], w["c"][0].rearrange("(p k) -> p k", k=KD)),
                 (norm_g[:, 0, :], w["norm_mix"][l].rearrange("(p k) -> p k", k=KD)),
                 (norm_g[:, 1, :], w["norm_ffn"][l].rearrange("(p k) -> p k", k=KD)),
                 (bias[0:1, :], w["ada_b"][l:l + 1, :]),
                 (bias[1:2, :], w["ada_b"][l:l + 1, :]),
                 (s.consts[:, :], w["consts"]),
                 (s.y[:, 0, :], w["x_prompt"][0]),
                 (s.y[:, 1:3, :], w["x_sample"][0].rearrange("(t p) d -> p t d", p=P))]
        for dst, src in loads:
            sp.dma_start(dst, src).then_inc(s.loads, 16)
            n += 16
        s.loaded += n
        ring_loads(s, sp, base + 12 + SLOT_RING)

    @block.scalar
    def _(act):
        act.wait_ge(zero, 1)
        act.wait_ge(s.loads, s.loaded)
        nc.scalar.activation(silu_c[:, :, 0:2].rearrange("p k g -> p g k"), cond[:, :, :], ACT.Silu).then_inc(silu_ready, 1)
        for j in range(12):
            act.wait_ge(s.ring_free, base + j + 1)
            if j >= 2:
                act.wait_ge(sum_ps, j - 1)
            nc.scalar.copy(part[:, j % 2, :], ps[:, j % 2, :]).then_inc(part_ev, 1)

    @block.tensor
    def _(pe):
        pe.wait_ge(silu_ready, 1)

        def add_up(j):
            pe.wait_ge(part_ev, j + 1)
            if j >= 2:
                pe.wait_ge(col_done, j - 1)
            pe.matmul(ps[0:2, 3 + j % 2, :], s.cid("sum4"), part[:, j % 2, :], start=True, stop=True).then_inc(sum_ps, 1)

        for j in range(12):
            ring_wait(s, pe, base + j)
            if j >= 2:
                pe.wait_ge(part_ev, j - 1)
            for k in range(KD):
                c = 32 * (k % 4)
                mm = pe.matmul(ps[c:c + 32, j % 2, :], silu_c[:, k, :], s.ring[:, (base + j) % SLOT_RING, k, :],
                               start=(k < 4), stop=(k >= 4))
            mm.then_inc(s.ring_free, 1)
            if j:
                add_up(j - 1)
        add_up(11)
        pe.wait_ge(col_done, 12)
        pe.wait_ge(s.loads, s.loaded)
        for qi, q in enumerate((0, 1, 3, 4)):
            for k in range(KD):
                c = (qi * KD + k) * 2
                mm = pe.transpose(ps[:, 2, c:c + 2], row[0:2, q * D + k:(q + 1) * D:KD], s.ident[0:2, 0:2])
        mm.then_inc(t_ps, 1)

    @block.vector
    def _(dve):
        nc.vector.memset(silu_c[:, :, :], 0.0).then_inc(zero, 1)
        dve.wait_ge(s.loads, s.loaded)
        for j in range(12):
            dve.wait_ge(sum_ps, j + 1)
            q, h = divmod(j, 2)
            dst = s.gates[0:2, q // 3, h * BANK:(h + 1) * BANK] if q in (2, 5) else row[:, j * BANK:(j + 1) * BANK]
            nc.vector.tensor_tensor(dst, ps[0:2, 3 + j % 2, :], bias[:, j * BANK:(j + 1) * BANK], ALU.add).then_inc(col_done, 1)
        dve.wait_ge(t_ps, 1)
        link(s, "dve", dve, nc.vector.tensor_copy(mod_t[:, :, :, :].rearrange("p q k g -> p (q k g)"), ps[:, 2, 0:4 * KD * 2]))
        shift_and_gain(s, dve, l, mod_t, norm_g)


def shift_and_gain(s, dve, l, mod_t, norm_g):
    for m in (MIX, FFN):
        link(s, "dve", dve, s.nc.vector.tensor_copy(s.shift[:, l, m, :, :], mod_t[:, 2 * m, :, :]))
        g = norm_g[:, m, :].unsqueeze(2).broadcast_to([P, KD, 2])
        link(s, "dve", dve, s.nc.vector.scalar_tensor_tensor(
            out=s.gain[:, l, m, :, :], in0=mod_t[:, 2 * m + 1, :, :], scalar=1.0, in1=g, op0=ALU.add, op1=ALU.mult))


class NextModulation:

    CHUNKS = 12

    def __init__(self, s, sb):
        self.s = s
        self.part = sb("mod_part", [P, BANK])
        self.row = sb("mod_row", [34, 4, D])
        self.norm_g = sb("mod_norm_g", [P, 2, KD])
        self.mod_t = sb("mod_t", [P, 4, KD, 2])
        self.part_ps, self.part_ev, self.sum_ps, self.sum_ev, self.t_ps = (
            s.sem("mod_" + n) for n in ("part_ps", "part_ev", "sum_ps", "sum_ev", "t_ps"))

    def loads(self):
        s, w = self.s, self.s.w
        bias = w["ada_b"][1:2, :].rearrange("o (q d) -> o q d", q=6)
        out = [(self.norm_g[:, 0, :], w["norm_mix"][1].rearrange("(p k) -> p k", k=KD)),
               (self.norm_g[:, 1, :], w["norm_ffn"][1].rearrange("(p k) -> p k", k=KD))]
        for r in (32, 33):
            for m in range(2):
                out += [(self.row[r:r + 1, 2 * m:2 * m + 2, :], bias[:, 3 * m:3 * m + 2, :]),
                        (s.gates[r:r + 1, m, :], bias[:, 3 * m + 2, :])]
        return out

    def products(self, pe, j):
        s = self.s
        n = s.at[("ada", 1), j]
        ring_wait(s, pe, n)
        if j:
            pe.wait_ge(self.sum_ev, j)
        for k in range(KD):
            c = 32 * (k % 4)
            mm = pe.matmul(s.ps[c:c + 32, 7, :], s.silu_c[:, k, :], s.ring[:, n % SLOT_RING, k, :], start=(k < 4), stop=(k >= 4))
        mm.then_inc(self.part_ps, 1)

    def take_part(self, dve, j):
        dve.wait_ge(self.part_ps, j + 1)
        self.s.nc.vector.tensor_copy(self.part[:, :], self.s.ps[:, 7, :]).then_inc(self.part_ev, 1)

    def sum(self, pe, j):
        pe.wait_ge(self.part_ev, j + 1)
        pe.sem_inc(self.s.ring_free, 1)
        pe.matmul(self.s.ps[32:34, 7, :], self.s.cid("sum4"), self.part[:, :], start=True, stop=True).then_inc(self.sum_ps, 1)

    def add_bias(self, dve, j):
        q, c = divmod(j, 2)
        row = self.s.gates[32:34, q // 3, :] if q in (2, 5) else self.row[32:34, q - q // 3, :]
        dst = row[:, BANK * c:BANK * (c + 1)]
        dve.wait_ge(self.sum_ps, j + 1)
        self.s.nc.vector.tensor_tensor(dst, self.s.ps[32:34, 7, :], dst, ALU.add).then_inc(self.sum_ev, 1)

    def turn(self, pe):
        pe.wait_ge(self.sum_ev, self.CHUNKS)
        for q in range(4):
            for k in range(KD):
                c = (q * KD + k) * 2
                mm = pe.transpose(self.s.ps[:, 7, c:c + 2], self.row[32:34, q, k::KD], self.s.ident[32:34, 32:34])
        mm.then_inc(self.t_ps, 1)

    def take_turned(self, dve):
        dve.wait_ge(self.t_ps, 1)
        link(self.s, "dve", dve, self.s.nc.vector.tensor_copy(self.mod_t[:, :, :, :].rearrange("p q k g -> p (q k g)"), self.s.ps[:, 7, 0:4 * KD * 2]))
        shift_and_gain(self.s, dve, 1, self.mod_t, self.norm_g)


def rsqrt_act(s, act, x, r0, x_ready, x_count, r0_ready):
    act.wait_ge(x_ready, x_count)
    link(s, "act", act, s.nc.scalar.activation(r0, x, ACT.Ln))
    s.nc.scalar.activation(r0, r0, ACT.Exp, scale=-0.5).then_inc(r0_ready, 1)


def rsqrt_dve(s, dve, x, r0, tmp, r0_ready, count):
    v = s.nc.vector
    dve.wait_ge(r0_ready, count)
    link(s, "dve", dve, v.tensor_tensor(tmp, r0, r0, ALU.mult))
    link(s, "dve", dve, v.tensor_tensor(tmp, tmp, x, ALU.mult))
    link(s, "dve", dve, v.tensor_scalar(tmp, tmp, -0.5, 1.5, ALU.mult, ALU.add))
    link(s, "dve", dve, v.tensor_tensor(r0, r0, tmp, ALU.mult))


def norm_stage(s, l, m, st, hp=None):
    nc, ps = s.nc, s.ps
    pre = f"n{l}{m}_"
    sb = stage_buffers(s, st, pre)
    sq = sb("sq", [P, D])
    ss = sb("ss", [P, T])
    x = sb("x", [P, T])
    r = sb("r", [P, T])
    tmp = sb("tmp", [P, T])
    hn = sb("hn", [P, T, KD, P])
    ss_ready, x_ready, r_ready, hn_ready, t_ps, ev_a, ev_d, b_ps, hi_ev = (
        s.sem(pre + n) for n in ("ss", "x", "r", "hn", "t_ps", "ev_a", "ev_d", "b_ps", "hi_ev"))
    block = st.enter_context(nc.Block())

    @block.scalar
    def _(act):
        for t in range(T):
            if t:
                act.wait_ge(ss_ready, t)
            nc.scalar.activation(sq[:, :], s.y[:, t, :], ACT.Square, accum_out=ss[:, t:t + 1]).then_inc(ss_ready, 1)
        rsqrt_act(s, act, x[:, :], r[:, :], x_ready, 1, r_ready)
        for t in range(T):
            act.wait_ge(t_ps, t + 1)
            for k in range(4, KD):
                nc.scalar.activation(s.hT[:, k, t * P:(t + 1) * P], ps[:, 2 * t + 1, (k - 4) * P:(k - 3) * P], ACT.Identity,
                                     scale=s.gain[:, l, m, k, min(t, 1):min(t, 1) + 1],
                                     bias=s.shift[:, l, m, k, min(t, 1):min(t, 1) + 1]).then_inc(ev_a, 1)
        if hp is not None:
            for t in range(T):
                act.wait_ge(b_ps, t + 1)
                nc.scalar.copy(hp[0][:, t, :, :].rearrange("n k p -> n (k p)"),
                               ps[:, 2 * t:2 * t + 2, :].rearrange("n b c -> n (b c)")).then_inc(hi_ev, 1)

    @block.vector
    def _(dve):
        dve.wait_ge(ss_ready, T)
        nc.vector.tensor_scalar(x[:, :], ss[:, :], 1.0 / D, EPS, ALU.mult, ALU.add).then_inc(x_ready, 1)
        rsqrt_dve(s, dve, x[:, :], r[:, :], tmp[:, :], r_ready, 1)
        for t in range(T):
            nc.vector.tensor_scalar(hn[:, t, :, :], s.y[:, t, :].rearrange("n (p k) -> n k p", k=KD),
                                    r[:, t:t + 1], None, ALU.mult).then_inc(hn_ready, 1)
        for t in range(T):
            dve.wait_ge(t_ps, t + 1)
            for k in range(4):
                g = min(t, 1)
                nc.vector.tensor_scalar(s.hT[:, k, t * P:(t + 1) * P], ps[:, 2 * t, k * P:(k + 1) * P],
                                        s.gain[:, l, m, k, g:g + 1], s.shift[:, l, m, k, g:g + 1],
                                        ALU.mult, ALU.add).then_inc(ev_d, 1)
        if hp is not None:
            for t in range(T):
                dve.wait_ge(hi_ev, t + 1)
                nc.vector.tensor_tensor(hp[1][:, t, :, :].rearrange("n k p -> n (k p)"),
                                        ps[:, 2 * t:2 * t + 2, :].rearrange("n b c -> n (b c)"),
                                        hp[0][:, t, :, :].rearrange("n k p -> n (k p)").bitcast(F32), ALU.subtract)

    @block.tensor
    def _(pe):
        for t in range(T):
            pe.wait_ge(hn_ready, t + 1)
            for k in range(KD):
                mm = pe.transpose(ps[:, 2 * t + k // 4, (k % 4) * P:(k % 4 + 1) * P], hn[:, t, k, :], s.ident)
            mm.then_inc(t_ps, 1)
        if hp is not None:
            for t in range(T):
                pe.wait_ge(ev_a, 4 * (t + 1))
                pe.wait_ge(ev_d, 4 * (t + 1))
                for k in range(KD):
                    mm = pe.transpose(ps[:, 2 * t + k // 4, (k % 4) * P:(k % 4 + 1) * P],
                                      s.hT[:, k, t * P:(t + 1) * P], s.ident)
                mm.then_inc(b_ps, 1)


def store_y(s):
    nc = s.nc
    with nc.Block() as block:
        @block.sync
        def _(sp):
            sp.dma_start(s.out["y_prompt"][0], s.y[:, 0, :]).then_inc(s.stores, 16)
            sp.dma_start(s.out["y_sample"][0].rearrange("(t p) d -> p t d", p=P), s.y[:, 1:3, :]).then_inc(s.stores, 16)
            s.stored += 32
            sp.wait_ge(s.stores, s.stored)


NTB = 7


def attention(s, st):
    att_tiles = ExitStack()
    sb = stage_buffers(s, st, "att_")
    qk_t = sb("qk_t", [P, T, 4, P])
    k_t = sb("k_t", [P, 2, 4, P])
    v_a = sb("v_a", [P, 4, P])
    qkb_t = sb("qkb_t", [HD_B, 8, NTB, P])
    v_b = sb("v_b", [P, 4, 8, V_B])
    small = sb("small", [P, 8])
    with att_tiles:
        att_project(s, att_tiles, qk_t, k_t, v_a, qkb_t, v_b, small)
    with ExitStack() as st2:
        att_scores(s, st2, qk_t, k_t, v_a, qkb_t, v_b, small)


def att_project(s, st, qk_t, k_t, v_a, qkb_t, v_b, sink):
    nc, w, ps, out = s.nc, s.w, s.ps, s.out
    sb = stage_buffers(s, st, "prj_")
    proj = sb("proj", [P, T, IN_ATT])
    heads = sb("heads", [P, T, 10, 64])
    cache_k = sb("cache_k", [P, P])
    cache_c = sb("cache_c", [P, P])
    cache_r = sb("cache_r", [P, ROPE])
    q_gain, k_gain = sb("q_gain", [P, 64]), sb("k_gain", [P, 64])
    qa_gain, kva_gain = sb("qa_gain", [P, 256]), sb("kva_gain", [P, P])
    b_gain = sb("b_gain", [P, 2, HD_B])
    lat_t = sb("lat_t", [P, 2, NTOK])
    ckv_t = sb("ckv_t", [P, 4 * P])
    qkb = sb("qkb", [P, NTB, 8, HD_B])
    ss = sb("ss", [P, T, 12])
    x, r, tmp = sb("x", [P, T * 12]), sb("r", [P, T * 12]), sb("tmp", [P, T * 12])
    ssb = sb("ssb", [P, NTB * 8])
    xb, rb, tmpb = sb("xb", [P, NTB * 8]), sb("rb", [P, NTB * 8]), sb("tmpb", [P, NTB * 8])
    sq = s.hT[:, :, :].rearrange("p k n -> p (k n)")
    rot = sb("rot", [P, 8, 64])
    names = ("in_ps", "in_a", "in_d", "norm_x", "norm_r", "heads_ready", "lat_ready", "ta_ps", "ta_ev",
             "tl_ps", "tl_ev", "up_ps", "up_a", "up_d", "b_x", "b_r", "b_ready", "tb_ps", "tb_ev", "zero")
    S = {n: s.sem("prj_" + n) for n in names}
    in0, up0 = s.at["att_in", 0], s.at["att_up", 0]
    widths = (512, 512, 160)
    slot = [s.ring[:, (in0 + j) % SLOT_RING] for j in range(3)]
    up = s.ring[:, up0 % SLOT_RING].rearrange("p k n -> p (k n)")
    wuq = up[:, 0:1536].rearrange("p (k n) -> p k n", k=2)
    wukv = up[:, 1536:2560]
    block = st.enter_context(nc.Block())

    @block.sync
    def _(sp):
        loads = [(cache_k[:, :], w["cache_a_k"][0, 0].rearrange("n h d -> n (h d)")),
                 (v_a[:, 3, :], w["cache_a_v"][0, 0].rearrange("n h d -> n (h d)")),
                 (cache_c[:, :], w["cache_b_ckv"][0, 0]),
                 (cache_r[:, :], w["cache_b_krope"][0, 0]),
                 (q_gain[:, :], w["att_a_qnorm"][0].partition_broadcast(P)),
                 (k_gain[:, :], w["att_a_knorm"][0].partition_broadcast(P)),
                 (qa_gain[:, :], w["att_b_qa_norm"][0].partition_broadcast(P)),
                 (kva_gain[:, :], w["att_b_kva_norm"][0].partition_broadcast(P)),
                 (b_gain[:, 0, :], w["att_b_qnorm"][0].partition_broadcast(P)),
                 (b_gain[:, 1, :], w["att_b_knorm"][0].partition_broadcast(P)),
                 (sink[:, :], w["att_a_sink"][0].partition_broadcast(P))]
        for dst, src in loads:
            sp.dma_start(dst, src).then_inc(s.loads, 16)
        s.loaded += 16 * len(loads)
        ring_loads(s, sp, up0 + 1 + SLOT_RING)
        sp.wait_ge(S["in_a"], 5)
        sp.wait_ge(S["in_d"], 4)
        sp.dma_start(out["new_a_v"][0, 0].rearrange("n h d -> n (h d)"), proj[:, 0, 640:768]).then_inc(s.stores, 16)
        sp.dma_start(out["new_b_krope"][0, 0], proj[:, 0, 1152:1184]).then_inc(s.stores, 16)
        sp.wait_ge(S["heads_ready"], 1)
        sp.dma_start(out["new_a_k"][0, 0], heads[:, 0, 8:10, :]).then_inc(s.stores, 16)
        sp.wait_ge(S["lat_ready"], 1)
        sp.dma_start(out["new_b_ckv"][0, 0], proj[:, 0, 1024:1152]).then_inc(s.stores, 16)
        s.stored += 64
        sp.wait_ge(s.stores, s.stored)

    units = [(c, t) for c in range(3) for t in range(T)]

    @block.tensor
    def _(pe):
        for n, (c, t) in enumerate(units):
            if t == 0:
                ring_wait(s, pe, in0 + c)
            if n >= 8:
                pe.wait_ge(S["in_a"], 1)
            for k in range(KD):
                mm = pe.matmul(ps[:, n % 8, 0:widths[c]], s.hT[:, k, t * P:(t + 1) * P], slot[c][:, k, 0:widths[c]],
                               start=(k == 0), stop=(k == KD - 1))
            mm.then_inc(S["in_ps"], 1)
            if t == T - 1:
                pe.wait_ge(S["in_ps"], n + 1)
                pe.sem_inc(s.ring_free, 1)
        pe.wait_ge(S["in_a"], 5)
        pe.wait_ge(S["in_d"], 4)
        pe.wait_ge(S["lat_ready"], 1)
        pe.wait_ge(s.loads, s.loaded)
        for t in range(T):
            for c in range(2):
                mm = pe.transpose(ps[:, c, t * P:(t + 1) * P], proj[:, t, 768 + c * P:768 + (c + 1) * P], s.ident)
            mm = pe.transpose(ps[:, 2, t * P:(t + 1) * P], proj[:, t, 1024:1152], s.ident)
        mm = pe.transpose(ps[:, 2, 3 * P:4 * P], cache_c[:, :], s.ident)
        mm.then_inc(S["tl_ps"], 1)
        pe.wait_ge(S["tl_ev"], 1)
        ring_wait(s, pe, up0)
        for n in range(NTB):
            b = 4 + 2 * (n % 2)
            if n >= 2:
                pe.wait_ge(S["up_d"], n - 1)
            if n < T:
                for h in range(2):
                    for k in range(2):
                        mm = pe.matmul(ps[:, b + h, 0:384], lat_t[:, k, n * P:(n + 1) * P], wuq[:, k, h * 384:(h + 1) * 384],
                                       start=(k == 0), stop=(k == 1))
            else:
                for h in range(2):
                    mm = pe.matmul(ps[:, b + h, :], ckv_t[:, (n - T) * P:(n - T + 1) * P], wukv[:, h * BANK:(h + 1) * BANK],
                                   start=True, stop=True)
            mm.then_inc(S["up_ps"], 1)
        pe.wait_ge(S["up_ps"], NTB)
        pe.sem_inc(s.ring_free, 1)
        pe.wait_ge(S["heads_ready"], 2)
        for t in range(T):
            for j in range(4):
                pe.transpose(ps[:, t, j * P:(j + 1) * P], heads[:, t, 2 * j:2 * j + 2, :].rearrange("n a d -> n (a d)"), s.ident)
            mm = pe.transpose(ps[:, 3, t * P:(t + 1) * P], heads[:, t, 8:10, :].rearrange("n a d -> n (a d)"), s.ident)
        mm = pe.transpose(ps[:, 3, 3 * P:4 * P], cache_k[:, :], s.ident)
        mm.then_inc(S["ta_ps"], 1)
        pe.wait_ge(S["up_d"], NTB)
        for n in range(NTB):
            b = 4 + 2 * (n % 2)
            if n >= 2:
                pe.wait_ge(S["tb_ev"], n - 1)
            if n == 0:
                pe.wait_ge(S["b_ready"], 1)
            for h in range(8):
                mm = pe.transpose(ps[0:HD_B, b + h // 4, (h % 4) * P:(h % 4 + 1) * P], qkb[:, n, h, :], s.ident)
            mm.then_inc(S["tb_ps"], 1)

    @block.scalar
    def _(act):
        for n, (c, t) in enumerate(units):
            if n % 2 == 0:
                act.wait_ge(S["in_ps"], n + 1)
                nc.scalar.copy(proj[:, t, c * BANK:c * BANK + widths[c]], ps[:, n % 8, 0:widths[c]]).then_inc(S["in_a"], 1)
        rsqrt_act(s, act, x[:, :], r[:, :], S["norm_x"], 1, S["norm_r"])
        act.wait_ge(S["tl_ps"], 1)
        link(s, "act", act, nc.scalar.copy(lat_t[:, :, :], ps[:, 0:2, 0:NTOK]))
        nc.scalar.copy(ckv_t[:, :], ps[:, 2, :]).then_inc(S["tl_ev"], 1)
        act.wait_ge(S["ta_ps"], 1)
        nc.scalar.copy(qk_t[:, :, :, :].rearrange("p t j n -> p (t j n)"), ps[:, 0:3, :].rearrange("p b n -> p (b n)")).then_inc(S["ta_ev"], 1)
        act.wait_ge(S["zero"], 1)
        for g in range(2):
            q = slice(64 * g, 64 * g + 64)
            nc.scalar.copy(k_t[q, g, :, :].rearrange("p t n -> p (t n)"), ps[q, 3, :]).then_inc(S["ta_ev"], 1)
        rsqrt_act(s, act, xb[:, :], rb[:, :], S["b_x"], 1, S["b_r"])
        for n in range(NTB):
            b = 4 + 2 * (n % 2)
            act.wait_ge(S["tb_ps"], n + 1)
            nc.scalar.copy(qkb_t[:, :, n, :], ps[0:HD_B, b:b + 2, :].rearrange("p b (h n) -> p (b h) n", h=4)).then_inc(S["tb_ev"], 1)

    @block.vector
    def _(dve):
        v = nc.vector
        v.memset(k_t[:, :, :, :], 0.0).then_inc(S["zero"], 1)
        for n, (c, t) in enumerate(units):
            if n % 2 == 1:
                dve.wait_ge(S["in_ps"], n + 1)
                v.tensor_copy(proj[:, t, c * BANK:c * BANK + widths[c]], ps[:, n % 8, 0:widths[c]]).then_inc(S["in_d"], 1)
        dve.wait_ge(S["in_a"], 5)
        dve.wait_ge(S["in_d"], 4)
        dve.wait_ge(s.loads, s.loaded)
        for t in range(T):
            link(s, "dve", dve, v.tensor_tensor(sq[:, 0:640], proj[:, t, 0:640], proj[:, t, 0:640], ALU.mult))
            link(s, "dve", dve, v.tensor_tensor(sq[:, 640:1024], proj[:, t, 768:1152], proj[:, t, 768:1152], ALU.mult))
            link(s, "dve", dve, v.tensor_reduce(ss[:, t, 0:10], sq[:, 0:640].rearrange("p (h d) -> p h d", d=64), AX.X, ALU.add))
            link(s, "dve", dve, v.tensor_reduce(ss[:, t, 10:11], sq[:, 640:896], AX.X, ALU.add))
            link(s, "dve", dve, v.tensor_reduce(ss[:, t, 11:12], sq[:, 896:1024], AX.X, ALU.add))
        x3 = x[:, :].rearrange("p (t h) -> p t h", t=T)
        link(s, "dve", dve, v.tensor_scalar(x3[:, :, 0:10], ss[:, :, 0:10], 1.0 / 64, EPS, ALU.mult, ALU.add))
        link(s, "dve", dve, v.tensor_scalar(x3[:, :, 10:11], ss[:, :, 10:11], 1.0 / 256, EPS, ALU.mult, ALU.add))
        v.tensor_scalar(x3[:, :, 11:12], ss[:, :, 11:12], 1.0 / P, EPS, ALU.mult, ALU.add).then_inc(S["norm_x"], 1)
        rsqrt_dve(s, dve, x[:, :], r[:, :], tmp[:, :], S["norm_r"], 1)
        r3 = r[:, :].rearrange("p (t h) -> p t h", t=T)
        for t in range(T):
            link(s, "dve", dve, v.scalar_tensor_tensor(out=proj[:, t, 768:1024], in0=proj[:, t, 768:1024], scalar=r3[:, t, 10:11],
                                                       in1=qa_gain[:, :], op0=ALU.mult, op1=ALU.mult))
            ins = v.scalar_tensor_tensor(out=proj[:, t, 1024:1152], in0=proj[:, t, 1024:1152], scalar=r3[:, t, 11:12],
                                         in1=kva_gain[:, :], op0=ALU.mult, op1=ALU.mult)
        ins.then_inc(S["lat_ready"], 1)
        for t in range(T):
            q_in = proj[:, t, 0:512].rearrange("p (v j d) -> p j v d", v=2, j=4)
            q_out = heads[:, t, 0:8, :].rearrange("p (j v) d -> p j v d", j=4)
            for kv in range(2):
                rr = r3[:, t, 4 * kv:4 * kv + 4].unsqueeze(2).broadcast_to([P, 4, 64])
                link(s, "dve", dve, v.tensor_tensor(q_out[:, :, kv, :], q_in[:, :, kv, :], rr, ALU.mult))
            rk = r3[:, t, 8:10].unsqueeze(2).broadcast_to([P, 2, 64])
            link(s, "dve", dve, v.tensor_tensor(heads[:, t, 8:10, :], proj[:, t, 512:640].rearrange("p (v d) -> p v d", v=2), rk, ALU.mult))
            link(s, "dve", dve, v.tensor_copy(v_a[:, t, :], proj[:, t, 640:768]))
            link(s, "dve", dve, v.tensor_tensor(heads[:, t, 0:8, :], heads[:, t, 0:8, :], q_gain[:, :].unsqueeze(1).broadcast_to([P, 8, 64]), ALU.mult))
            ins = v.tensor_tensor(heads[:, t, 8:10, :], heads[:, t, 8:10, :], k_gain[:, :].unsqueeze(1).broadcast_to([P, 2, 64]), ALU.mult)
            if t == 0:
                ins.then_inc(S["heads_ready"], 1)
            else:
                link(s, "dve", dve, ins)
                ins = rope(s, dve, heads[:, t], "a", t - 1, 10, rot_pool(sq, 640))
                if t == T - 1:
                    ins.then_inc(S["heads_ready"], 1)
                else:
                    link(s, "dve", dve, ins)
        dve.wait_ge(S["tl_ps"], 1)
        for n in range(NTB):
            b = 4 + 2 * (n % 2)
            dve.wait_ge(S["up_ps"], n + 1)
            if n < T:
                ins = v.tensor_copy(qkb[:, n, :, :].rearrange("p (b h) d -> p b (h d)", b=2), ps[:, b:b + 2, 0:384])
            else:
                kv = ps[:, b:b + 2, :].rearrange("p b (h d) -> p (b h) d", h=4)
                link(s, "dve", dve, v.tensor_copy(v_b[:, n - T, :, :], kv[:, :, 64:128]))
                rope_src = (proj[:, n - T, 1152:1184] if n < NTB - 1 else cache_r[:, :]).unsqueeze(1).broadcast_to([P, 8, ROPE])
                link(s, "dve", dve, v.tensor_copy(qkb[:, n, :, 64:96], rope_src))
                ins = v.tensor_copy(qkb[:, n, :, 0:64], kv[:, :, 0:64])
            ins.then_inc(S["up_d"], 1)
            dve.wait_ge(S["up_d"], n + 1)
            sqn = sq[:, 0:768]
            flat = qkb[:, n, :, :].rearrange("p h d -> p (h d)")
            link(s, "dve", dve, v.tensor_tensor(sqn, flat, flat, ALU.mult))
            link(s, "dve", dve, v.tensor_reduce(ssb[:, 8 * n:8 * n + 8], sqn.rearrange("p (h d) -> p h d", h=8), AX.X, ALU.add))
        v.tensor_scalar(xb[:, :], ssb[:, :], 1.0 / HD_B, EPS, ALU.mult, ALU.add).then_inc(S["b_x"], 1)
        rsqrt_dve(s, dve, xb[:, :], rb[:, :], tmpb[:, :], S["b_r"], 1)
        for n in range(NTB):
            rr = rb[:, 8 * n:8 * n + 8].unsqueeze(2).broadcast_to([P, 8, HD_B])
            g = b_gain[:, 0 if n < T else 1, :].unsqueeze(1).broadcast_to([P, 8, HD_B])
            link(s, "dve", dve, v.tensor_tensor(qkb[:, n, :, :], qkb[:, n, :, :], rr, ALU.mult))
            ins = v.tensor_tensor(qkb[:, n, :, :], qkb[:, n, :, :], g, ALU.mult)
            if n in (1, 2, 4, 5):
                link(s, "dve", dve, ins)
                ins = rope(s, dve, qkb[:, n, :, 64:96], "b", (n % 3) - 1, 8, rot_pool(sq, 256))
            if n < NTB - 1:
                link(s, "dve", dve, ins)
        ins.then_inc(S["b_ready"], 1)


def rot_pool(sq, n):
    return sq[:, 1024:1024 + n]


def rope(s, dve, x, which, tile, nh, scratch):
    v = s.nc.vector
    rot = HD_A if which == "a" else ROPE
    qtr = rot // 4
    cos = s.cid("cos_" + which)[:, tile * rot:(tile + 1) * rot].unsqueeze(1).broadcast_to([P, nh, rot])
    sin = s.cid("sin_" + which)[:, tile * rot:(tile + 1) * rot]
    tmp = scratch.rearrange("p (h d) -> p h d", h=nh)
    for blk in range(2):
        for u in range(2):
            a, b = blk * 2 * qtr + u * qtr, blk * 2 * qtr + (1 - u) * qtr
            link(s, "dve", dve, v.tensor_tensor(tmp[:, :, a:a + qtr], x[:, :, b:b + qtr],
                                                sin[:, a:a + qtr].unsqueeze(1).broadcast_to([P, nh, qtr]), ALU.mult))
    link(s, "dve", dve, v.tensor_tensor(x, x, cos, ALU.mult))
    return v.tensor_tensor(x, x, tmp, ALU.add)


def att_scores(s, st, qk_t, k_t, v_a, qkb_t, v_b, sink):
    nc, ps = s.nc, s.ps
    sb = stage_buffers(s, st, "sc_")
    prob = sb("prob", [P, 2, 4, 3 * P])
    prob_t = sb("prob_t", [P, 2, 12, P])
    o = sb("o", [P, T, D])
    mx, nb, den, rec, e_sink = (sb(n, [P, 2, 4]) for n in ("mx", "nb", "den", "rec", "e_sink"))
    names = ("s_ps", "nb", "exp", "den", "t_ps", "t_ev", "o_ps", "o_ev", "ot_ps", "ot_ev")
    S = {n: s.sem("sc_" + n) for n in names}
    mod = NextModulation(s, sb)
    score = ps[:, 0:3, :].rearrange("p b n -> p (b n)")
    units = [(kind, t, g) for t in range(T) for kind in "AB" for g in range(2)]
    NU = len(units)
    block = st.enter_context(nc.Block())

    def keys(t):
        return 1 if t == 0 else 3

    @block.sync
    def _(sp):
        loads = mod.loads()
        for dst, src in loads:
            sp.dma_start(dst, src).then_inc(s.loads, 16)
        s.loaded += 16 * len(loads)
        ring_loads(s, sp, s.at["att_out", 0] + 2)

    @block.tensor
    def _(pe):
        def scores(n):
            kind, t, g = units[n]
            nk = keys(t)
            if n >= 1:
                pe.wait_ge(S["exp"], 4 * n)
            for j in range(4):
                for c in range(nk):
                    kt = 0 if nk == 1 else 1 + c
                    if kind == "A":
                        lhs, rhs = qk_t[:, t, j, :], k_t[:, g, kt, :]
                    else:
                        lhs, rhs = qkb_t[:, 4 * g + j, t, :], qkb_t[:, 4 * g + j, 3 + kt, :]
                    masked = kind == "A" and (t, c) in ((1, 1), (2, 0))
                    i = j * nk + c
                    dst = ps[:, i // 4, (i % 4) * P:(i % 4 + 1) * P]
                    mm = pe.matmul(dst, lhs, rhs, start=True, stop=not masked)
                    if masked:
                        mm = pe.matmul(dst, s.ident, s.cid("mask_high") if t == 2 else s.cid("mask_low"), start=False, stop=True)
            mm.then_inc(S["s_ps"], 1)

        def turn(n):
            nk = keys(units[n][1])
            pe.wait_ge(S["exp"], 4 * n + 4)
            if n >= 1:
                pe.wait_ge(S["t_ev"], n)
            for j in range(4):
                for c in range(nk):
                    i = j * nk + c
                    mm = pe.transpose(ps[:, 3 + i // 4, (i % 4) * P:(i % 4 + 1) * P], prob[:, n % 2, j, c * P:(c + 1) * P], s.ident)
            mm.then_inc(S["t_ps"], 1)

        def weigh(n):
            kind, t, g = units[n]
            nk = keys(t)
            pe.wait_ge(S["t_ev"], n + 1)
            if n >= 1:
                pe.wait_ge(S["o_ev"], n)
            for j in range(4):
                for c in range(nk):
                    kt = 0 if nk == 1 else 1 + c
                    rhs = v_a[:, kt, 64 * g:64 * g + 64] if kind == "A" else v_b[:, kt, 4 * g + j, :]
                    mm = narrow_matmul(pe, ps[:, 6, j * 64:(j + 1) * 64], prob_t[:, n % 2, j * nk + c, :], rhs,
                                       start=(c == 0), stop=(c == nk - 1))
            mm.then_inc(S["o_ps"], 1)

        scores(0)
        for n in range(NU):
            turn(n)
            if n + 1 < NU:
                scores(n + 1)
            mod.products(pe, n)
            weigh(n)
            mod.sum(pe, n)
        mod.turn(pe)
        for t in range(T):
            pe.wait_ge(S["o_ev"], NU)
            b = 2 * t
            for k in range(KD):
                mm = pe.transpose(ps[:, b + k // 4, (k % 4) * P:(k % 4 + 1) * P], o[:, t, k::KD], s.ident)
            mm.then_inc(S["ot_ps"], 1)

    @block.scalar
    def _(act):
        for n in range(NU):
            kind, t, g = units[n]
            nk = keys(t)
            scale = HD_A ** -0.5 if kind == "A" else HD_B ** -0.5
            act.wait_ge(S["nb"], n + 1)
            if n >= 2:
                act.wait_ge(S["t_ps"], n - 1)
            for j in range(4):
                nc.scalar.activation(prob[:, n % 2, j, 0:nk * P], score[:, j * nk * P:(j + 1) * nk * P], ACT.Exp, scale=scale,
                                     bias=nb[:, n % 2, j:j + 1], accum_out=den[:, n % 2, j:j + 1]).then_inc(S["exp"], 1)
            if kind == "A":
                for j in range(4):
                    nc.scalar.activation(e_sink[:, n % 2, j:j + 1], sink[:, 4 * g + j:4 * g + j + 1], ACT.Exp,
                                         bias=nb[:, n % 2, j:j + 1]).then_inc(S["den"], 1)
            act.wait_ge(S["t_ps"], n + 1)
            nc.scalar.copy(prob_t[:, n % 2, 0:4 * nk, :].rearrange("p i n -> p (i n)"),
                           ps[:, 3:3 + nk, :].rearrange("p b n -> p (b n)")).then_inc(S["t_ev"], 1)

    @block.vector
    def _(dve):
        v = nc.vector

        def bias(n):
            kind, t, g = units[n]
            nk, b = keys(t), n % 2
            scale = HD_A ** -0.5 if kind == "A" else HD_B ** -0.5
            dve.wait_ge(S["s_ps"], n + 1)
            link(s, "dve", dve, v.tensor_reduce(mx[:, b, :], score[:, 0:4 * nk * P].rearrange("p (j n) -> p j n", j=4), AX.X, ALU.max))
            if kind == "A":
                link(s, "dve", dve, v.scalar_tensor_tensor(out=mx[:, b, :], in0=mx[:, b, :], scalar=scale,
                                                           in1=sink[:, 4 * g:4 * g + 4], op0=ALU.mult, op1=ALU.max))
                v.tensor_scalar(nb[:, b, :], mx[:, b, :], -1.0, None, ALU.mult).then_inc(S["nb"], 1)
            else:
                v.tensor_scalar(nb[:, b, :], mx[:, b, :], -scale, None, ALU.mult).then_inc(S["nb"], 1)

        sinks = 0
        dve.wait_ge(s.loads, s.loaded)
        bias(0)
        for n in range(NU):
            kind, t, g = units[n]
            b = n % 2
            dve.wait_ge(S["exp"], 4 * n + 4)
            if kind == "A":
                sinks += 4
                dve.wait_ge(S["den"], sinks)
                link(s, "dve", dve, v.tensor_tensor(den[:, b, :], den[:, b, :], e_sink[:, b, :], ALU.add))
            link(s, "dve", dve, v.reciprocal(rec[:, b, :], den[:, b, :]))
            if n + 1 < NU:
                bias(n + 1)
            mod.take_part(dve, n)
            dve.wait_ge(S["o_ps"], n + 1)
            c0 = (0 if kind == "A" else 512) + 256 * g
            v.tensor_tensor(o[:, t, c0:c0 + 256].rearrange("p (h d) -> p h d", h=4),
                            ps[:, 6, 0:256].rearrange("p (h d) -> p h d", h=4),
                            rec[:, b, :].unsqueeze(2).broadcast_to([P, 4, 64]), ALU.mult).then_inc(S["o_ev"], 1)
            mod.add_bias(dve, n)
        mod.take_turned(dve)
        for t in range(T):
            dve.wait_ge(S["ot_ps"], t + 1)
            v.tensor_copy(s.hT[:, :, t * P:(t + 1) * P], ps[:, 2 * t:2 * t + 2, :].rearrange("p b (k n) -> p (b k) n", k=4)).then_inc(S["ot_ev"], 1)

    st.close()
    with ExitStack() as st3:
        project_out(s, 0, st3, "ao_", s.hT, KD, [("att_out", 0), ("att_out", 1)], MIX)


def project_out(s, l, st, pre, src, nk, keys, m):
    nc, ps = s.nc, s.ps
    sb = stage_buffers(s, st, pre)
    gate = sb("gate", [P, 2, D])
    tmp = sb("tmp", [P, 2, BANK])
    rows = slice(32 * l, 32 * l + 2)
    g_ps, g_ev, o_ps, o_ev = (s.sem(pre + n) for n in ("g_ps", "g_ev", "o_ps", "o_ev"))
    per = nk // KD
    block = st.enter_context(nc.Block())
    last = s.at[keys[-1]]

    @block.sync
    def _(sp):
        ring_loads(s, sp, last + 1 + SLOT_RING)

    @block.tensor
    def _(pe):
        for g in range(2):
            for h in range(2):
                mm = pe.matmul(ps[:, 2 * g + h, :], s.cid("pick")[rows, g * P:(g + 1) * P], s.gates[rows, m, h * BANK:(h + 1) * BANK],
                               start=True, stop=True)
        mm.then_inc(g_ps, 1)
        for h in range(2):
            for kh in range(per):
                ring_wait(s, pe, s.at[keys[h * per + kh]])
            if h:
                pe.wait_ge(o_ev, 3)
            for t in range(T):
                for k in range(nk):
                    n = s.at[keys[h * per + k // KD]]
                    mm = pe.matmul(ps[:, 4 + t, :], src[:, k, t * P:(t + 1) * P], s.ring[:, n % SLOT_RING, k % KD, :],
                                   start=(k == 0), stop=(k == nk - 1))
                mm.then_inc(o_ps, 1)
            pe.wait_ge(o_ps, 3 * (h + 1))
            pe.sem_inc(s.ring_free, per)

    @block.vector
    def _(dve):
        v = nc.vector
        dve.wait_ge(g_ps, 1)
        link(s, "dve", dve, v.tensor_copy(gate[:, :, :].rearrange("p g n -> p (g n)"), ps[:, 0:4, :].rearrange("p b n -> p (b n)")))
        for h in range(2):
            for t in range(T):
                n = 3 * h + t
                dve.wait_ge(o_ps, n + 1)
                v.tensor_tensor(tmp[:, n % 2, :], ps[:, 4 + t, :], gate[:, min(t, 1), h * BANK:(h + 1) * BANK], ALU.mult).then_inc(o_ev, 1)
                dve.wait_ge(o_ev, n + 1)
                ys = s.y[:, t, h * BANK:(h + 1) * BANK]
                v.tensor_tensor(ys, ys, tmp[:, n % 2, :], ALU.add)


def ssd(s, st):
    sb = stage_buffers(s, st, "ssd_")
    xs = sb("xs", [P, T, D_INNER])
    with ExitStack() as st2:
        sb2 = stage_buffers(s, st2, "ssd_")
        g = Shared()
        g.b_t, g.c_t = sb2("b_t", [P, G_C, NTOK]), sb2("c_t", [P, G_C, NTOK])
        g.b_n = sb2("b_n", [P, T, G_C, N_C])
        g.state = sb2("state", [P, 2, D_INNER])
        g.dt, g.dta = sb2("dt", [P, T, 64]), sb2("dta", [P, T, 64])
        g.nacs, g.eacs, g.etot, g.toend = (sb2(n, [P, T, 64]) for n in ("nacs", "eacs", "etot", "toend"))
        with ExitStack() as st3:
            ssd_conv(s, st3, xs, g)
        with ExitStack() as st3:
            ssd_scan(s, st3, xs, g)
    y_t = sb("y_t", [P, 2 * KD, NTOK])
    with ExitStack() as st2:
        ssd_gate(s, st2, xs, y_t)
    with ExitStack() as st2:
        project_out(s, 1, st2, "so_", y_t, 2 * KD, [("ssd_out", (j, kh)) for j in range(2) for kh in range(2)], MIX)


def ssd_conv(s, st, xs, g):
    nc, w, ps = s.nc, s.w, s.ps
    sb = stage_buffers(s, st, "cv_")
    taps_in, taps = sb("taps_in", [32, 6, P]), sb("taps", [P, 6, 32])
    PAD = NTOK + 8
    xp, cv, x_t = sb("xp", [P, 2, PAD]), sb("cv", [P, 2, PAD - 4]), sb("x_t", [P, 2, NTOK])
    dtb, alog, ea = sb("dtb", [P, 64]), sb("alog", [P, 64]), sb("ea", [P, 64])
    v1, v2, v3, v4 = (sb(n, [P, T * 64]) for n in ("v1", "v2", "v3", "v4"))
    names = ("turn_ps", "turn_ev", "mm_ps", "xp", "cv", "silu", "tr_ps", "tr_ev", "dt_ps", "dt_x", "dt_e", "dta", "acs_ps",
             "acs_x", "acs_e", "zero")
    S = {n: s.sem("cv_" + n) for n in names}
    s0 = xs[:, :, :].rearrange("p t n -> p (t n)")[:, 0:4096].rearrange("p (d c n) -> p d c n", d=2, c=16)
    u0, dt0 = s.at["ssd_xbc", 0], s.at["ssd_dt", 0]
    NT = 32
    block = st.enter_context(nc.Block())

    def turned(n):
        return n < 24

    @block.sync
    def _(sp):
        loads = [(taps_in[:, 0:5, :], w["ssd_conv_w"][0].rearrange("k (c p) -> c k p", p=P)),
                 (taps_in[:, 5, :], w["ssd_conv_b"][0].rearrange("(c p) -> c p", p=P)),
                 (dtb[:, 0:32], w["ssd_dtb_fwd"][0].partition_broadcast(P)),
                 (dtb[:, 32:64], w["ssd_dtb_bwd"][0].partition_broadcast(P)),
                 (alog[:, 0:32], w["ssd_alog_fwd"][0].partition_broadcast(P)),
                 (alog[:, 32:64], w["ssd_alog_bwd"][0].partition_broadcast(P)),
                 (s0[:, 0], w["state_c_fwd"][0, 0].rearrange("h p n -> (h p) n").rearrange("(c q) n -> q c n", q=P)),
                 (s0[:, 1], w["state_c_bwd"][0, 0].rearrange("h p n -> (h p) n").rearrange("(c q) n -> q c n", q=P))]
        for dst, src in loads:
            sp.dma_start(dst, src).then_inc(s.loads, 16)
        s.loaded += 16 * len(loads)
        ring_loads(s, sp, dt0 + 1 + SLOT_RING)

    @block.tensor
    def _(pe):
        pe.wait_ge(s.loads, s.loaded)
        for k in range(6):
            mm = pe.transpose(ps[:, 4, k * 32:(k + 1) * 32], taps_in[:, k, :], s.ident[0:32, 0:32])
        mm.then_inc(S["turn_ps"], 1)
        for q in range(4):
            if q >= 2:
                pe.wait_ge(S["turn_ev"], q)
            for c in range(8):
                mm = pe.transpose(ps[:, 2 * (q % 2) + c // 4, (c % 4) * P:(c % 4 + 1) * P], s0[:, q // 2, 8 * (q % 2) + c, :], s.ident)
            mm.then_inc(S["turn_ps"], 1)

        def turn(n):
            pe.wait_ge(S["silu"], 2 * (n + 1))
            if n >= 2:
                pe.wait_ge(S["tr_ev"], n - 1)
            src = x_t[:, n % 2, :] if n < 16 else g.b_t[:, n - 16, :]
            for t in range(T):
                mm = pe.transpose(ps[:, 2 + n % 2, t * P:(t + 1) * P], src[:, t * P:(t + 1) * P], s.ident)
            mm.then_inc(S["tr_ps"], 1)

        pe.wait_ge(S["turn_ev"], 5)
        for n in range(NT):
            c, i = divmod(n, 4)
            if i == 0:
                ring_wait(s, pe, u0 + c)
            if n >= 2:
                pe.wait_ge(S["xp"], 2 * (n - 1))
            for k in range(KD):
                mm = pe.matmul(ps[:, n % 2, 0:NTOK], s.ring[:, (u0 + c) % SLOT_RING, k, i * P:(i + 1) * P], s.hT[:, k, :],
                               start=(k == 0), stop=(k == KD - 1))
            mm.then_inc(S["mm_ps"], 1)
            if n >= 2 and turned(n - 2):
                turn(n - 2)
            if i == 0 and c >= 1:
                pe.wait_ge(S["mm_ps"], n)
                pe.sem_inc(s.ring_free, 1)
        pe.wait_ge(S["mm_ps"], NT)
        pe.sem_inc(s.ring_free, 1)
        ring_wait(s, pe, dt0)
        for t in range(T):
            for k in range(KD):
                mm = narrow_matmul(pe, ps[:, 4, t * 64:(t + 1) * 64], s.hT[:, k, t * P:(t + 1) * P], s.ring[:, dt0 % SLOT_RING, k, 0:64],
                                   start=(k == 0), stop=(k == KD - 1))
        mm.then_inc(S["dt_ps"], 1)
        pe.wait_ge(S["dt_ps"], 1)
        pe.sem_inc(s.ring_free, 1)
        pe.wait_ge(S["dta"], 1)
        for t in range(T):
            for d in range(2):
                narrow_matmul(pe, ps[:, 5, t * 64 + 32 * d:t * 64 + 32 * d + 32], s.cid("from_" if d else "upto"),
                          g.dta[:, t, 32 * d:32 * d + 32], start=True, stop=True)
            mm = narrow_matmul(pe, ps[:, 6, t * 64:(t + 1) * 64], s.cid("ones"), g.dta[:, t, :], start=True, stop=True)
        mm.then_inc(S["acs_ps"], 1)

    @block.scalar
    def _(act):
        a = nc.scalar

        def silu(n):
            act.wait_ge(S["cv"], n + 1)
            if n < 16 and n >= 2:
                act.wait_ge(S["tr_ps"], n - 1)
            dst = x_t[:, n % 2, :] if n < 16 else (g.b_t[:, n - 16, :] if n < 24 else g.c_t[:, n - 24, :])
            bias = taps[:, 5, n:n + 1]
            a.activation(dst[:, 0:P], cv[:, n % 2, 0:P], ACT.Silu, bias=bias).then_inc(S["silu"], 1)
            a.activation(dst[:, P:NTOK], cv[:, n % 2, P + 4:NTOK + 4], ACT.Silu, bias=bias).then_inc(S["silu"], 1)

        def turned_out(n):
            act.wait_ge(S["tr_ps"], n + 1)
            dst = xs[:, :, n * P:(n + 1) * P] if n < 16 else g.b_n[:, :, n - 16, :]
            a.copy(dst, ps[:, 2 + n % 2, 0:NTOK].rearrange("p (t n) -> p t n", t=T)).then_inc(S["tr_ev"], 1)

        act.wait_ge(s.loads, s.loaded)
        act.wait_ge(S["turn_ps"], 1)
        a.copy(taps[:, :, :].rearrange("p k c -> p (k c)"), ps[:, 4, 0:192]).then_inc(S["turn_ev"], 1)
        for q in range(4):
            act.wait_ge(S["turn_ps"], q + 2)
            a.copy(g.state[:, q // 2, (q % 2) * D:(q % 2 + 1) * D], ps[:, 2 * (q % 2):2 * (q % 2) + 2, :].rearrange("p b n -> p (b n)")).then_inc(S["turn_ev"], 1)
        act.wait_ge(S["zero"], 1)
        for n in range(NT + 3):
            if n < NT:
                act.wait_ge(S["mm_ps"], n + 1)
                if n >= 2:
                    act.wait_ge(S["cv"], n - 1)
                a.copy(xp[:, n % 2, 2:P + 2], ps[:, n % 2, 0:P]).then_inc(S["xp"], 1)
                a.copy(xp[:, n % 2, P + 6:NTOK + 6], ps[:, n % 2, P:NTOK]).then_inc(S["xp"], 1)
            if 1 <= n <= NT:
                silu(n - 1)
            if n >= 3 and turned(n - 3):
                turned_out(n - 3)
        a.activation(ea[:, :], alog[:, :], ACT.Exp).then_inc(S["dt_e"], 1)
        act.wait_ge(S["dt_x"], 1)
        a.activation(v2[:, :], v2[:, :], ACT.Exp, scale=-1.0).then_inc(S["dt_e"], 1)
        act.wait_ge(S["acs_x"], 1)
        a.activation(flat3(g.toend), flat3(g.toend), ACT.Exp).then_inc(S["acs_e"], 1)
        a.activation(flat3(g.eacs), flat3(g.nacs), ACT.Exp, scale=-1.0).then_inc(S["acs_e"], 1)
        a.activation(flat3(g.etot), flat3(g.etot), ACT.Exp).then_inc(S["acs_e"], 1)

    @block.vector
    def _(dve):
        v = nc.vector
        v.memset(xp[:, :, :], 0.0).then_inc(S["zero"], 1)
        dve.wait_ge(S["turn_ev"], 1)
        for n in range(NT):
            dve.wait_ge(S["xp"], 2 * (n + 1))
            if n >= 2:
                dve.wait_ge(S["silu"], 2 * (n - 1))
            o = cv[:, n % 2, :]
            link(s, "dve", dve, v.tensor_scalar(o, xp[:, n % 2, 0:PAD - 4], taps[:, 0, n:n + 1], None, ALU.mult))
            for k in range(1, 5):
                ins = v.scalar_tensor_tensor(out=o, in0=xp[:, n % 2, k:k + PAD - 4], scalar=taps[:, k, n:n + 1], in1=o,
                                             op0=ALU.mult, op1=ALU.add)
                if k < 4:
                    link(s, "dve", dve, ins)
            ins.then_inc(S["cv"], 1)
        dve.wait_ge(s.loads, s.loaded)
        dve.wait_ge(S["dt_ps"], 1)
        link(s, "dve", dve, v.tensor_tensor(v1[:, :].rearrange("p (t h) -> p t h", t=T), ps[:, 4, 0:T * 64].rearrange("p (t h) -> p t h", t=T),
                                            dtb[:, :].unsqueeze(1).broadcast_to([P, T, 64]), ALU.add))
        v.scalar_tensor_tensor(out=v2[:, :], in0=v1[:, :], scalar=-1.0, in1=v1[:, :], op0=ALU.mult, op1=ALU.max).then_inc(S["dt_x"], 1)
        dve.wait_ge(S["dt_e"], 2)
        link(s, "dve", dve, v.tensor_scalar(v3[:, :], v2[:, :], 2.0, None, ALU.add))
        link(s, "dve", dve, v.reciprocal(v3[:, :], v3[:, :]))
        link(s, "dve", dve, v.tensor_tensor(v2[:, :], v2[:, :], v3[:, :], ALU.mult))
        link(s, "dve", dve, v.tensor_tensor(v3[:, :], v2[:, :], v2[:, :], ALU.mult))
        link(s, "dve", dve, v.tensor_scalar(v4[:, :], v3[:, :], 1.0 / 13, None, ALU.mult))
        for odd in (11, 9, 7, 5, 3):
            link(s, "dve", dve, v.scalar_tensor_tensor(out=v4[:, :], in0=v4[:, :], scalar=1.0 / odd, in1=v3[:, :], op0=ALU.add, op1=ALU.mult))
        link(s, "dve", dve, v.scalar_tensor_tensor(out=v4[:, :], in0=v4[:, :], scalar=1.0, in1=v2[:, :], op0=ALU.add, op1=ALU.mult))
        link(s, "dve", dve, v.tensor_scalar(v4[:, :], v4[:, :], 2.0, None, ALU.mult))
        link(s, "dve", dve, v.scalar_tensor_tensor(out=flat3(g.dt), in0=v1[:, :], scalar=0.0, in1=v4[:, :], op0=ALU.max, op1=ALU.add))
        v.scalar_tensor_tensor(out=g.dta[:, :, :], in0=g.dt[:, :, :], scalar=-1.0, in1=ea[:, :].unsqueeze(1).broadcast_to([P, T, 64]),
                               op0=ALU.mult, op1=ALU.mult).then_inc(S["dta"], 1)
        dve.wait_ge(S["acs_ps"], 1)
        link(s, "dve", dve, v.tensor_scalar(flat3(g.nacs), ps[:, 5, 0:T * 64], -1.0, None, ALU.mult))
        link(s, "dve", dve, v.tensor_tensor(flat3(g.toend), flat3(g.nacs), ps[:, 6, 0:T * 64], ALU.add))
        v.tensor_copy(flat3(g.etot), ps[:, 6, 0:T * 64]).then_inc(S["acs_x"], 1)
        dve.wait_ge(S["acs_e"], 3)
        link(s, "dve", dve, v.tensor_tensor(flat3(g.toend), flat3(g.toend), flat3(g.dt), ALU.mult))


def flat3(t):
    return t[:, :, :].rearrange("p a b -> p (a b)")


def ssd_scan(s, st, xs, g):
    nc, w, ps, out = s.nc, s.w, s.ps, s.out
    sb = stage_buffers(s, st, "scan_")
    W = R_C * P_C
    e = sb("e", [P, 2, 2, R_C, P])
    cb = sb("cb", [P, T, P])
    xdt = sb("xdt", [P, T, 2, R_C, P_C])
    xe = sb("xe", [P, 4, R_C, P_C])
    inter = sb("inter", [P, 2, W])
    stage = sb("stage", [P, BANK])
    skip = sb("skip", [P, H_C])
    ident_h = sb("ident_h", [P, P], BF16)
    mask_h = sb("mask_h", [P, 2, P], BF16)
    names = ("cb_ps", "cb_ev", "a_ps", "exp", "m", "pool", "y_ps", "y_ev", "i_ps", "i_ev", "sp_ps", "sp_ev", "s1_ps", "upd", "init", "stage")
    S = {n: s.sem("scan_" + n) for n in names}
    EX = ((0, 0), (0, 1), (1, 0), (2, 1))
    block = st.enter_context(nc.Block())

    @block.sync
    def _(sp):
        sp.dma_start(skip[:, :], w["ssd_d"][0].partition_broadcast(P)).then_inc(s.loads, 16)
        s.loaded += 16
        for q in range(G_C):
            sp.wait_ge(S["sp_ev"], q + 1)
            for d in range(2):
                dst = out["new_state_bwd" if d else "new_state_fwd"][0, 0, 4 * q:4 * q + 4].rearrange("(a b) p n -> (b p) a n", a=2)
                sp.dma_start(dst, stage[:, d * 256:(d + 1) * 256].rearrange("p (a n) -> p a n", a=2)).then_inc(S["stage"], 16)
        sp.wait_ge(S["stage"], 32 * G_C)

    @block.gpsimd
    def _(pool):
        pool.wait_ge(s.loads, s.loaded)

        def scaled(dst, t, src, col):
            return nc.gpsimd.tensor_tensor(dst, xs[:, t, q * W:(q + 1) * W].rearrange("p (h d) -> p h d", h=R_C),
                                           src[:, col:col + R_C].unsqueeze(2).broadcast_to([P, R_C, P_C]), ALU.mult)
        for q in range(G_C):
            if q:
                pool.wait_ge(S["y_ps"], 3 * q)
                pool.wait_ge(S["y_ev"], 3 * q)
                pool.wait_ge(S["s1_ps"], q)
            for t in range(T):
                for d in range(2):
                    scaled(xdt[:, t, d], t, g.dt[:, t, :], 32 * d + 4 * q)
                for i, (tt, d) in enumerate(EX):
                    if tt == t:
                        scaled(xe[:, i], t, g.toend[:, t, :], 32 * d + 4 * q)
                scaled(xs[:, t, q * W:(q + 1) * W].rearrange("p (h d) -> p h d", h=R_C), t, skip, 4 * q).then_inc(S["pool"], 1)

    @block.tensor
    def _(pe):
        pe.wait_ge(S["init"], 3)

        def decay(q, t):
            u = 3 * q + t
            if u >= 2:
                pe.wait_ge(S["exp"], 8 * (u - 1))
            for d in range(2):
                b = 1 + 2 * (u % 2) + d
                for r in range(R_C):
                    c = 32 * d + 4 * q + r
                    pe.matmul(ps[:, b, r * P:(r + 1) * P], g.dta[:, t, c:c + 1].broadcast_to([P, P]),
                              s.cid("from_" if d else "upto"), start=(r == 0), stop=False, skip_group_check=True)
                mm = pe.matmul(ps[:, b, :].rearrange("p (r i) -> p r i", r=R_C), ident_h[:, :],
                               mask_h[:, d, :].unsqueeze(1).broadcast_to([P, R_C, P]), start=False, stop=True, skip_group_check=True)
            mm.then_inc(S["a_ps"], 1)

        def give(q, t):
            u = 3 * q + t
            pe.wait_ge(S["m"], u + 1)
            pe.wait_ge(S["pool"], u + 1)
            if u:
                pe.wait_ge(S["y_ev"], u)
            for r in range(R_C):
                for d in range(2):
                    mm = narrow_matmul(pe, ps[:, 5, r * P_C:(r + 1) * P_C], e[:, u % 2, d, r, :], xdt[:, t, d, r, :],
                                       start=(d == 0), stop=(d == 1))
            mm.then_inc(S["y_ps"], 1)

        def from_state(q, rnd):
            n = 2 * q + rnd
            if n:
                pe.wait_ge(S["i_ev"], n)
            if rnd:
                pe.wait_ge(S["upd"], 2 * (q + 1))
            for d in range(2):
                t = (1, 2)[d] if rnd == 0 else (2, 1)[d]
                mm = pe.matmul(ps[:, 7, d * W:(d + 1) * W], g.c_t[:, q, t * P:(t + 1) * P], g.state[:, d, q * W:(q + 1) * W],
                               start=True, stop=True)
            mm.then_inc(S["i_ps"], 1)

        for q in range(G_C):
            if q:
                pe.wait_ge(S["cb_ev"], q)
            for t in range(T):
                mm = pe.matmul(ps[:, 0, t * P:(t + 1) * P], g.b_t[:, q, t * P:(t + 1) * P], g.c_t[:, q, t * P:(t + 1) * P],
                               start=True, stop=True)
            mm.then_inc(S["cb_ps"], 1)
            decay(q, 0)
            decay(q, 1)
            from_state(q, 0)
            pe.wait_ge(S["pool"], 3 * q + 1)
            if q:
                pe.wait_ge(S["upd"], 2 * q)
            for d in range(2):
                for a in range(2):
                    mm = pe.matmul(ps[:, 6, (2 * d + a) * P:(2 * d + a + 1) * P], xe[:, d, 2 * a:2 * a + 2, :].rearrange("p h d -> p (h d)"),
                                   g.b_n[:, 0, q, :], start=True, stop=True)
            mm.then_inc(S["sp_ps"], 1)
            give(q, 0)
            decay(q, 2)
            pe.wait_ge(S["pool"], 3 * q + 3)
            pe.wait_ge(S["sp_ev"], q + 1)
            for d in range(2):
                mm = pe.matmul(ps[:, 6, d * W:(d + 1) * W], g.b_n[:, 1 + d, q, :], xe[:, 2 + d, :, :].rearrange("p h d -> p (h d)"),
                               start=True, stop=True)
            mm.then_inc(S["s1_ps"], 1)
            give(q, 1)
            from_state(q, 1)
            give(q, 2)

    @block.scalar
    def _(act):
        a = nc.scalar
        for u in range(3 * G_C):
            q, t = divmod(u, T)
            act.wait_ge(S["a_ps"], u + 1)
            if u >= 2:
                act.wait_ge(S["y_ps"], u - 1)
            for d in range(2):
                for r in range(R_C):
                    c = 32 * d + 4 * q + r
                    a.activation(e[:, u % 2, d, r, :], ps[:, 1 + 2 * (u % 2) + d, r * P:(r + 1) * P], ACT.Exp,
                                 bias=g.nacs[:, t, c:c + 1]).then_inc(S["exp"], 1)
            if t == 1:
                act.wait_ge(S["sp_ps"], q + 1)
                if q >= 1:
                    act.wait_ge(S["stage"], 32 * q)
                a.copy(stage[:, :], ps[:, 6, :]).then_inc(S["sp_ev"], 1)

    @block.vector
    def _(dve):
        v = nc.vector
        v.tensor_copy(ident_h[:, :], s.ident).then_inc(S["init"], 1)
        v.tensor_copy(mask_h[:, 0, :], s.cid("mask_high")).then_inc(S["init"], 1)
        v.tensor_copy(mask_h[:, 1, :], s.cid("mask_low")).then_inc(S["init"], 1)

        def weigh(q, t):
            u = 3 * q + t
            dve.wait_ge(S["exp"], 8 * (u + 1))
            m = e[:, u % 2].rearrange("p d r i -> p (d r) i")
            v.tensor_tensor(m, m, cb[:, t, :].unsqueeze(1).broadcast_to([P, 2 * R_C, P]), ALU.mult).then_inc(S["m"], 1)

        def take(q, t):
            u = 3 * q + t
            dve.wait_ge(S["y_ps"], u + 1)
            dve.wait_ge(S["pool"], u + 1)
            v.tensor_tensor(xs[:, t, q * W:(q + 1) * W], ps[:, 5, 0:W], xs[:, t, q * W:(q + 1) * W], ALU.add).then_inc(S["y_ev"], 1)
            dve.wait_ge(S["y_ev"], u + 1)

        def add_inter(q, rnd, d):
            t = (1, 2)[d] if rnd == 0 else (2, 1)[d]
            yq = xs[:, t, q * W:(q + 1) * W]
            link(s, "dve", dve, v.tensor_tensor(yq, yq, inter[:, d, :], ALU.add))

        def scale_inter(q, rnd):
            dve.wait_ge(S["i_ps"], 2 * q + rnd + 1)
            for d in range(2):
                t = (1, 2)[d] if rnd == 0 else (2, 1)[d]
                c = 32 * d + 4 * q
                ins = v.tensor_tensor(inter[:, d, :].rearrange("p (h d) -> p h d", h=R_C), ps[:, 7, d * W:(d + 1) * W].rearrange("p (h d) -> p h d", h=R_C),
                                      g.eacs[:, t, c:c + 4].unsqueeze(2).broadcast_to([P, R_C, P_C]), ALU.mult)
                if d == 0:
                    link(s, "dve", dve, ins)
            ins.then_inc(S["i_ev"], 1)
            dve.wait_ge(S["i_ev"], 2 * q + rnd + 1)

        for q in range(G_C):
            dve.wait_ge(S["cb_ps"], q + 1)
            v.tensor_copy(cb[:, :, :].rearrange("p t i -> p (t i)"), ps[:, 0, 0:NTOK]).then_inc(S["cb_ev"], 1)
            dve.wait_ge(S["cb_ev"], q + 1)
            weigh(q, 0)
            weigh(q, 1)
            scale_inter(q, 0)
            for d in range(2):
                c, tt = 32 * d + 4 * q, 1 + d
                sq = g.state[:, d, q * W:(q + 1) * W].rearrange("p (h d) -> p h d", h=R_C)
                link(s, "dve", dve, v.tensor_tensor(sq, sq, g.etot[:, tt, c:c + 4].unsqueeze(2).broadcast_to([P, R_C, P_C]), ALU.mult))
            take(q, 0)
            weigh(q, 2)
            dve.wait_ge(S["s1_ps"], q + 1)
            for d in range(2):
                sq = g.state[:, d, q * W:(q + 1) * W]
                v.tensor_tensor(sq, sq, ps[:, 6, d * W:(d + 1) * W], ALU.add).then_inc(S["upd"], 1)
            take(q, 1)
            add_inter(q, 0, 0)
            take(q, 2)
            add_inter(q, 0, 1)
            scale_inter(q, 1)
            add_inter(q, 1, 0)
            add_inter(q, 1, 1)


def ssd_gate(s, st, xs, y_t):
    nc, w, ps = s.nc, s.w, s.ps
    sb = stage_buffers(s, st, "gate_")
    z = sb("z", [P, 2, BANK])
    gw_in, gw = sb("gw_in", [16, P]), sb("gw", [P, 16])
    sq = sb("sq", [P, 256])
    ss, x, r, tmp = (sb(n, [P, T * G_C]) for n in ("ss", "x", "r", "tmp"))
    names = ("z_ps", "z", "y", "ss", "x", "r", "yn", "gw_ps", "gw", "t_ps", "t_ev")
    S = {n: s.sem("gate_" + n) for n in names}
    z0 = s.at["ssd_z", 0]
    block = st.enter_context(nc.Block())

    @block.sync
    def _(sp):
        sp.dma_start(gw_in[:, :], w["ssd_norm"][0].rearrange("(k p) -> k p", p=P)).then_inc(s.loads, 16)
        s.loaded += 16
        ring_loads(s, sp, z0 + 4 + SLOT_RING)

    @block.tensor
    def _(pe):
        for j in range(4):
            ring_wait(s, pe, z0 + j)
            for t in range(T):
                n = 3 * j + t
                if n >= 4:
                    pe.wait_ge(S["z"], n - 3)
                for k in range(KD):
                    mm = pe.matmul(ps[:, n % 4, :], s.hT[:, k, t * P:(t + 1) * P], s.ring[:, (z0 + j) % SLOT_RING, k, :],
                                   start=(k == 0), stop=(k == KD - 1))
                mm.then_inc(S["z_ps"], 1)
            pe.wait_ge(S["z_ps"], 3 * j + 3)
            pe.sem_inc(s.ring_free, 1)
        pe.wait_ge(s.loads, s.loaded)
        pe.wait_ge(S["z"], 12)
        pe.transpose(ps[:, 0, 0:16], gw_in[:, :], s.ident[0:16, 0:16]).then_inc(S["gw_ps"], 1)
        pe.wait_ge(S["gw"], 1)
        for t in range(T):
            pe.wait_ge(S["yn"], t + 1)
            if t >= 2:
                pe.wait_ge(S["t_ev"], 4 * (t - 1))
            for k in range(16):
                mm = pe.transpose(ps[:, 4 * (t % 2) + k // 4, (k % 4) * P:(k % 4 + 1) * P], xs[:, t, k * P:(k + 1) * P], s.ident)
            mm.then_inc(S["t_ps"], 1)

    @block.scalar
    def _(act):
        a = nc.scalar
        for n in range(12):
            act.wait_ge(S["z_ps"], n + 1)
            if n >= 2:
                act.wait_ge(S["y"], n - 1)
            a.activation(z[:, n % 2, :], ps[:, n % 4, :], ACT.Silu).then_inc(S["z"], 1)
        act.wait_ge(S["y"], 12)
        for t in range(T):
            for q in range(G_C):
                i = t * G_C + q
                if i:
                    act.wait_ge(S["ss"], i)
                a.activation(sq[:, :], xs[:, t, q * 256:(q + 1) * 256], ACT.Square, accum_out=ss[:, i:i + 1]).then_inc(S["ss"], 1)
        rsqrt_act(s, act, x[:, :], r[:, :], S["x"], 1, S["r"])

    @block.vector
    def _(dve):
        v = nc.vector
        for n in range(12):
            j, t = divmod(n, T)
            dve.wait_ge(S["z"], n + 1)
            yj = xs[:, t, j * BANK:(j + 1) * BANK]
            v.tensor_tensor(yj, yj, z[:, n % 2, :], ALU.mult).then_inc(S["y"], 1)
        dve.wait_ge(S["gw_ps"], 1)
        v.tensor_copy(gw[:, :], ps[:, 0, 0:16]).then_inc(S["gw"], 1)
        dve.wait_ge(S["ss"], T * G_C)
        v.tensor_scalar(x[:, :], ss[:, :], 1.0 / 256, EPS, ALU.mult, ALU.add).then_inc(S["x"], 1)
        rsqrt_dve(s, dve, x[:, :], r[:, :], tmp[:, :], S["r"], 1)
        for t in range(T):
            yt = xs[:, t, :].rearrange("p (q c) -> p q c", q=G_C)
            v.tensor_tensor(yt, yt, r[:, t * G_C:(t + 1) * G_C].unsqueeze(2).broadcast_to([P, G_C, 256]), ALU.mult).then_inc(S["yn"], 1)
        for t in range(T):
            dve.wait_ge(S["t_ps"], t + 1)
            for b in range(4):
                v.tensor_tensor(y_t[:, 4 * b:4 * b + 4, t * P:(t + 1) * P], ps[:, 4 * (t % 2) + b, :].rearrange("p (k n) -> p k n", k=4),
                                gw[:, 4 * b:4 * b + 4].unsqueeze(2).broadcast_to([P, 4, P]), ALU.mult).then_inc(S["t_ev"], 1)


def moe(s, l, st):
    sb = stage_buffers(s, st, f"moe{l}_")
    m = Shared()
    m.hp = [sb(n, [P, T, KD, P], F32R) for n in ("hp_hi", "hp_lo")]
    m.acc = s.hT[:, :, :].rearrange("p k n -> p (k n)").rearrange("p (t d) -> p t d", t=T)
    m.gates = sb("gates", [P, T, NE])
    m.code = sb("code", [P, T, NE])
    m.most = sb("most", [1, 1], I32)
    with ExitStack() as st2:
        norm_stage(s, l, FFN, st2, hp=m.hp)
    with ExitStack() as st2:
        route(s, l, st2, m)
    with ExitStack() as st2:
        experts(s, l, st2, m)
    with ExitStack() as st2:
        add_moe(s, l, st2, m)


def route(s, l, st, m):
    nc, w, ps = s.nc, s.w, s.ps
    sb = stage_buffers(s, st, f"rt{l}_")
    rw, rb = sb("rw", [P, KD, NG + NE]), sb("rb", [P, NG + NE])
    lg = sb("lg", [P, T, NG + NE])
    v4 = sb("v4", [P, T, NG])
    oh4 = sb("oh4", [P, T, NG])
    le, eq, oh1, oh2, sel = (sb(n, [P, T, NE]) for n in ("le", "eq", "oh1", "oh2", "sel"))
    mx, m1, m2, t1, ptop, w1, w2 = (sb(n, [P, T, 1]) for n in ("mx", "m1", "m2", "t1", "ptop", "w1", "w2"))
    top = sb("top", [P, 1])
    names = ("lg_ps", "x4", "e4", "x2", "e2", "sel", "rank_ps")
    S = {n: s.sem(f"rt{l}_" + n) for n in names}
    block = st.enter_context(nc.Block())

    @block.sync
    def _(sp):
        loads = [(rw[:, :, 0:NG], w["moe_wg"][l].rearrange("(p k) n -> p k n", k=KD)),
                 (rw[:, :, NG:NG + NE], w["moe_we"][l].rearrange("(p k) n -> p k n", k=KD)),
                 (rb[:, 0:NG], w["moe_bg"][l].partition_broadcast(P)),
                 (rb[:, NG:NG + NE], w["moe_be"][l].partition_broadcast(P))]
        for dst, src in loads:
            sp.dma_start(dst, src).then_inc(s.loads, 16)
        s.loaded += 16 * len(loads)

    @block.tensor
    def _(pe):
        pe.wait_ge(s.loads, s.loaded)
        for t in range(T):
            for k in range(KD):
                mm = narrow_matmul(pe, ps[:, 0, t * 36:(t + 1) * 36], s.hT[:, k, t * P:(t + 1) * P], rw[:, k, :],
                                   start=(k == 0), stop=(k == KD - 1))
        mm.then_inc(S["lg_ps"], 1)
        pe.wait_ge(S["sel"], 1)
        for t in range(T):
            for b in range(t):
                narrow_matmul(pe, ps[:, 1, t * NE:(t + 1) * NE], s.cid("ones"), sel[:, b, :], start=(b == 0), stop=False)
            narrow_matmul(pe, ps[:, 1, t * NE:(t + 1) * NE], s.cid("before"), sel[:, t, :], start=(t == 0), stop=True)
        for t in range(T):
            mm = narrow_matmul(pe, ps[:, 1, T * NE:(T + 1) * NE], s.cid("ones"), sel[:, t, :], start=(t == 0), stop=(t == T - 1))
        mm.then_inc(S["rank_ps"], 1)

    @block.scalar
    def _(act):
        act.wait_ge(S["x4"], 1)
        nc.scalar.activation(v4[:, :, :], v4[:, :, :], ACT.Exp).then_inc(S["e4"], 1)
        act.wait_ge(S["x2"], 1)
        nc.scalar.activation(w2[:, :, :], w2[:, :, :], ACT.Exp).then_inc(S["e2"], 1)

    @block.vector
    def _(dve):
        v = nc.vector

        def do(ins):
            link(s, "dve", dve, ins)

        def wide(a, n):
            return a.broadcast_to([P, T, n])

        def first_of(dst, values, most, order, n):
            e = eq[:, :, 0:n]
            do(v.tensor_tensor(e, values, wide(most, n), ALU.is_equal))
            do(v.tensor_tensor(e, e, order.unsqueeze(1).broadcast_to([P, T, n]), ALU.mult))
            do(v.tensor_reduce(t1[:, :, :], e, AX.X, ALU.max))
            do(v.tensor_tensor(dst, e, wide(t1[:, :, :], n), ALU.is_equal))

        dve.wait_ge(s.loads, s.loaded)
        dve.wait_ge(S["lg_ps"], 1)
        do(v.tensor_tensor(lg[:, :, :], ps[:, 0, 0:T * 36].rearrange("p (t n) -> p t n", t=T), rb[:, :].unsqueeze(1).broadcast_to([P, T, 36]), ALU.add))
        grp = lg[:, :, 0:NG]
        do(v.tensor_reduce(mx[:, :, :], grp, AX.X, ALU.max))
        v.tensor_tensor(v4[:, :, :], grp, wide(mx[:, :, :], NG), ALU.subtract).then_inc(S["x4"], 1)
        first_of(oh4[:, :, :], grp, mx[:, :, :], s.cid("rank4"), NG)
        do(v.tensor_scalar(oh4[:, :, :], oh4[:, :, :], -1.0, BIG, ALU.add, ALU.mult))
        do(v.tensor_copy(le[:, :, :], lg[:, :, NG:]))
        for t in range(T):
            le_t = le[:, t, :].rearrange("p (g e) -> p g e", g=NG)
            do(v.tensor_tensor(le_t, le_t, oh4[:, t, :].unsqueeze(2).broadcast_to([P, NG, PER]), ALU.add))
        do(v.tensor_reduce(m1[:, :, :], le[:, :, :], AX.X, ALU.max))
        first_of(oh1[:, :, :], le[:, :, :], m1[:, :, :], s.cid("rank32"), NE)
        do(v.scalar_tensor_tensor(out=le[:, :, :], in0=oh1[:, :, :], scalar=-3 * BIG, in1=le[:, :, :], op0=ALU.mult, op1=ALU.add))
        do(v.tensor_reduce(m2[:, :, :], le[:, :, :], AX.X, ALU.max))
        first_of(oh2[:, :, :], le[:, :, :], m2[:, :, :], s.cid("rank32"), NE)
        v.tensor_tensor(w2[:, :, :], m2[:, :, :], m1[:, :, :], ALU.subtract).then_inc(S["x2"], 1)
        v.tensor_tensor(sel[:, :, :], oh1[:, :, :], oh2[:, :, :], ALU.add).then_inc(S["sel"], 1)
        dve.wait_ge(S["e4"], 1)
        do(v.tensor_reduce(ptop[:, :, :], v4[:, :, :], AX.X, ALU.add))
        dve.wait_ge(S["e2"], 1)
        do(v.tensor_scalar(w1[:, :, :], w2[:, :, :], 1.0, None, ALU.add))
        do(v.tensor_tensor(w1[:, :, :], w1[:, :, :], ptop[:, :, :], ALU.mult))
        do(v.reciprocal(w1[:, :, :], w1[:, :, :]))
        do(v.tensor_tensor(w2[:, :, :], w2[:, :, :], w1[:, :, :], ALU.mult))
        do(v.tensor_tensor(oh1[:, :, :], oh1[:, :, :], wide(w1[:, :, :], NE), ALU.mult))
        do(v.tensor_tensor(oh2[:, :, :], oh2[:, :, :], wide(w2[:, :, :], NE), ALU.mult))
        do(v.tensor_tensor(m.gates[:, :, :], oh1[:, :, :], oh2[:, :, :], ALU.add))
        dve.wait_ge(S["sel"], 1)
        dve.wait_ge(S["rank_ps"], 1)
        do(v.scalar_tensor_tensor(out=m.code[:, :, :], in0=ps[:, 1, 0:T * NE].rearrange("p (t n) -> p t n", t=T), scalar=1.0,
                                  in1=sel[:, :, :], op0=ALU.add, op1=ALU.mult))
        do(v.tensor_scalar(m.code[:, :, :], m.code[:, :, :], -1.0, None, ALU.add))
        do(v.tensor_reduce(top[:, :], ps[:, 1, T * NE:(T + 1) * NE], AX.X, ALU.max))
        do(v.tensor_copy(m.most[:, :], top[0:1, :]))


class PairSteps:

    NAMES = ("onehot", "gate_in", "gt_ps", "gt_ev", "hg_ps", "hg_ev", "h_ps", "silu", "hid", "ht_ps", "ht_ev", "o_ps", "o_ev", "lo_ev", "sc_ps", "sc_ev")

    def __init__(self, s, m, bufs, sems, deep, wide):
        self.s, self.m, self.b, self.S, self.deep, self.wide = s, m, bufs, sems, deep, wide

    def wait(self, eng, name, value, at_least=1):
        if at_least > 0:
            eng.wait_ge(self.S[name], value)

    def onehot(self, dve, i, n, g, j, n0):
        v, m = self.s.nc.vector, self.m
        back = self.deep * self.wide
        halves = 2 // self.wide
        self.wait(dve, "hg_ps", halves * (n - j + self.wide - back), n0 - j + self.wide - back)
        self.wait(dve, "gt_ps", n + 1 - back, n0 + 1 - back)
        for e in range(2):
            c = j * P + e * SLOTS
            v.tensor_tensor(self.b.onehot[:, g, :, c:c + SLOTS],
                            self.s.cid("slot_no")[:, 0:SLOTS].unsqueeze(1).broadcast_to([P, T, SLOTS]),
                            m.code[:, :, bass.ds(2 * i + e, 1)].broadcast_to([P, T, SLOTS]), ALU.is_equal).then_inc(self.S["onehot"], 1)

    def take_gates(self, dve, i, n, b, n0):
        self.wait(dve, "gt_ps", n + 1 - self.deep, n0 + 1 - self.deep)
        self.s.nc.vector.tensor_copy(self.b.turn[:, b, :, P:P + 2], self.m.gates[:, :, bass.ds(2 * i, 2)]).then_inc(self.S["gate_in"], 1)

    def take_turned(self, dve, n, b, n0):
        v = self.s.nc.vector
        dve.wait_ge(self.S["gt_ps"], n + 1)
        self.wait(dve, "sc_ps", 6 * (n + 1 - self.deep), n0 + 1 - self.deep)
        turned = self.s.ps[:, 3, 0:T * (P + 2)].rearrange("p (t c) -> p t c", t=T)
        v.tensor_copy(self.b.onehot_t[:, b, :].rearrange("p (t n) -> p t n", t=T), turned[:, :, 0:P]).then_inc(self.S["gt_ev"], 1)
        for e in range(2):
            q = slice(e * SLOTS, (e + 1) * SLOTS)
            v.tensor_reduce(self.b.slot_gate[q, b:b + 1], turned[q, :, P + e:P + e + 1].rearrange("p t c -> p c t"), AX.X, ALU.add).then_inc(self.S["gt_ev"], 1)

    def hidden(self, dve, n, b):
        dve.wait_ge(self.S["silu"], n + 1)
        dve.wait_ge(self.S["gt_ev"], 3 * (n + 1))
        self.s.nc.vector.scalar_tensor_tensor(out=self.b.hid[:, :], in0=self.s.ps[:, 2, FE:2 * FE], scalar=self.b.slot_gate[:, b:b + 1],
                                              in1=self.b.silu[:, :], op0=ALU.mult, op1=ALU.mult).then_inc(self.S["hid"], 1)

    def take_hidden(self, dve, n, n0):
        dve.wait_ge(self.S["ht_ps"], n + 1)
        self.wait(dve, "o_ps", 2 * n, n0)
        self.s.nc.vector.tensor_copy(self.b.hid_t[:, :], self.s.ps[:, 2, 0:2 * P]).then_inc(self.S["ht_ev"], 1)

    def out_low(self, dve, n, b, n0):
        self.wait(dve, "sc_ps", 6 * (n + 1 - self.deep), n0 + 1 - self.deep)
        for h in range(2):
            c = slice(h * BANK, (h + 1) * BANK)
            dve.wait_ge(self.S["o_ev"], 2 * n + h + 1)
            self.s.nc.vector.tensor_tensor(self.b.o_lo[:, b, c], self.s.ps[:, 5 + h, :], self.b.o_hi[:, b, c].bitcast(F32),
                                           ALU.subtract).then_inc(self.S["lo_ev"], 1)

    def add_tokens(self, dve, n):
        v, acc = self.s.nc.vector, self.m.acc
        for q in range(6):
            t, h = divmod(q, 2)
            dve.wait_ge(self.S["sc_ps"], 6 * n + q + 1)
            a = acc[:, t, h * BANK:(h + 1) * BANK]
            v.tensor_tensor(a, a, self.s.ps[:, 4 if q % 2 else 7, :], ALU.add).then_inc(self.S["sc_ev"], 1)

    def gathered(self, x):
        return self.s.ps[:, 0:2, :].rearrange("p b (k n) -> p (b k) n", k=2)[:, :, 0:x]

    def take_gathered(self, act, h, g, half, h0):
        act.wait_ge(self.S["hg_ps"], h + 1)
        self.wait(act, "h_ps", self.wide * (h - half) + 2 * self.wide * (1 - self.deep), h0 - half + 2 * (1 - self.deep))
        n = self.wide * P
        self.s.nc.scalar.copy(self.b.hg[:, g, 4 * half:4 * half + 4, 0:n], self.gathered(n)).then_inc(self.S["hg_ev"], 1)

    def silu(self, act, n, n0):
        act.wait_ge(self.S["h_ps"], 2 * (n + 1))
        self.wait(act, "hid", n, n0)
        self.s.nc.scalar.activation(self.b.silu[:, :], self.s.ps[:, 2, 0:FE], ACT.Silu).then_inc(self.S["silu"], 1)

    def take_out(self, act, n, b, n0):
        act.wait_ge(self.S["o_ps"], 2 * (n + 1))
        self.wait(act, "sc_ps", 6 * (n + 1 - self.deep), n0 + 1 - self.deep)
        for h in range(2):
            self.s.nc.scalar.copy(self.b.o_hi[:, b, h * BANK:(h + 1) * BANK], self.s.ps[:, 5 + h, :]).then_inc(self.S["o_ev"], 1)

    def turn_onehot(self, pe, n, b, g, j, n0):
        ps, oh = self.s.ps, self.b.onehot
        pe.wait_ge(self.S["onehot"], 2 * (n + 1))
        pe.wait_ge(self.S["gate_in"], n + 1)
        self.wait(pe, "gt_ev", 3 * n, n0)
        for t in range(T):
            mm = pe.matmul(ps[:, 3, t * (P + 2):(t + 1) * (P + 2)], oh[:, g, t, j * P:(j + 1) * P].bitcast(F32), self.b.turn[:, b, t, :], start=True, stop=True)
        mm.then_inc(self.S["gt_ps"], 1)

    def gather(self, pe, h, g, half, h0):
        pe.wait_ge(self.S["onehot"], self.wide * (h - half) + 2 * self.wide)
        self.wait(pe, "hg_ev", h, h0)
        n = self.wide * P
        for k in range(4):
            for t in range(T):
                for part in (0, 1):
                    mm = pe.matmul(self.gathered(n)[:, k, :], self.m.hp[part][:, t, 4 * half + k, :], self.b.onehot[:, g, t, 0:n],
                                   start=(t + part == 0), stop=(t + part == T))
        mm.then_inc(self.S["hg_ps"], 1)

    def hidden_products(self, pe, n, g, j, n0, w13, ready):
        ps = self.s.ps
        pe.wait_ge(self.S["hg_ev"], n - j + 2 if self.wide == 2 else 2 * n + 2)
        self.wait(pe, "ht_ev", n, n0)
        for e, k in self.order(pe, ready, range(KD)):
            c = j * P + e * SLOTS
            mm = pe.matmul(ps[e * SLOTS:(e + 1) * SLOTS, 2, :], self.b.hg[:, g, k, c:c + SLOTS],
                           w13(e)[:, k, :], start=(k == 0), stop=(k == KD - 1))
            if k == KD - 1:
                mm.then_inc(self.S["h_ps"], 1)

    def order(self, pe, ready, steps):
        if self.deep == 1:
            for e in range(2):
                ready(pe, e)
                for x in steps:
                    yield e, x
        else:
            ready(pe, 0)
            ready(pe, 1)
            for x in steps:
                yield 0, x
                yield 1, x

    def turn_hidden(self, pe, n):
        pe.wait_ge(self.S["hid"], n + 1)
        for c in range(2):
            mm = pe.transpose(self.s.ps[:, 2, c * P:(c + 1) * P], self.b.hid[:, c::2], self.s.ident)
        mm.then_inc(self.S["ht_ps"], 1)

    def out_products(self, pe, n, n0, w2, ready, halves=(0, 1)):
        pe.wait_ge(self.S["ht_ev"], n + 1)
        self.wait(pe, "lo_ev", 2 * n, n0)
        for e, (h, c) in self.order(pe, ready, [(h, c) for h in halves for c in range(2)]):
            mm = pe.matmul(self.s.ps[e * SLOTS:(e + 1) * SLOTS, 5 + h, :], self.b.hid_t[:, c * P + e * SLOTS:c * P + (e + 1) * SLOTS],
                           w2(e)[:, c, h * BANK:(h + 1) * BANK], start=(c == 0), stop=(c == 1))
            if (h, c) == (1, 1):
                mm.then_inc(self.S["o_ps"], 1)

    def scatter(self, pe, n, b, n0, parts=range(6)):
        pe.wait_ge(self.S["lo_ev"], 2 * (n + 1))
        pe.wait_ge(self.S["gt_ev"], 3 * (n + 1))
        for q in parts:
            t, h = divmod(q, 2)
            if q >= 2 or n0 > 0:
                pe.wait_ge(self.S["sc_ev"], 6 * n + q - 1)
            for part in (self.b.o_hi, self.b.o_lo):
                mm = pe.matmul(self.s.ps[:, 4 if q % 2 else 7, :], self.b.onehot_t[:, b, t * P:(t + 1) * P],
                               part[:, b, h * BANK:(h + 1) * BANK], start=(part is self.b.o_hi), stop=(part is self.b.o_lo))
            mm.then_inc(self.S["sc_ps"], 1)


def experts(s, l, st, m):
    nc, w = s.nc, s.w
    sb = stage_buffers(s, st, f"ex{l}_")

    def buffers(pre, deep):
        b = Shared()
        b.onehot = sb(pre + "onehot", [P, deep, T, 2 * P], F32R)
        b.turn = sb(pre + "turn", [P, deep, T, P + 2])
        b.onehot_t = sb(pre + "onehot_t", [P, deep, NTOK], F32R)
        b.slot_gate = sb(pre + "slot_gate", [P, deep])
        b.hg = sb(pre + "hg", [P, deep, KD, 2 * P])
        b.silu, b.hid = sb(pre + "silu", [P, FE]), sb(pre + "hid", [P, FE])
        b.hid_t = sb(pre + "hid_t", [P, 2 * P])
        b.o_hi, b.o_lo = (sb(pre + n, [P, deep, D], F32R) for n in ("o_hi", "o_lo"))
        return b

    w2_ring = sb("w2_ring", [P, 4, 2, D])
    bufs = buffers("", 2)
    over_w = w2_ring[:, 2:4, :, :].rearrange("p e c (h n) -> p (e c h) n", n=BANK)
    S = {n: s.sem(f"ex{l}_" + n) for n in PairSteps.NAMES}
    V = {n: s.sem(f"ov{l}_" + n) for n in PairSteps.NAMES}
    w2_full = [s.sem(f"ex{l}_w2_full{n}") for n in range(4)]
    zeroed, shifted, ov_w13, ov_w2 = (s.sem(f"ex{l}_" + n) for n in ("zeroed", "shifted", "ov_w13", "ov_w2"))
    base = s.at["moe", l]
    main = PairSteps(s, m, bufs, S, 2, 2)
    over = PairSteps(s, m, bufs, V, 1, 1)
    w1v = w["moe_w1"][l].rearrange("e (p k) f -> p e k f", k=KD)
    w3v = w["moe_w3"][l].rearrange("e (p k) f -> p e k f", k=KD)
    w2v = w["moe_w2"][l].rearrange("e (p c) d -> p e c d", c=2)
    block = st.enter_context(nc.Block())

    def engine_rounds(eng, steps, before):
        most = eng.value_load(m.most[0:1, 0:1], min_val=0, max_val=NTOK)
        with eng.If(most > SLOTS):
            eng.wait_ge(S["sc_ev"], 6 * PAIRS)
            for r in range(1, ROUNDS):
                before()
                first = PAIRS * (r - 1)
                steps(0, first, first)
                with eng.Fori(1, PAIRS) as i:
                    steps(i, first + i, first + 1)

    @block.sync
    def _(sp):
        def w13_load(dst, ex, done):
            for src, c in ((w1v, 0), (w3v, FE)):
                sp.dma_start(dst[:, :, c:c + FE], src[:, bass.ds(ex, 1)].rearrange("p e k f -> p (e k) f")).then_inc(done, 16)

        def w2_load(dst, ex, done):
            sp.dma_start(dst, w2v[:, bass.ds(ex, 1)].rearrange("p e c d -> p (e c) d")).then_inc(done, 16)

        for e in range(4):
            slot = (base + e) % SLOT_RING
            if s.issued <= base + e:
                sp.wait_ge(s.ring_free, base + e - SLOT_RING + 1)
                w13_load(s.ring[:, slot], e, s.ring_full[slot])
            w2_load(w2_ring[:, e], e, w2_full[e])
        with sp.Fori(0, NE // 4 - 1) as q:
            for e in range(4):
                slot = (base + e) % SLOT_RING
                sp.wait_ge(S["h_ps"], 4 * q + e + 1)
                w13_load(s.ring[:, slot], 4 * q + 4 + e, s.ring_full[slot])
                sp.wait_ge(S["o_ps"], 4 * q + e + 1)
                w2_load(w2_ring[:, e], 4 * q + 4 + e, w2_full[e])
        s.issued = base + NE
        ring_loads(s, sp, base + NE + SLOT_RING)
        sp.wait_ge(S["o_ps"], NE)

        def steps(i, n, n0):
            for e in range(2):
                if n0 + e > 0:
                    sp.wait_ge(V["h_ps"], 2 * n + e)
                w13_load(over_w, 2 * i + e, ov_w13)
                if n0 + e > 0:
                    sp.wait_ge(V["o_ps"], 2 * n + e)
                w2_load(w2_ring[:, 0], 2 * i + e, ov_w2)

        engine_rounds(sp, steps, lambda: None)

    @block.tensor
    def _(pe):
        def step(i, p, j):
            n0, b = p, p % 2
            def w13_ready(eng, e):
                x = 2 * p + e
                eng.wait_ge(s.ring_full[(base + x) % SLOT_RING], s.fill_of[base + x] + 32 * j)

            def w2_ready(eng, e):
                x = 2 * p + e
                eng.wait_ge(w2_full[x % 4], 16 * (x // 4 + 1) + 16 * j)

            g, place = (p // 2) % 2, p % 2
            main.hidden_products(pe, i, g, place, n0, lambda e: s.ring[:, (base + 2 * p + e) % SLOT_RING], w13_ready)
            if p < PAIRS - 2:
                main.gather(pe, i + 2, 1 - g, place, n0 + 2)
            if p < PAIRS - 1:
                main.turn_onehot(pe, i + 1, 1 - b, ((p + 1) // 2) % 2, 1 - place, n0 + 1)
            main.turn_hidden(pe, i)
            for h in range(2):
                if p > 0:
                    main.scatter(pe, i - 1, 1 - b, n0 - 1, (2 * h, 2 * h + 1))
                main.out_products(pe, i, n0, lambda e: w2_ring[:, (2 * p + e) % 4], w2_ready, (h,))
            if p > 0:
                main.scatter(pe, i - 1, 1 - b, n0 - 1, (4, 5))

        pe.wait_ge(zeroed, 1 + 2 * T)
        main.gather(pe, 0, 0, 0, 0)
        main.gather(pe, 1, 0, 1, 1)
        main.turn_onehot(pe, 0, 0, 0, 0, 0)
        for p in range(TURN):
            step(p, p, 0)
        with pe.Fori(0, TURNS) as j:
            for p in range(TURN, 2 * TURN):
                step(TURN * j + p, p, 2 * j)
        for p in range(PAIRS - TURN, PAIRS):
            step(p, p, 0)
        main.scatter(pe, PAIRS - 1, (PAIRS - 1) % 2, PAIRS - 1)
        pe.wait_ge(S["h_ps"], NE)
        pe.sem_inc(s.ring_free, NE)

        def steps(i, n, n0):
            for half in range(2):
                over.gather(pe, 2 * n + half, 0, half, 2 * n0 + half)
            over.turn_onehot(pe, n, 0, 0, 0, n0)
            over.hidden_products(pe, n, 0, 0, n0, lambda e: over_w, lambda eng, e: eng.wait_ge(ov_w13, 64 * n + 32 * (e + 1)))
            over.turn_hidden(pe, n)
            over.out_products(pe, n, n0, lambda e: w2_ring[:, 0], lambda eng, e: eng.wait_ge(ov_w2, 32 * n + 16 * (e + 1)))
            over.scatter(pe, n, 0, n0)

        engine_rounds(pe, steps, lambda: None)

    @block.scalar
    def _(act):
        def step(i, p):
            main.silu(act, i, p)
            if p < PAIRS - 2:
                main.take_gathered(act, i + 2, (p // 2 + 1) % 2, p % 2, p + 2)
            main.take_out(act, i, p % 2, p)

        main.take_gathered(act, 0, 0, 0, 0)
        main.take_gathered(act, 1, 0, 1, 1)
        for p in range(TURN):
            step(p, p)
        with act.Fori(0, TURNS) as j:
            for p in range(TURN, 2 * TURN):
                step(TURN * j + p, p)
        for p in range(PAIRS - TURN, PAIRS):
            step(p, p)

        def steps(i, n, n0):
            for half in range(2):
                over.take_gathered(act, 2 * n + half, 0, half, 2 * n0 + half)
            over.silu(act, n, n0)
            over.take_out(act, n, 0, n0)

        engine_rounds(act, steps, lambda: None)

    @block.vector
    def _(dve):
        def step(i, p):
            if p > 0:
                main.out_low(dve, i - 1, (p - 1) % 2, p - 1)
            main.hidden(dve, i, p % 2)
            main.take_hidden(dve, i, p)
            if p > 0:
                main.add_tokens(dve, i - 1)
            if p < PAIRS - 1:
                main.take_turned(dve, i + 1, (p + 1) % 2, p + 1)
            if p < PAIRS - 2:
                main.take_gates(dve, i + 2, i + 2, p % 2, p + 2)
            if p < PAIRS - 4:
                main.onehot(dve, i + 4, i + 4, (p // 2) % 2, p % 2, p + 4)

        nc.vector.memset(m.acc[:, :, :], 0.0).then_inc(zeroed, 1)
        for b in range(2):
            for t in range(T):
                nc.vector.tensor_copy(bufs.turn[:, b, t, 0:P], s.ident).then_inc(zeroed, 1)
        for p in range(4):
            main.onehot(dve, p, p, p // 2, p % 2, p)
        for p in range(2):
            main.take_gates(dve, p, p, p, p)
        main.take_turned(dve, 0, 0, 0)
        for p in range(TURN):
            step(p, p)
        with dve.Fori(0, TURNS) as j:
            for p in range(TURN, 2 * TURN):
                step(TURN * j + p, p)
        for p in range(PAIRS - TURN, PAIRS):
            step(p, p)
        main.out_low(dve, PAIRS - 1, (PAIRS - 1) % 2, PAIRS - 1)
        main.add_tokens(dve, PAIRS - 1)

        rounds = [0]

        def next_round():
            rounds[0] += 1
            if rounds[0] > 1:
                dve.wait_ge(V["hg_ps"], 2 * PAIRS * (rounds[0] - 1))
            nc.vector.tensor_scalar(m.code[:, :, :], m.code[:, :, :], -float(SLOTS), None, ALU.add).then_inc(shifted, 1)
            dve.wait_ge(shifted, rounds[0])

        def steps(i, n, n0):
            over.onehot(dve, i, n, 0, 0, n0)
            over.take_gates(dve, i, n, 0, n0)
            over.take_turned(dve, n, 0, n0)
            over.hidden(dve, n, 0)
            over.take_hidden(dve, n, n0)
            over.out_low(dve, n, 0, n0)
            over.add_tokens(dve, n)

        engine_rounds(dve, steps, next_round)


TURN = 4
TURNS = PAIRS // TURN - 2


def add_moe(s, l, st, m):
    nc, ps = s.nc, s.ps
    g_ps, mul = s.sem(f"am{l}_g_ps"), s.sem(f"am{l}_mul")
    rows = slice(32 * l, 32 * l + 2)
    block = st.enter_context(nc.Block())

    @block.tensor
    def _(pe):
        for g in range(2):
            for h in range(2):
                mm = pe.matmul(ps[:, 2 * g + h, :], s.cid("pick")[rows, g * P:(g + 1) * P], s.gates[rows, FFN, h * BANK:(h + 1) * BANK],
                               start=True, stop=True)
        mm.then_inc(g_ps, 1)

    @block.vector
    def _(dve):
        v = nc.vector
        dve.wait_ge(g_ps, 1)
        for n in range(2 * T):
            t, h = divmod(n, 2)
            a = m.acc[:, t, h * BANK:(h + 1) * BANK]
            v.tensor_tensor(a, a, ps[:, 2 * min(t, 1) + h, :], ALU.mult).then_inc(mul, 1)
        for n in range(2 * T):
            t, h = divmod(n, 2)
            dve.wait_ge(mul, n + 1)
            ys = s.y[:, t, h * BANK:(h + 1) * BANK]
            v.tensor_tensor(ys, ys, m.acc[:, t, h * BANK:(h + 1) * BANK], ALU.add)


_INS = ["x_prompt", "x_sample", "cache_a_k", "cache_a_v", "cache_b_ckv", "cache_b_krope", "state_c_fwd", "state_c_bwd",
        "c", "c_ctx", "ada_w", "ada_b", "norm_mix", "norm_ffn",
        "att_w_in", "att_a_qnorm", "att_a_knorm", "att_a_sink", "att_b_qa_norm", "att_b_wuq", "att_b_kva_norm",
        "att_b_wukv", "att_b_qnorm", "att_b_knorm", "att_w_out",
        "ssd_w_in", "ssd_conv_w", "ssd_conv_b", "ssd_alog_fwd", "ssd_alog_bwd", "ssd_dtb_fwd", "ssd_dtb_bwd", "ssd_d",
        "ssd_norm", "ssd_w_out", "moe_wg", "moe_bg", "moe_we", "moe_be", "moe_w1", "moe_w3", "moe_w2"]
_OUTS = [("y_prompt", (1, 128, 1024)), ("y_sample", (1, 256, 1024)), ("new_a_k", (1, 1, 128, 2, 64)),
         ("new_a_v", (1, 1, 128, 2, 64)), ("new_b_ckv", (1, 1, 128, 128)), ("new_b_krope", (1, 1, 128, 32)),
         ("new_state_fwd", (1, 1, 32, 64, 128)), ("new_state_bwd", (1, 1, 32, 64, 128))]


def kernel(**inputs):
    import concourse.bacc as _bacc
    from concourse.bass_utils import run_bass_kernel_spmd as _run

    nc = _bacc.Bacc("TRN2", target_bir_lowering=False, num_devices=1)
    arrays, ins, outs = {}, {}, {}
    given = {name: inputs[name] for name in _INS}
    given["consts"] = const_table()[0]
    for name, value in given.items():
        a = np.ascontiguousarray(value)
        arrays[f"in_{name}_dram"] = a
        ins[name] = nc.dram_tensor(f"in_{name}_dram", a.shape, mybir.dt.from_np(a.dtype), kind="ExternalInput").ap()
    for name, shape in _OUTS:
        outs[name] = nc.dram_tensor(f"out_{name}_dram", shape, F32, kind="ExternalOutput").ap()
    build(nc, ins, outs)
    r = _run(nc, [arrays], core_ids=[0])
    return tuple(r.results[0][f"out_{name}_dram"] for name, _ in _OUTS)
```

```python
from contextlib import ExitStack

import numpy as np
import concourse.bass as bass
from concourse import mybir

P = 128
D = 1024
KD = D // P
T = 3
NTOK = T * P
F32 = mybir.dt.float32
I32 = mybir.dt.int32
F32R = mybir.dt.float32r
BF16 = mybir.dt.bfloat16
ALU = mybir.AluOpType
ACT = mybir.ActivationFunctionType
AX = mybir.AxisListType
EPS = 1e-6
BIG = 1e30
BANK = 512

HD_A, HD_B, NOPE, ROPE, V_B = 64, 96, 64, 32, 64
IN_ATT = 1184
H_C, P_C, G_C, N_C, D_INNER = 32, 64, 8, 128, 2048
CONV_CH = 4096
R_C = H_C // G_C
NE, NG, PER, FE = 32, 4, 8, 256
SLOTS = 64
PAIRS = NE // 2
ROUNDS = NTOK // SLOTS

SLOT_RING = 4
MIX, FFN = 0, 1


def const_table():
    i = np.arange(P)
    low = (i[None, :] <= i[:, None])
    high = (i[None, :] >= i[:, None])
    cols, at = [], {}

    def put(name, a):
        a = np.broadcast_to(np.asarray(a, np.float32), (P, a.shape[1]))
        at[name] = (sum(c.shape[1] for c in cols), a.shape[1])
        cols.append(a)

    put("ident", np.eye(P))
    put("ones", np.ones((P, P)))
    put("upto", high)
    put("from_", low)
    put("before", i[None, :] > i[:, None])
    put("mask_high", np.where(high, 0.0, -BIG))
    put("mask_low", np.where(low, 0.0, -BIG))
    put("slot_no", np.arange(SLOTS)[None, :])
    put("rank32", np.arange(NE, 0, -1)[None, :])
    put("rank4", np.arange(NG, 0, -1)[None, :])
    pick = np.zeros((P, 2 * P), np.float32)
    pick[[0, 32], 0:P] = 1
    pick[[1, 33], P:] = 1
    put("pick", pick)
    put("sum4", np.stack([(i % 32 == g) for g in range(2)], axis=1))
    tok = np.arange(2 * P)
    for name, rot in (("a", HD_A), ("b", ROPE)):
        quarter = rot // 4
        inv = np.float32(10000.0) ** (-np.arange(quarter, dtype=np.float32) / np.float32(quarter))
        ar = (tok // 64).astype(np.float32)[:, None] * inv[None, :]
        ac = (tok % 64).astype(np.float32)[:, None] * inv[None, :]
        ang = np.concatenate([ar, ar, ac, ac], axis=1).astype(np.float32)
        sign = np.repeat(np.array([-1, 1, -1, 1], np.float32), quarter)
        cos, sin = np.cos(ang), np.sin(ang) * sign[None, :]
        put("cos_" + name, cos.reshape(2, P, rot).transpose(1, 0, 2).reshape(P, 2 * rot))
        put("sin_" + name, sin.reshape(2, P, rot).transpose(1, 0, 2).reshape(P, 2 * rot))
    return np.ascontiguousarray(np.concatenate(cols, axis=1)), at


class Shared:
    pass


FIRST_MOD = 4
GATE_MOD = [(l, j) for l in range(2) for j in (4, 5, 10, 11)]
SHIFT_MOD = [(0, j) for j in (6, 7, 8, 9)] + [(1, j) for j in (0, 1, 2, 3, 6, 7, 8, 9)]


def stream_plan(w):
    plan, at = [], {}

    def add(stage, key, *moves):
        at[stage, key] = len(plan)
        plan.append(moves)

    def cols(a, c0, n, k0=0):
        return (lambda slot: slot[:, :, 0:n] if n == BANK else slot[:, :, 0:n],
                a[:, k0:k0 + KD, c0:c0 + n])

    def ada(l, j):
        add(("ada", l), j, cols(w["ada_w"][l].rearrange("(p k) n -> p k n", k=KD), j * BANK, BANK))

    for l in range(2):
        if l == 0:
            for j in range(FIRST_MOD):
                ada(0, j)
            win = w["att_w_in"][0].rearrange("(p k) n -> p k n", k=KD)
            for j, n in enumerate((512, 512, 160)):
                add("att_in", j, cols(win, j * BANK, n))
            for later in GATE_MOD[:2]:
                ada(*later)
            wuq = w["att_b_wuq"][0].rearrange("(k p) n -> p k n", p=P)
            wukv = w["att_b_wukv"][0]
            add("att_up", 0,
                (lambda s: s.rearrange("p k n -> p (k n)")[:, 0:1536].rearrange("p (k n) -> p k n", k=2), wuq),
                (lambda s: s.rearrange("p k n -> p (k n)")[:, 1536:2560], wukv))
            for later in GATE_MOD[2:] + SHIFT_MOD:
                ada(*later)
            wout = w["att_w_out"][0].rearrange("(p k) n -> p k n", k=KD)
            for j in range(2):
                add("att_out", j, cols(wout, j * BANK, BANK))
        else:
            win = w["ssd_w_in"][0].rearrange("(p k) n -> p k n", k=KD)
            add("ssd_dt", 0, cols(win, D_INNER + CONV_CH, 2 * H_C))
            for j in range(8):
                add("ssd_xbc", j, cols(win, D_INNER + j * BANK, BANK))
            for j in range(4):
                add("ssd_z", j, cols(win, j * BANK, BANK))
            wout = w["ssd_w_out"][0].rearrange("(k p) n -> p k n", p=P)
            for j in range(2):
                for kh in range(2):
                    add("ssd_out", (j, kh), cols(wout, j * BANK, BANK, kh * KD))
        at["moe", l] = len(plan)
        for e in range(SLOT_RING):
            plan.append(tuple((lambda slot, c=c: slot[:, :, c:c + FE], w[name][l, e].rearrange("(p k) f -> p k f", k=KD))
                              for name, c in (("moe_w1", 0), ("moe_w3", FE))))
        plan.extend([None] * (NE - SLOT_RING))
    return plan, at


def build(nc, w, out):
    ctx = ExitStack()
    s = Shared()
    with ctx:
        def sb(name, shape, dt=F32):
            return ctx.enter_context(nc.sbuf_tensor(name, shape, dt))

        def sem(name):
            return ctx.enter_context(nc.semaphore(name))

        s.nc, s.w, s.out = nc, w, out
        s.ps = ctx.enter_context(nc.psum_tensor("ps", [P, 8, BANK], F32))
        s.y = sb("y", [P, T, D])
        s.hT, s.hT_r = with_f32r_view(nc, sb, "hT", [P, KD, NTOK])
        s.ring, s.ring_r = with_f32r_view(nc, sb, "ring", [P, SLOT_RING, KD, BANK])
        s.gates = sb("gates", [34, 2, D])
        s.shift = sb("shift", [P, 2, 2, KD, 2])
        s.gain = sb("gain", [P, 2, 2, KD, 2])
        _, s.cat = const_table()
        s.consts = sb("consts", [P, w["consts"].shape[1]])
        s.cid = lambda name: s.consts[:, s.cat[name][0]:s.cat[name][0] + s.cat[name][1]]
        s.ident = s.cid("ident")
        s.ring_full = [sem(f"ring_full{n}") for n in range(SLOT_RING)]
        s.ring_free = sem("ring_free")
        s.plan, s.at = stream_plan(w)
        s.slot_of = ring_slots(s)
        s.fill_of = fill_counts(s)
        s.issued = 0
        s.loads = sem("loads")
        s.loaded = 0
        s.stores = sem("stores")
        s.stored = 0
        s.chain = {e: sem(f"chain_{e}") for e in ("dve", "act")}
        s.chained = {"dve": 0, "act": 0}

        for l in range(2):
            layer = ctx.enter_context(ExitStack())
            own = []

            def layer_sem(name, layer=layer, own=own):
                own.append(layer.enter_context(nc.semaphore(name)))
                return own[-1]

            s.sem = layer_sem
            if l == 0:
                with ExitStack() as ada:
                    s.silu_c = ada.enter_context(nc.sbuf_tensor("silu_c", [P, KD, 32], F32))
                    with ExitStack() as st:
                        ada_stage(s, st)
                    with ExitStack() as st:
                        norm_stage(s, l, MIX, st)
                    with ExitStack() as st:
                        attention(s, st)
            else:
                with ExitStack() as st:
                    norm_stage(s, l, MIX, st)
                with ExitStack() as st:
                    ssd(s, st)
            with ExitStack() as st:
                moe(s, l, st)
            if l == 0:
                with nc.Block() as block:
                    @block.gpsimd
                    def _(pool):
                        for one in own:
                            pool.sem_clear(one)
                layer.close()


def with_f32r_view(nc, sb, name, shape):
    at = nc.sbuf_base
    tensor = sb(name, shape)
    return tensor, nc.alloc_sbuf_tensor_at(name + "_r", shape, F32R, offset=at)


def narrow_matmul(pe, dst, lhs, rhs, start, stop):
    for q in (slice(0, 64), slice(64, 128)):
        mm = pe.matmul(dst[q], lhs[:, q], rhs, start=start, stop=stop)
    return mm


def link(s, name, eng, ins):
    s.chained[name] += 1
    ins.then_inc(s.chain[name], 1)
    eng.wait_ge(s.chain[name], s.chained[name])


def ring_loads(s, sp, upto):
    while s.issued < min(upto, len(s.plan)):
        n = s.issued
        if s.plan[n] is None:
            break
        if n >= SLOT_RING:
            sp.wait_ge(s.ring_free, n - SLOT_RING + 1)
        slot = s.ring[:, s.slot_of[n]]
        for part, src in s.plan[n]:
            sp.dma_start(part(slot), src).then_inc(s.ring_full[s.slot_of[n]], 16)
        s.issued += 1


def ring_slots(s):
    done = list(range(len(s.plan)))
    dt0, z0 = s.at["ssd_dt", 0], s.at["ssd_z", 0]
    done.remove(dt0)
    done.insert(z0 + 3, dt0)
    slots = list(range(SLOT_RING))
    for n in range(SLOT_RING, len(s.plan)):
        slots.append(slots[done[n - SLOT_RING]])
    return slots


class SplitWeights:

    def __init__(self, s, sb, pre, deep, shape, pieces):
        self.s, self.deep, self.pieces = s, deep, pieces
        self.buf = sb("w_hi", [P, deep] + shape, F32R)
        self.hi_ready, self.lo_ready, self.used = (s.sem(pre + n) for n in ("w_hi", "w_lo", "w_used"))

    def hi(self, i):
        return self.buf[:, i % self.deep]

    def lo(self, i):
        n, part = self.pieces[i]
        return part(self.s.ring_r[:, self.s.slot_of[n]])

    def piece(self, i):
        n, part = self.pieces[i]
        return part(self.s.ring[:, self.s.slot_of[n]])

    def make_hi(self, act, i):
        ring_wait(self.s, act, self.pieces[i][0])
        if i >= self.deep:
            act.wait_ge(self.used, i - self.deep + 1)
        self.s.nc.scalar.copy(self.hi(i), self.piece(i)).then_inc(self.hi_ready, 1)

    def make_lo(self, eng, ops, i):
        eng.wait_ge(self.hi_ready, i + 1)
        ops.tensor_tensor(self.lo(i), self.piece(i), self.hi(i).bitcast(F32), ALU.subtract).then_inc(self.lo_ready, 1)

    def free(self, pe, i):
        if i >= 0 and (i + 1 == len(self.pieces) or self.pieces[i + 1][0] != self.pieces[i][0]):
            pe.wait_ge(self.used, i + 1)
            pe.sem_inc(self.s.ring_free, 1)


def split_passes(pe, dst, lhs, rhs, start, stop):
    for a, b in ((0, 0), (0, 1), (1, 0)):
        mm = pe.matmul(dst, lhs[a], rhs[b], start=start and (a, b) == (0, 0), stop=stop and (a, b) == (1, 0))
    return mm


def fill_counts(s):
    total, out = [0] * SLOT_RING, []
    for n, moves in enumerate(s.plan):
        total[s.slot_of[n]] += 16 * (2 if moves is None else len(moves))
        out.append(total[s.slot_of[n]])
    return out


def ring_wait(s, pe, n):
    pe.wait_ge(s.ring_full[s.slot_of[n]], s.fill_of[n])


def stage_buffers(s, st, prefix):
    def sb(name, shape, dt=F32):
        return st.enter_context(s.nc.sbuf_tensor(prefix + name, shape, dt))
    return sb


def ada_stage(s, st):
    nc, w, ps = s.nc, s.w, s.ps
    l = 0
    sb = stage_buffers(s, st, f"ada{l}_")
    cond = sb("cond", [P, 2, KD])
    silu_c = s.silu_c
    part = sb("part", [P, 2, BANK])
    bias = sb("bias", [2, FIRST_MOD * BANK])
    row = sb("row", [2, FIRST_MOD * BANK])
    norm_g = sb("norm_g", [P, KD])
    mod_t = sb("mod_t", [P, 2, KD, 2])
    silu_ready, col_ps, col_done, t_ps = (s.sem(f"ada{l}_{x}") for x in ("silu", "col_ps", "col_done", "t_ps"))
    zero, part_ev, sum_ps = (s.sem(f"ada{l}_{x}") for x in ("zero", "part_ev", "sum_ps"))
    base = s.at[("ada", l), 0]
    block = st.enter_context(nc.Block())

    @block.sync
    def _(sp):
        n = 0
        loads = [(cond[:, 0, :], w["c_ctx"].rearrange("(p k) -> p k", k=KD)),
                 (cond[:, 1, :], w["c"][0].rearrange("(p k) -> p k", k=KD)),
                 (norm_g[:, :], w["norm_mix"][l].rearrange("(p k) -> p k", k=KD)),
                 (bias[0:1, :], w["ada_b"][l:l + 1, 0:FIRST_MOD * BANK]),
                 (bias[1:2, :], w["ada_b"][l:l + 1, 0:FIRST_MOD * BANK]),
                 (s.consts[:, :], w["consts"]),
                 (s.y[:, 0, :], w["x_prompt"][0]),
                 (s.y[:, 1:3, :], w["x_sample"][0].rearrange("(t p) d -> p t d", p=P))]
        for dst, src in loads:
            sp.dma_start(dst, src).then_inc(s.loads, 16)
            n += 16
        s.loaded += n
        ring_loads(s, sp, base + FIRST_MOD + SLOT_RING)

    @block.scalar
    def _(act):
        act.wait_ge(zero, 1)
        act.wait_ge(s.loads, s.loaded)
        nc.scalar.activation(silu_c[:, :, 0:2].rearrange("p k g -> p g k"), cond[:, :, :], ACT.Silu).then_inc(silu_ready, 1)
        for j in range(FIRST_MOD):
            act.wait_ge(s.ring_free, base + j + 1)
            if j >= 2:
                act.wait_ge(sum_ps, j - 1)
            nc.scalar.copy(part[:, j % 2, :], ps[:, j % 2, :]).then_inc(part_ev, 1)

    @block.tensor
    def _(pe):
        pe.wait_ge(silu_ready, 1)

        def add_up(j):
            pe.wait_ge(part_ev, j + 1)
            if j >= 2:
                pe.wait_ge(col_done, j - 1)
            pe.matmul(ps[0:2, 3 + j % 2, :], s.cid("sum4"), part[:, j % 2, :], start=True, stop=True).then_inc(sum_ps, 1)

        for j in range(FIRST_MOD):
            ring_wait(s, pe, base + j)
            if j >= 2:
                pe.wait_ge(part_ev, j - 1)
            for k in range(KD):
                c = 32 * (k % 4)
                mm = pe.matmul(ps[c:c + 32, j % 2, :], silu_c[:, k, :], s.ring[:, s.slot_of[base + j], k, :],
                               start=(k < 4), stop=(k >= 4))
            mm.then_inc(s.ring_free, 1)
            if j:
                add_up(j - 1)
        add_up(FIRST_MOD - 1)
        pe.wait_ge(col_done, FIRST_MOD)
        pe.wait_ge(s.loads, s.loaded)
        for q in range(2):
            for k in range(KD):
                c = (q * KD + k) * 2
                mm = pe.transpose(ps[:, 2, c:c + 2], row[0:2, q * D + k:(q + 1) * D:KD], s.ident[0:2, 0:2])
        mm.then_inc(t_ps, 1)

    @block.vector
    def _(dve):
        nc.vector.memset(silu_c[:, :, :], 0.0).then_inc(zero, 1)
        dve.wait_ge(s.loads, s.loaded)
        for j in range(FIRST_MOD):
            dve.wait_ge(sum_ps, j + 1)
            dst = row[:, j * BANK:(j + 1) * BANK]
            nc.vector.tensor_tensor(dst, ps[0:2, 3 + j % 2, :], bias[:, j * BANK:(j + 1) * BANK], ALU.add).then_inc(col_done, 1)
        dve.wait_ge(t_ps, 1)
        link(s, "dve", dve, nc.vector.tensor_copy(mod_t[:, :, :, :].rearrange("p q k g -> p (q k g)"), ps[:, 2, 0:2 * KD * 2]))
        shift_and_gain(s, dve, l, MIX, mod_t, norm_g[:, :])


def shift_and_gain(s, dve, l, m, mod_t, norm_g):
    link(s, "dve", dve, s.nc.vector.tensor_copy(s.shift[:, l, m, :, :], mod_t[:, 0, :, :]))
    link(s, "dve", dve, s.nc.vector.scalar_tensor_tensor(
        out=s.gain[:, l, m, :, :], in0=mod_t[:, 1, :, :], scalar=1.0, in1=norm_g.unsqueeze(2).broadcast_to([P, KD, 2]),
        op0=ALU.add, op1=ALU.mult))


class LaterModulation:

    NORMS = ((0, FFN), (1, MIX), (1, FFN))

    def __init__(self, s, pre, chunks, bank, part):
        self.s, self.chunks, self.bank, self.part = s, chunks, bank, part
        self.part_ps, self.part_ev, self.sum_ps, self.sum_ev = (
            s.sem(pre + n) for n in ("part_ps", "part_ev", "sum_ps", "sum_ev"))

    def with_rows(self, sb):
        self.row = sb("mod_row", [34, 4, D])
        self.norm_g = sb("mod_norm_g", [P, 3, KD])
        self.mod_t = sb("mod_t", [P, 3, 2, KD, 2])
        self.t_ps = self.s.sem("mod_t_ps")
        return self

    def bias(self, l):
        return self.s.w["ada_b"][l:l + 1, :].rearrange("o (q d) -> o q d", q=6)

    def gate_loads(self):
        return [(self.s.gates[32 * l + g:32 * l + g + 1, m, :], self.bias(l)[:, 3 * m + 2, :])
                for l in range(2) for g in range(2) for m in range(2)]

    def row_loads(self):
        s, w = self.s, self.s.w
        out = [(self.norm_g[:, i, :], w["norm_mix" if m == MIX else "norm_ffn"][l].rearrange("(p k) -> p k", k=KD))
               for i, (l, m) in enumerate(self.NORMS)]
        for l, m in self.NORMS:
            for r in (32 * l, 32 * l + 1):
                out.append((self.row[r:r + 1, 2 * m:2 * m + 2, :], self.bias(l)[:, 3 * m:3 * m + 2, :]))
        return out

    def products(self, pe, i):
        s = self.s
        n = s.at[("ada", self.chunks[i][0]), self.chunks[i][1]]
        ring_wait(s, pe, n)
        if i:
            pe.wait_ge(self.sum_ev, i)
        for k in range(KD):
            c = 32 * (k % 4)
            mm = pe.matmul(s.ps[c:c + 32, self.bank, :], s.silu_c[:, k, :], s.ring[:, s.slot_of[n], k, :], start=(k < 4), stop=(k >= 4))
        mm.then_inc(self.part_ps, 1)

    def take_part_act(self, act, i):
        act.wait_ge(self.part_ps, i + 1)
        self.s.nc.scalar.copy(self.part, self.s.ps[:, self.bank, :]).then_inc(self.part_ev, 1)

    def take_part(self, dve, i):
        dve.wait_ge(self.part_ps, i + 1)
        self.s.nc.vector.tensor_copy(self.part, self.s.ps[:, self.bank, :]).then_inc(self.part_ev, 1)

    def sum(self, pe, i):
        r = 32 * self.chunks[i][0]
        pe.wait_ge(self.part_ev, i + 1)
        pe.sem_inc(self.s.ring_free, 1)
        pe.matmul(self.s.ps[r:r + 2, self.bank, :], self.s.cid("sum4"), self.part, start=True, stop=True).then_inc(self.sum_ps, 1)

    def add_bias(self, dve, i):
        l, j = self.chunks[i]
        q, c = divmod(j, 2)
        rows = slice(32 * l, 32 * l + 2)
        row = self.s.gates[rows, q // 3, :] if q in (2, 5) else self.row[rows, q - q // 3, :]
        dst = row[:, BANK * c:BANK * (c + 1)]
        dve.wait_ge(self.sum_ps, i + 1)
        self.s.nc.vector.tensor_tensor(dst, self.s.ps[rows, self.bank, :], dst, ALU.add).then_inc(self.sum_ev, 1)

    def turn(self, pe):
        pe.wait_ge(self.sum_ev, len(self.chunks))
        for i, (l, m) in enumerate(self.NORMS):
            rows = slice(32 * l, 32 * l + 2)
            for q in range(2):
                for k in range(KD):
                    c = ((2 * i + q) * KD + k) * 2
                    mm = pe.transpose(self.s.ps[:, 6 + l, c:c + 2], self.row[rows, 2 * m + q, k::KD], self.s.ident[rows, rows])
        mm.then_inc(self.t_ps, 1)

    def take_turned(self, dve):
        dve.wait_ge(self.t_ps, 1)
        n = 2 * KD * 2
        for i, (l, m) in enumerate(self.NORMS):
            link(self.s, "dve", dve, self.s.nc.vector.tensor_copy(self.mod_t[:, i].rearrange("p q k g -> p (q k g)"),
                                                                  self.s.ps[:, 6 + l, i * n:(i + 1) * n]))
        for i, (l, m) in enumerate(self.NORMS):
            shift_and_gain(self.s, dve, l, m, self.mod_t[:, i], self.norm_g[:, i, :])


def rsqrt_act(s, act, x, r0, x_ready, x_count, r0_ready):
    act.wait_ge(x_ready, x_count)
    link(s, "act", act, s.nc.scalar.activation(r0, x, ACT.Ln))
    s.nc.scalar.activation(r0, r0, ACT.Exp, scale=-0.5).then_inc(r0_ready, 1)


def rsqrt_dve(s, dve, x, r0, tmp, r0_ready, count):
    v = s.nc.vector
    dve.wait_ge(r0_ready, count)
    link(s, "dve", dve, v.tensor_tensor(tmp, r0, r0, ALU.mult))
    link(s, "dve", dve, v.tensor_tensor(tmp, tmp, x, ALU.mult))
    link(s, "dve", dve, v.tensor_scalar(tmp, tmp, -0.5, 1.5, ALU.mult, ALU.add))
    link(s, "dve", dve, v.tensor_tensor(r0, r0, tmp, ALU.mult))


def norm_stage(s, l, m, st, hp=None, loads=()):
    nc, ps = s.nc, s.ps
    pre = f"n{l}{m}_"
    sb = stage_buffers(s, st, pre)
    sq = sb("sq", [P, D])
    ss = sb("ss", [P, T])
    x = sb("x", [P, T])
    r = sb("r", [P, T])
    tmp = sb("tmp", [P, T])
    hn = sb("hn", [P, T, KD, P])
    s.loaded += 16 * len(loads)
    ss_ready, x_ready, r_ready, hn_ready, t_ps, ev_a, ev_d, b_ps, hi_ev = (
        s.sem(pre + n) for n in ("ss", "x", "r", "hn", "t_ps", "ev_a", "ev_d", "b_ps", "hi_ev"))
    block = st.enter_context(nc.Block())

    @block.sync
    def _(sp):
        for dst, src in loads:
            sp.dma_start(dst, src).then_inc(s.loads, 16)

    @block.scalar
    def _(act):
        for t in range(T):
            if t:
                act.wait_ge(ss_ready, t)
            nc.scalar.activation(sq[:, :], s.y[:, t, :], ACT.Square, accum_out=ss[:, t:t + 1]).then_inc(ss_ready, 1)
        rsqrt_act(s, act, x[:, :], r[:, :], x_ready, 1, r_ready)
        for t in range(T):
            act.wait_ge(t_ps, t + 1)
            for k in range(4, KD):
                nc.scalar.activation(s.hT[:, k, t * P:(t + 1) * P], ps[:, 2 * t + 1, (k - 4) * P:(k - 3) * P], ACT.Identity,
                                     scale=s.gain[:, l, m, k, min(t, 1):min(t, 1) + 1],
                                     bias=s.shift[:, l, m, k, min(t, 1):min(t, 1) + 1]).then_inc(ev_a, 1)
        if hp is not None:
            for t in range(T):
                act.wait_ge(b_ps, t + 1)
                nc.scalar.copy(hp[0][:, t, :, :].rearrange("n k p -> n (k p)"),
                               ps[:, 2 * t:2 * t + 2, :].rearrange("n b c -> n (b c)")).then_inc(hi_ev, 1)

    @block.vector
    def _(dve):
        dve.wait_ge(ss_ready, T)
        nc.vector.tensor_scalar(x[:, :], ss[:, :], 1.0 / D, EPS, ALU.mult, ALU.add).then_inc(x_ready, 1)
        rsqrt_dve(s, dve, x[:, :], r[:, :], tmp[:, :], r_ready, 1)
        for t in range(T):
            nc.vector.tensor_scalar(hn[:, t, :, :], s.y[:, t, :].rearrange("n (p k) -> n k p", k=KD),
                                    r[:, t:t + 1], None, ALU.mult).then_inc(hn_ready, 1)
        for t in range(T):
            dve.wait_ge(t_ps, t + 1)
            for k in range(4):
                g = min(t, 1)
                nc.vector.tensor_scalar(s.hT[:, k, t * P:(t + 1) * P], ps[:, 2 * t, k * P:(k + 1) * P],
                                        s.gain[:, l, m, k, g:g + 1], s.shift[:, l, m, k, g:g + 1],
                                        ALU.mult, ALU.add).then_inc(ev_d, 1)
        if hp is not None:
            for t in range(T):
                dve.wait_ge(hi_ev, t + 1)
                nc.vector.tensor_tensor(hp[1][:, t, :, :].rearrange("n k p -> n (k p)"),
                                        ps[:, 2 * t:2 * t + 2, :].rearrange("n b c -> n (b c)"),
                                        hp[0][:, t, :, :].rearrange("n k p -> n (k p)").bitcast(F32), ALU.subtract)

    @block.tensor
    def _(pe):
        for t in range(T):
            pe.wait_ge(hn_ready, t + 1)
            for k in range(KD):
                mm = pe.transpose(ps[:, 2 * t + k // 4, (k % 4) * P:(k % 4 + 1) * P], hn[:, t, k, :], s.ident)
            mm.then_inc(t_ps, 1)
        if hp is not None:
            for t in range(T):
                pe.wait_ge(ev_a, 4 * (t + 1))
                pe.wait_ge(ev_d, 4 * (t + 1))
                for k in range(KD):
                    mm = pe.transpose(ps[:, 2 * t + k // 4, (k % 4) * P:(k % 4 + 1) * P],
                                      s.hT[:, k, t * P:(t + 1) * P], s.ident)
                mm.then_inc(b_ps, 1)


NTB = 7


def attention(s, st):
    att_tiles = ExitStack()
    sb = stage_buffers(s, st, "att_")
    qk_t = sb("qk_t", [P, T, 4, P])
    k_t = sb("k_t", [P, 2, 4, P])
    v_a = sb("v_a", [P, 4, P])
    qkb_t = sb("qkb_t", [HD_B, 8, NTB, P])
    v_b = sb("v_b", [P, 4, 8, V_B])
    small = sb("small", [P, 8])
    with att_tiles:
        att_project(s, att_tiles, qk_t, k_t, v_a, qkb_t, v_b, small)
    with ExitStack() as st2:
        att_scores(s, st2, qk_t, k_t, v_a, qkb_t, v_b, small)


def att_project(s, st, qk_t, k_t, v_a, qkb_t, v_b, sink):
    nc, w, ps, out = s.nc, s.w, s.ps, s.out
    sb = stage_buffers(s, st, "prj_")
    proj = sb("proj", [P, T, IN_ATT])
    heads = sb("heads", [P, T, 10, 64])
    cache_k = sb("cache_k", [P, P])
    cache_c = sb("cache_c", [P, P])
    cache_r = sb("cache_r", [P, ROPE])
    q_gain, k_gain = sb("q_gain", [P, 64]), sb("k_gain", [P, 64])
    qa_gain, kva_gain = sb("qa_gain", [P, 256]), sb("kva_gain", [P, P])
    b_gain = sb("b_gain", [P, 2, HD_B])
    lat_t = sb("lat_t", [P, 2, NTOK])
    ckv_t = sb("ckv_t", [P, 4 * P])
    qkb = sb("qkb", [P, NTB, 8, HD_B])
    ss = sb("ss", [P, T, 12])
    x, r, tmp = sb("x", [P, T * 12]), sb("r", [P, T * 12]), sb("tmp", [P, T * 12])
    ssb = sb("ssb", [P, NTB * 8])
    junk = sb("junk", [P, 256])
    xb, rb, tmpb = sb("xb", [P, NTB * 8]), sb("rb", [P, NTB * 8]), sb("tmpb", [P, NTB * 8])
    sq = s.hT[:, :, :].rearrange("p k n -> p (k n)")
    mod = LaterModulation(s, "prj_mod_", GATE_MOD, 3, sq[:, 2048:2048 + BANK])
    names = ("in_ps", "in_a", "in_d", "norm_x", "norm_r", "heads_ready", "lat_ready", "ta_ps", "ta_ev",
             "tl_ps", "tl_ev", "up_ps", "up_a", "up_d", "b_x", "b_r", "b_ready", "tb_ps", "tb_ev", "zero",
             "ss", "ssb", "scaled", "refined")
    S = {n: s.sem("prj_" + n) for n in names}
    in0, up0 = s.at["att_in", 0], s.at["att_up", 0]
    widths = (512, 512, 160)
    slot = [s.ring[:, s.slot_of[in0 + j]] for j in range(3)]
    up = s.ring[:, s.slot_of[up0]].rearrange("p k n -> p (k n)")
    wuq = up[:, 0:1536].rearrange("p (k n) -> p k n", k=2)
    wukv = up[:, 1536:2560]
    block = st.enter_context(nc.Block())

    @block.sync
    def _(sp):
        loads = [(cache_k[:, :], w["cache_a_k"][0, 0].rearrange("n h d -> n (h d)")),
                 (v_a[:, 3, :], w["cache_a_v"][0, 0].rearrange("n h d -> n (h d)")),
                 (cache_c[:, :], w["cache_b_ckv"][0, 0]),
                 (cache_r[:, :], w["cache_b_krope"][0, 0]),
                 (q_gain[:, :], w["att_a_qnorm"][0].partition_broadcast(P)),
                 (k_gain[:, :], w["att_a_knorm"][0].partition_broadcast(P)),
                 (qa_gain[:, :], w["att_b_qa_norm"][0].partition_broadcast(P)),
                 (kva_gain[:, :], w["att_b_kva_norm"][0].partition_broadcast(P)),
                 (b_gain[:, 0, :], w["att_b_qnorm"][0].partition_broadcast(P)),
                 (b_gain[:, 1, :], w["att_b_knorm"][0].partition_broadcast(P)),
                 (sink[:, :], w["att_a_sink"][0].partition_broadcast(P))] + mod.gate_loads()
        for dst, src in loads:
            sp.dma_start(dst, src).then_inc(s.loads, 16)
        s.loaded += 16 * len(loads)
        ring_loads(s, sp, s.at[("ada", 1), GATE_MOD[-1][1]] + 1 + SLOT_RING)
        sp.wait_ge(S["in_a"], 5)
        sp.wait_ge(S["in_d"], 4)
        sp.dma_start(out["new_a_v"][0, 0].rearrange("n h d -> n (h d)"), proj[:, 0, 640:768]).then_inc(s.stores, 16)
        sp.dma_start(out["new_b_krope"][0, 0], proj[:, 0, 1152:1184]).then_inc(s.stores, 16)
        sp.wait_ge(S["heads_ready"], 1)
        sp.dma_start(out["new_a_k"][0, 0], heads[:, 0, 8:10, :]).then_inc(s.stores, 16)
        sp.wait_ge(S["lat_ready"], 1)
        sp.dma_start(out["new_b_ckv"][0, 0], proj[:, 0, 1024:1152]).then_inc(s.stores, 16)
        s.stored += 64
        sp.wait_ge(s.stores, s.stored)

    units = [(c, t) for c in range(3) for t in range(T)]

    def in_bank(n):
        return (0, 1, 2, 4, 5, 6, 7)[n % 7]

    @block.tensor
    def _(pe):
        for n, (c, t) in enumerate(units):
            if t == 0:
                ring_wait(s, pe, in0 + c)
            if n >= 7:
                pe.wait_ge(S["in_a"] if n % 2 else S["in_d"], (n - 7) // 2 + 1)
            for k in range(KD):
                mm = pe.matmul(ps[:, in_bank(n), 0:widths[c]], s.hT[:, k, t * P:(t + 1) * P], slot[c][:, k, 0:widths[c]],
                               start=(k == 0), stop=(k == KD - 1))
            mm.then_inc(S["in_ps"], 1)
            if t == T - 1:
                pe.wait_ge(S["in_ps"], n + 1)
                pe.sem_inc(s.ring_free, 1)
        for i in range(2):
            mod.products(pe, i)
            mod.sum(pe, i)
        pe.wait_ge(S["in_a"], 5)
        pe.wait_ge(S["in_d"], 4)
        pe.wait_ge(S["lat_ready"], 1)
        pe.wait_ge(s.loads, s.loaded)
        for t in range(T):
            for c in range(2):
                mm = pe.transpose(ps[:, c, t * P:(t + 1) * P], proj[:, t, 768 + c * P:768 + (c + 1) * P], s.ident)
            mm = pe.transpose(ps[:, 2, t * P:(t + 1) * P], proj[:, t, 1024:1152], s.ident)
        mm = pe.transpose(ps[:, 2, 3 * P:4 * P], cache_c[:, :], s.ident)
        mm.then_inc(S["tl_ps"], 1)
        pe.wait_ge(S["tl_ev"], 1)
        ring_wait(s, pe, up0)
        for n in range(NTB):
            b = 4 + 2 * (n % 2)
            if n >= 2:
                pe.wait_ge(S["up_d"], n - 1)
            if n < T:
                for h in range(2):
                    for k in range(2):
                        mm = pe.matmul(ps[:, b + h, 0:384], lat_t[:, k, n * P:(n + 1) * P], wuq[:, k, h * 384:(h + 1) * 384],
                                       start=(k == 0), stop=(k == 1))
            else:
                for h in range(2):
                    mm = pe.matmul(ps[:, b + h, :], ckv_t[:, (n - T) * P:(n - T + 1) * P], wukv[:, h * BANK:(h + 1) * BANK],
                                   start=True, stop=True)
            mm.then_inc(S["up_ps"], 1)
        pe.wait_ge(S["up_ps"], NTB)
        pe.sem_inc(s.ring_free, 1)
        for i in (2, 3):
            mod.products(pe, i)
            mod.sum(pe, i)
        pe.wait_ge(S["heads_ready"], 2)
        pe.wait_ge(S["up_d"], NTB)
        for t in range(T):
            for j in range(4):
                pe.transpose(ps[:, t, j * P:(j + 1) * P], heads[:, t, 2 * j:2 * j + 2, :].rearrange("n a d -> n (a d)"), s.ident)
            mm = pe.transpose(ps[:, 4, t * P:(t + 1) * P], heads[:, t, 8:10, :].rearrange("n a d -> n (a d)"), s.ident)
        mm = pe.transpose(ps[:, 4, 3 * P:4 * P], cache_k[:, :], s.ident)
        mm.then_inc(S["ta_ps"], 1)
        for i in range(4, len(GATE_MOD)):
            mod.products(pe, i)
            mod.sum(pe, i)
        pe.wait_ge(S["ta_ev"], 3)
        for n in range(NTB):
            b = 4 + 2 * (n % 2)
            if n >= 2:
                pe.wait_ge(S["tb_ev"], n - 1)
            if n == 0:
                pe.wait_ge(S["b_ready"], 1)
            for h in range(8):
                mm = pe.transpose(ps[0:HD_B, b + h // 4, (h % 4) * P:(h % 4 + 1) * P], qkb[:, n, h, :], s.ident)
            mm.then_inc(S["tb_ps"], 1)

    SEGMENTS = [(64 * h, 64) for h in range(10)] + [(768, 256), (1024, P)]

    def square_sum(src, dst):
        return nc.scalar.activation(junk[:, 0:src.shape[-1]], src, ACT.Square, accum_out=dst)

    @block.scalar
    def _(act):
        for n, (c, t) in enumerate(units):
            if n % 2 == 0:
                act.wait_ge(S["in_ps"], n + 1)
                nc.scalar.copy(proj[:, t, c * BANK:c * BANK + widths[c]], ps[:, in_bank(n), 0:widths[c]]).then_inc(S["in_a"], 1)
                act.wait_ge(S["in_a"], n // 2 + 1)
            else:
                act.wait_ge(S["in_d"], (n + 1) // 2)
            for h, (c0, width) in enumerate(SEGMENTS):
                if c0 // BANK == c:
                    ins = square_sum(proj[:, t, c0:c0 + width], ss[:, t, h:h + 1])
                    if n < len(units) - 1:
                        link(s, "act", act, ins)
                    else:
                        ins.then_inc(S["ss"], 1)
        rsqrt_act(s, act, x[:, :], r[:, :], S["norm_x"], 1, S["norm_r"])
        for i in range(2):
            mod.take_part_act(act, i)
        act.wait_ge(S["tl_ps"], 1)
        link(s, "act", act, nc.scalar.copy(lat_t[:, :, :], ps[:, 0:2, 0:NTOK]))
        nc.scalar.copy(ckv_t[:, :], ps[:, 2, :]).then_inc(S["tl_ev"], 1)
        for n in range(T, NTB):
            act.wait_ge(S["up_d"], n + 1)
            for h in range(8):
                ins = square_sum(qkb[:, n, h, :], ssb[:, 8 * n + h:8 * n + h + 1])
                if (n, h) != (NTB - 1, 7):
                    link(s, "act", act, ins)
        ins.then_inc(S["ssb"], 1)
        rsqrt_act(s, act, xb[:, :], rb[:, :], S["b_x"], 1, S["b_r"])
        for i in (2, 3):
            mod.take_part_act(act, i)
        act.wait_ge(S["refined"], 1)
        for n in range(T, NTB):
            for h in range(8):
                ins = nc.scalar.activation(qkb[:, n, h, :], qkb[:, n, h, :], ACT.Copy, scale=rb[:, 8 * n + h:8 * n + h + 1])
            ins.then_inc(S["scaled"], 1)
        act.wait_ge(S["ta_ps"], 1)
        nc.scalar.copy(qk_t[:, :, :, :].rearrange("p t j n -> p (t j n)"), ps[:, 0:3, :].rearrange("p b n -> p (b n)")).then_inc(S["ta_ev"], 1)
        act.wait_ge(S["zero"], 1)
        for g in range(2):
            q = slice(64 * g, 64 * g + 64)
            nc.scalar.copy(k_t[q, g, :, :].rearrange("p t n -> p (t n)"), ps[q, 4, :]).then_inc(S["ta_ev"], 1)
        for i in range(4, len(GATE_MOD)):
            mod.take_part_act(act, i)
        for n in range(NTB):
            b = 4 + 2 * (n % 2)
            act.wait_ge(S["tb_ps"], n + 1)
            nc.scalar.copy(qkb_t[:, :, n, :], ps[0:HD_B, b:b + 2, :].rearrange("p b (h n) -> p (b h) n", h=4)).then_inc(S["tb_ev"], 1)

    @block.vector
    def _(dve):
        v = nc.vector
        v.memset(k_t[:, :, :, :], 0.0).then_inc(S["zero"], 1)
        for n, (c, t) in enumerate(units):
            if n % 2 == 1:
                dve.wait_ge(S["in_ps"], n + 1)
                v.tensor_copy(proj[:, t, c * BANK:c * BANK + widths[c]], ps[:, in_bank(n), 0:widths[c]]).then_inc(S["in_d"], 1)
        dve.wait_ge(S["in_a"], 5)
        dve.wait_ge(S["in_d"], 4)
        dve.wait_ge(s.loads, s.loaded)
        dve.wait_ge(S["ss"], 1)
        x3 = x[:, :].rearrange("p (t h) -> p t h", t=T)
        link(s, "dve", dve, v.tensor_scalar(x3[:, :, 0:10], ss[:, :, 0:10], 1.0 / 64, EPS, ALU.mult, ALU.add))
        link(s, "dve", dve, v.tensor_scalar(x3[:, :, 10:11], ss[:, :, 10:11], 1.0 / 256, EPS, ALU.mult, ALU.add))
        v.tensor_scalar(x3[:, :, 11:12], ss[:, :, 11:12], 1.0 / P, EPS, ALU.mult, ALU.add).then_inc(S["norm_x"], 1)
        rsqrt_dve(s, dve, x[:, :], r[:, :], tmp[:, :], S["norm_r"], 1)
        r3 = r[:, :].rearrange("p (t h) -> p t h", t=T)
        for t in range(T):
            link(s, "dve", dve, v.scalar_tensor_tensor(out=proj[:, t, 768:1024], in0=proj[:, t, 768:1024], scalar=r3[:, t, 10:11],
                                                       in1=qa_gain[:, :], op0=ALU.mult, op1=ALU.mult))
            ins = v.scalar_tensor_tensor(out=proj[:, t, 1024:1152], in0=proj[:, t, 1024:1152], scalar=r3[:, t, 11:12],
                                         in1=kva_gain[:, :], op0=ALU.mult, op1=ALU.mult)
        ins.then_inc(S["lat_ready"], 1)
        mod.add_bias(dve, 0)
        for t in range(T):
            q_in = proj[:, t, 0:512].rearrange("p (v j d) -> p j v d", v=2, j=4)
            q_out = heads[:, t, 0:8, :].rearrange("p (j v) d -> p j v d", j=4)
            for kv in range(2):
                rr = r3[:, t, 4 * kv:4 * kv + 4].unsqueeze(2).broadcast_to([P, 4, 64])
                link(s, "dve", dve, v.tensor_tensor(q_out[:, :, kv, :], q_in[:, :, kv, :], rr, ALU.mult))
            rk = r3[:, t, 8:10].unsqueeze(2).broadcast_to([P, 2, 64])
            link(s, "dve", dve, v.tensor_tensor(heads[:, t, 8:10, :], proj[:, t, 512:640].rearrange("p (v d) -> p v d", v=2), rk, ALU.mult))
            link(s, "dve", dve, v.tensor_copy(v_a[:, t, :], proj[:, t, 640:768]))
            link(s, "dve", dve, v.tensor_tensor(heads[:, t, 0:8, :], heads[:, t, 0:8, :], q_gain[:, :].unsqueeze(1).broadcast_to([P, 8, 64]), ALU.mult))
            ins = v.tensor_tensor(heads[:, t, 8:10, :], heads[:, t, 8:10, :], k_gain[:, :].unsqueeze(1).broadcast_to([P, 2, 64]), ALU.mult)
            if t == 0:
                ins.then_inc(S["heads_ready"], 1)
                mod.add_bias(dve, 1)
            else:
                link(s, "dve", dve, ins)
                ins = rope(s, dve, heads[:, t], "a", t - 1, 10, rot_pool(sq, 640))
                if t == T - 1:
                    ins.then_inc(S["heads_ready"], 1)
                else:
                    link(s, "dve", dve, ins)
        dve.wait_ge(S["tl_ps"], 1)
        for n in range(NTB):
            b = 4 + 2 * (n % 2)
            dve.wait_ge(S["up_ps"], n + 1)
            if n < T:
                ins = v.tensor_copy(qkb[:, n, :, :].rearrange("p (b h) d -> p b (h d)", b=2), ps[:, b:b + 2, 0:384])
            else:
                kv = ps[:, b:b + 2, :].rearrange("p b (h d) -> p (b h) d", h=4)
                link(s, "dve", dve, v.tensor_copy(v_b[:, n - T, :, :], kv[:, :, 64:128]))
                rope_src = (proj[:, n - T, 1152:1184] if n < NTB - 1 else cache_r[:, :]).unsqueeze(1).broadcast_to([P, 8, ROPE])
                link(s, "dve", dve, v.tensor_copy(qkb[:, n, :, 64:96], rope_src))
                ins = v.tensor_copy(qkb[:, n, :, 0:64], kv[:, :, 0:64])
            ins.then_inc(S["up_d"], 1)
            if n < T:
                dve.wait_ge(S["up_d"], n + 1)
                sqn = sq[:, 0:768]
                flat = qkb[:, n, :, :].rearrange("p h d -> p (h d)")
                link(s, "dve", dve, v.tensor_tensor(sqn, flat, flat, ALU.mult))
                link(s, "dve", dve, v.tensor_reduce(ssb[:, 8 * n:8 * n + 8], sqn.rearrange("p (h d) -> p h d", h=8), AX.X, ALU.add))
        dve.wait_ge(S["ssb"], 1)
        v.tensor_scalar(xb[:, :], ssb[:, :], 1.0 / HD_B, EPS, ALU.mult, ALU.add).then_inc(S["b_x"], 1)
        rsqrt_dve(s, dve, xb[:, :], rb[:, :], tmpb[:, :], S["b_r"], 1)
        dve.sem_inc(S["refined"], 1)
        mod.add_bias(dve, 2)
        for n in range(NTB):
            rr = rb[:, 8 * n:8 * n + 8].unsqueeze(2).broadcast_to([P, 8, HD_B])
            g = b_gain[:, 0 if n < T else 1, :].unsqueeze(1).broadcast_to([P, 8, HD_B])
            if n < T:
                link(s, "dve", dve, v.tensor_tensor(qkb[:, n, :, :], qkb[:, n, :, :], rr, ALU.mult))
            else:
                dve.wait_ge(S["scaled"], n - T + 1)
            ins = v.tensor_tensor(qkb[:, n, :, :], qkb[:, n, :, :], g, ALU.mult)
            if n in (1, 2, 4, 5):
                link(s, "dve", dve, ins)
                ins = rope(s, dve, qkb[:, n, :, 64:96], "b", (n % 3) - 1, 8, rot_pool(sq, 256))
            if n < NTB - 1:
                link(s, "dve", dve, ins)
                if n + 3 < len(GATE_MOD):
                    mod.add_bias(dve, n + 3)
        ins.then_inc(S["b_ready"], 1)


def rot_pool(sq, n):
    return sq[:, 1024:1024 + n]


def rope(s, dve, x, which, tile, nh, scratch):
    v = s.nc.vector
    rot = HD_A if which == "a" else ROPE
    qtr = rot // 4
    cos = s.cid("cos_" + which)[:, tile * rot:(tile + 1) * rot].unsqueeze(1).broadcast_to([P, nh, rot])
    sin = s.cid("sin_" + which)[:, tile * rot:(tile + 1) * rot]
    tmp = scratch.rearrange("p (h d) -> p h d", h=nh)
    for blk in range(2):
        for u in range(2):
            a, b = blk * 2 * qtr + u * qtr, blk * 2 * qtr + (1 - u) * qtr
            link(s, "dve", dve, v.tensor_tensor(tmp[:, :, a:a + qtr], x[:, :, b:b + qtr],
                                                sin[:, a:a + qtr].unsqueeze(1).broadcast_to([P, nh, qtr]), ALU.mult))
    link(s, "dve", dve, v.tensor_tensor(x, x, cos, ALU.mult))
    return v.tensor_tensor(x, x, tmp, ALU.add)


def att_scores(s, st, qk_t, k_t, v_a, qkb_t, v_b, sink):
    nc, ps = s.nc, s.ps
    sb = stage_buffers(s, st, "sc_")
    prob = sb("prob", [P, 2, 4, 3 * P])
    prob_t = sb("prob_t", [P, 2, 12, P])
    o = sb("o", [P, T, D])
    mx, nb, den, rec, e_sink = (sb(n, [P, 2, 4]) for n in ("mx", "nb", "den", "rec", "e_sink"))
    names = ("s_ps", "nb", "exp", "den", "t_ps", "t_ev", "o_ps", "o_ev", "ot_ps", "ot_ev")
    S = {n: s.sem("sc_" + n) for n in names}
    mod = LaterModulation(s, "mod_", SHIFT_MOD, 7, sb("mod_part", [P, BANK])[:, :]).with_rows(sb)
    score = ps[:, 0:3, :].rearrange("p b n -> p (b n)")
    units = [(kind, t, g) for t in range(T) for kind in "AB" for g in range(2)]
    NU = len(units)
    assert len(SHIFT_MOD) == NU
    block = st.enter_context(nc.Block())

    def keys(t):
        return 1 if t == 0 else 3

    @block.sync
    def _(sp):
        loads = mod.row_loads()
        for dst, src in loads:
            sp.dma_start(dst, src).then_inc(s.loads, 16)
        s.loaded += 16 * len(loads)
        ring_loads(s, sp, s.at["att_out", 0] + 2)

    @block.tensor
    def _(pe):
        def scores(n):
            kind, t, g = units[n]
            nk = keys(t)
            if n >= 1:
                pe.wait_ge(S["exp"], 4 * n)
            for j in range(4):
                for c in range(nk):
                    kt = 0 if nk == 1 else 1 + c
                    if kind == "A":
                        lhs, rhs = qk_t[:, t, j, :], k_t[:, g, kt, :]
                    else:
                        lhs, rhs = qkb_t[:, 4 * g + j, t, :], qkb_t[:, 4 * g + j, 3 + kt, :]
                    masked = kind == "A" and (t, c) in ((1, 1), (2, 0))
                    i = j * nk + c
                    dst = ps[:, i // 4, (i % 4) * P:(i % 4 + 1) * P]
                    mm = pe.matmul(dst, lhs, rhs, start=True, stop=not masked)
                    if masked:
                        mm = pe.matmul(dst, s.ident, s.cid("mask_high") if t == 2 else s.cid("mask_low"), start=False, stop=True)
            mm.then_inc(S["s_ps"], 1)

        def turn(n):
            nk = keys(units[n][1])
            pe.wait_ge(S["exp"], 4 * n + 4)
            if n >= 1:
                pe.wait_ge(S["t_ev"], n)
            for j in range(4):
                for c in range(nk):
                    i = j * nk + c
                    mm = pe.transpose(ps[:, 3 + i // 4, (i % 4) * P:(i % 4 + 1) * P], prob[:, n % 2, j, c * P:(c + 1) * P], s.ident)
            mm.then_inc(S["t_ps"], 1)

        def weigh(n):
            kind, t, g = units[n]
            nk = keys(t)
            pe.wait_ge(S["t_ev"], n + 1)
            if n >= 1:
                pe.wait_ge(S["o_ev"], n)
            for j in range(4):
                for c in range(nk):
                    kt = 0 if nk == 1 else 1 + c
                    rhs = v_a[:, kt, 64 * g:64 * g + 64] if kind == "A" else v_b[:, kt, 4 * g + j, :]
                    mm = narrow_matmul(pe, ps[:, 6, j * 64:(j + 1) * 64], prob_t[:, n % 2, j * nk + c, :], rhs,
                                       start=(c == 0), stop=(c == nk - 1))
            mm.then_inc(S["o_ps"], 1)

        scores(0)
        for n in range(NU):
            turn(n)
            if n + 1 < NU:
                scores(n + 1)
            mod.products(pe, n)
            weigh(n)
            mod.sum(pe, n)
        pe.wait_ge(S["o_ev"], NU)
        mod.turn(pe)
        for t in range(T):
            pe.wait_ge(S["o_ev"], NU)
            b = 2 * t
            for k in range(KD):
                mm = pe.transpose(ps[:, b + k // 4, (k % 4) * P:(k % 4 + 1) * P], o[:, t, k::KD], s.ident)
            mm.then_inc(S["ot_ps"], 1)

    @block.scalar
    def _(act):
        for n in range(NU):
            kind, t, g = units[n]
            nk = keys(t)
            scale = HD_A ** -0.5 if kind == "A" else HD_B ** -0.5
            act.wait_ge(S["nb"], n + 1)
            if n >= 2:
                act.wait_ge(S["t_ps"], n - 1)
            for j in range(4):
                nc.scalar.activation(prob[:, n % 2, j, 0:nk * P], score[:, j * nk * P:(j + 1) * nk * P], ACT.Exp, scale=scale,
                                     bias=nb[:, n % 2, j:j + 1], accum_out=den[:, n % 2, j:j + 1]).then_inc(S["exp"], 1)
            if kind == "A":
                for j in range(4):
                    nc.scalar.activation(e_sink[:, n % 2, j:j + 1], sink[:, 4 * g + j:4 * g + j + 1], ACT.Exp,
                                         bias=nb[:, n % 2, j:j + 1]).then_inc(S["den"], 1)
            act.wait_ge(S["t_ps"], n + 1)
            nc.scalar.copy(prob_t[:, n % 2, 0:4 * nk, :].rearrange("p i n -> p (i n)"),
                           ps[:, 3:3 + nk, :].rearrange("p b n -> p (b n)")).then_inc(S["t_ev"], 1)

    @block.vector
    def _(dve):
        v = nc.vector

        def bias(n):
            kind, t, g = units[n]
            nk, b = keys(t), n % 2
            scale = HD_A ** -0.5 if kind == "A" else HD_B ** -0.5
            dve.wait_ge(S["s_ps"], n + 1)
            link(s, "dve", dve, v.tensor_reduce(mx[:, b, :], score[:, 0:4 * nk * P].rearrange("p (j n) -> p j n", j=4), AX.X, ALU.max))
            if kind == "A":
                link(s, "dve", dve, v.scalar_tensor_tensor(out=mx[:, b, :], in0=mx[:, b, :], scalar=scale,
                                                           in1=sink[:, 4 * g:4 * g + 4], op0=ALU.mult, op1=ALU.max))
                v.tensor_scalar(nb[:, b, :], mx[:, b, :], -1.0, None, ALU.mult).then_inc(S["nb"], 1)
            else:
                v.tensor_scalar(nb[:, b, :], mx[:, b, :], -scale, None, ALU.mult).then_inc(S["nb"], 1)

        sinks = 0
        dve.wait_ge(s.loads, s.loaded)
        bias(0)
        for n in range(NU):
            kind, t, g = units[n]
            b = n % 2
            dve.wait_ge(S["exp"], 4 * n + 4)
            if kind == "A":
                sinks += 4
                dve.wait_ge(S["den"], sinks)
                link(s, "dve", dve, v.tensor_tensor(den[:, b, :], den[:, b, :], e_sink[:, b, :], ALU.add))
            link(s, "dve", dve, v.reciprocal(rec[:, b, :], den[:, b, :]))
            if n + 1 < NU:
                bias(n + 1)
            mod.take_part(dve, n)
            dve.wait_ge(S["o_ps"], n + 1)
            c0 = (0 if kind == "A" else 512) + 256 * g
            v.tensor_tensor(o[:, t, c0:c0 + 256].rearrange("p (h d) -> p h d", h=4),
                            ps[:, 6, 0:256].rearrange("p (h d) -> p h d", h=4),
                            rec[:, b, :].unsqueeze(2).broadcast_to([P, 4, 64]), ALU.mult).then_inc(S["o_ev"], 1)
            mod.add_bias(dve, n)
        mod.take_turned(dve)
        for t in range(T):
            dve.wait_ge(S["ot_ps"], t + 1)
            v.tensor_copy(s.hT[:, :, t * P:(t + 1) * P], ps[:, 2 * t:2 * t + 2, :].rearrange("p b (k n) -> p (b k) n", k=4)).then_inc(S["ot_ev"], 1)

    st.close()
    with ExitStack() as st3:
        project_out(s, 0, st3, "ao_", s.hT, s.hT_r, KD, [("att_out", 0), ("att_out", 1)], MIX)


def project_out(s, l, st, pre, src, src_lo, nk, keys, m):
    nc, ps = s.nc, s.ps
    sb = stage_buffers(s, st, pre)
    gate = sb("gate", [P, 2, D])
    tmp = sb("tmp", [P, 2, BANK])
    src_hi = sb("src_hi", [P, nk, NTOK], F32R)
    rows = slice(32 * l, 32 * l + 2)
    g_ps, g_ev, o_ps, o_ev, s_hi, s_lo = (s.sem(pre + n) for n in ("g_ps", "g_ev", "o_ps", "o_ev", "s_hi", "s_lo"))
    pieces = [(s.at[keys[(h * nk + k) // KD]], lambda slot, k=k: slot[:, k % KD, :]) for h in range(2) for k in range(nk)]
    ws = SplitWeights(s, sb, pre, 4, [BANK], pieces)
    block = st.enter_context(nc.Block())
    last = s.at[keys[-1]]

    @block.sync
    def _(sp):
        ring_loads(s, sp, last + 1 + SLOT_RING)

    @block.tensor
    def _(pe):
        for g in range(2):
            for h in range(2):
                mm = pe.matmul(ps[:, 2 * g + h, :], s.cid("pick")[rows, g * P:(g + 1) * P], s.gates[rows, m, h * BANK:(h + 1) * BANK],
                               start=True, stop=True)
        mm.then_inc(g_ps, 1)
        for h in range(2):
            if h:
                pe.wait_ge(g_ev, 1)
            for k in range(nk):
                i = h * nk + k
                if h == 0 and k % 2 == 0:
                    pe.wait_ge(s_lo, k // 2 + 1)
                pe.wait_ge(ws.lo_ready, i + 1)
                for t in range(T):
                    c = slice(t * P, (t + 1) * P)
                    mm = split_passes(pe, ps[:, 4 * (1 - h) + t, :], (src_hi[:, k, c], src_lo[:, k, c]), (ws.hi(i), ws.lo(i)),
                                      k == 0, k == nk - 1)
                    if k == nk - 1 and t < T - 1:
                        mm.then_inc(o_ps, 1)
                mm.then_inc(ws.used, 1)
                ws.free(pe, i - 1)
        ws.free(pe, 2 * nk - 1)

    @block.scalar
    def _(act):
        for i in range(2 * nk):
            if i < nk and i % 2 == 0:
                nc.scalar.copy(src_hi[:, i:i + 2, :], src[:, i:i + 2, :]).then_inc(s_hi, 1)
            ws.make_hi(act, i)

    @block.vector
    def _(dve):
        v = nc.vector

        def take(h):
            for t in range(T):
                n = T * h + t
                if t < T - 1:
                    dve.wait_ge(o_ps, (T - 1) * h + t + 1)
                else:
                    dve.wait_ge(ws.used, nk * (h + 1))
                v.tensor_tensor(tmp[:, n % 2, :], ps[:, 4 * (1 - h) + t, :], gate[:, min(t, 1), h * BANK:(h + 1) * BANK], ALU.mult).then_inc(o_ev, 1)
                dve.wait_ge(o_ev, n + 1)
                ys = s.y[:, t, h * BANK:(h + 1) * BANK]
                v.tensor_tensor(ys, ys, tmp[:, n % 2, :], ALU.add)

        for i in range(2 * nk):
            if i < nk and i % 2 == 0:
                dve.wait_ge(s_hi, i // 2 + 1)
                v.tensor_tensor(src_lo[:, i:i + 2, :], src[:, i:i + 2, :], src_hi[:, i:i + 2, :].bitcast(F32), ALU.subtract).then_inc(s_lo, 1)
            ws.make_lo(dve, v, i)
            if i == 4:
                dve.wait_ge(g_ps, 1)
                v.tensor_copy(gate[:, :, :].rearrange("p g n -> p (g n)"), ps[:, 0:4, :].rearrange("p b n -> p (b n)")).then_inc(g_ev, 1)
                dve.wait_ge(g_ev, 1)
            if i == nk + 1:
                take(0)
        take(1)


def ssd(s, st):
    sb = stage_buffers(s, st, "ssd_")
    xs = sb("xs", [P, T, D_INNER])
    with ExitStack() as st2:
        sb2 = stage_buffers(s, st2, "ssd_")
        g = Shared()
        g.b_t, g.c_t = sb2("b_t", [P, G_C, NTOK]), sb2("c_t", [P, G_C, NTOK])
        g.b_n = sb2("b_n", [P, T, G_C, N_C])
        g.state = sb2("state", [P, 2, D_INNER])
        g.dt, g.dta = sb2("dt", [P, T, 64]), sb2("dta", [P, T, 64])
        g.nacs, g.eacs, g.etot, g.toend = (sb2(n, [P, T, 64]) for n in ("nacs", "eacs", "etot", "toend"))
        with ExitStack() as st3:
            ssd_conv(s, st3, xs, g)
        with ExitStack() as st3:
            ssd_scan(s, st3, xs, g)
    y_t, y_t_r = with_f32r_view(s.nc, sb, "y_t", [P, 2 * KD, NTOK])
    with ExitStack() as st2:
        ssd_gate(s, st2, xs, y_t)
    with ExitStack() as st2:
        project_out(s, 1, st2, "so_", y_t, y_t_r, 2 * KD, [("ssd_out", (j, kh)) for j in range(2) for kh in range(2)], MIX)


def ssd_conv(s, st, xs, g):
    nc, w, ps = s.nc, s.w, s.ps
    sb = stage_buffers(s, st, "cv_")
    taps_in, taps = sb("taps_in", [32, 6, P]), sb("taps", [P, 6, 32])
    PAD = NTOK + 8
    xp, cv, x_t = sb("xp", [P, 2, PAD]), sb("cv", [P, 2, PAD - 4]), sb("x_t", [P, 2, NTOK])
    dtb, alog, ea = sb("dtb", [P, 64]), sb("alog", [P, 64]), sb("ea", [P, 64])
    xs_flat = xs[:, :, :].rearrange("p t n -> p (t n)")
    v1, v2, v3, v4 = (xs_flat[:, 4096 + 192 * i:4096 + 192 * (i + 1)] for i in range(4))
    names = ("turn_ps", "turn_ev", "xp", "cv", "silu", "tr_ps", "tr_ev", "dt_ps", "dt_x", "dt_e", "dta", "acs_ps",
             "acs_x", "acs_e", "zero", "h_hi", "h_lo")
    S = {n: s.sem("cv_" + n) for n in names}
    s0 = xs[:, :, :].rearrange("p t n -> p (t n)")[:, 0:4096].rearrange("p (d c n) -> p d c n", d=2, c=16)
    u0, dt0 = s.at["ssd_xbc", 0], s.at["ssd_dt", 0]
    NT = 32
    s.h_parts = (s.ring_r[:, s.slot_of[dt0], :, P:P + NTOK], s.hT_r[:, :, :])
    pieces = [(u0 + n // 4, lambda slot, n=n, h=h: slot[:, 4 * h:4 * h + 4, (n % 4) * P:(n % 4 + 1) * P]) for n in range(NT) for h in range(2)]
    ws = SplitWeights(s, sb, "cv_", 4, [4, P], pieces)
    block = st.enter_context(nc.Block())

    def turned(n):
        return n < 24

    @block.sync
    def _(sp):
        loads = [(taps_in[:, 0:5, :], w["ssd_conv_w"][0].rearrange("k (c p) -> c k p", p=P)),
                 (taps_in[:, 5, :], w["ssd_conv_b"][0].rearrange("(c p) -> c p", p=P)),
                 (dtb[:, 0:32], w["ssd_dtb_fwd"][0].partition_broadcast(P)),
                 (dtb[:, 32:64], w["ssd_dtb_bwd"][0].partition_broadcast(P)),
                 (alog[:, 0:32], w["ssd_alog_fwd"][0].partition_broadcast(P)),
                 (alog[:, 32:64], w["ssd_alog_bwd"][0].partition_broadcast(P)),
                 (s0[:, 0], w["state_c_fwd"][0, 0].rearrange("h p n -> (h p) n").rearrange("(c q) n -> q c n", q=P)),
                 (s0[:, 1], w["state_c_bwd"][0, 0].rearrange("h p n -> (h p) n").rearrange("(c q) n -> q c n", q=P))]
        for dst, src in loads:
            sp.dma_start(dst, src).then_inc(s.loads, 16)
        s.loaded += 16 * len(loads)
        ring_loads(s, sp, u0 + 8 + SLOT_RING - 1)

    @block.tensor
    def _(pe):
        ring_wait(s, pe, dt0)
        for t in range(T):
            for k in range(KD):
                mm = narrow_matmul(pe, ps[:, 5, t * 64:(t + 1) * 64], s.hT[:, k, t * P:(t + 1) * P], s.ring[:, s.slot_of[dt0], k, 0:64],
                                   start=(k == 0), stop=(k == KD - 1))
        mm.then_inc(S["dt_ps"], 1)

        def tables():
            pe.wait_ge(s.loads, s.loaded)
            for k in range(6):
                mm = pe.transpose(ps[:, 4, k * 32:(k + 1) * 32], taps_in[:, k, :], s.ident[0:32, 0:32])
            mm.then_inc(S["turn_ps"], 1)
            for q in range(4):
                if q >= 2:
                    pe.wait_ge(S["turn_ev"], q)
                for c in range(8):
                    mm = pe.transpose(ps[:, (2, 6)[q % 2] + c // 4, (c % 4) * P:(c % 4 + 1) * P], s0[:, q // 2, 8 * (q % 2) + c, :], s.ident)
                mm.then_inc(S["turn_ps"], 1)
            pe.wait_ge(S["turn_ev"], 5)

        def sums():
            pe.wait_ge(S["dta"], 1)
            for t in range(T):
                for d in range(2):
                    narrow_matmul(pe, ps[:, 6, t * 64 + 32 * d:t * 64 + 32 * d + 32], s.cid("from_" if d else "upto"),
                                  g.dta[:, t, 32 * d:32 * d + 32], start=True, stop=True)
                mm = narrow_matmul(pe, ps[:, 7, t * 64:(t + 1) * 64], s.cid("ones"), g.dta[:, t, :], start=True, stop=True)
            mm.then_inc(S["acs_ps"], 1)

        def turn(n):
            pe.wait_ge(S["silu"], 2 * (n + 1))
            if n >= 2:
                pe.wait_ge(S["tr_ev"], n - 1)
            src = x_t[:, n % 2, :] if n < 16 else g.b_t[:, n - 16, :]
            for t in range(T):
                mm = pe.transpose(ps[:, 2 + n % 2, t * P:(t + 1) * P], src[:, t * P:(t + 1) * P], s.ident)
            mm.then_inc(S["tr_ps"], 1)

        pe.wait_ge(S["h_lo"], 4)
        for n in range(NT):
            if n >= 2:
                pe.wait_ge(S["xp"], 2 * (n - 1))
            for half in range(2):
                i = 2 * n + half
                pe.wait_ge(ws.lo_ready, i + 1)
                for k in range(4):
                    kk = 4 * half + k
                    mm = split_passes(pe, ps[:, n % 2, 0:NTOK], (ws.hi(i)[:, k, :], ws.lo(i)[:, k, :]),
                                      (s.h_parts[0][:, kk, :], s.h_parts[1][:, kk, :]), kk == 0, kk == KD - 1)
                mm.then_inc(ws.used, 1)
                ws.free(pe, i - 1)
            if n == 1:
                tables()
            if n == 3:
                sums()
            if n >= 2 and turned(n - 2):
                turn(n - 2)
        ws.free(pe, 2 * NT - 1)

    @block.gpsimd
    def _(pool):
        for i in range(2 * NT):
            ws.make_lo(pool, nc.gpsimd, i)

    @block.scalar
    def _(act):
        a = nc.scalar

        def silu(n):
            act.wait_ge(S["cv"], n + 1)
            if n < 16 and n >= 2:
                act.wait_ge(S["tr_ps"], n - 1)
            dst = x_t[:, n % 2, :] if n < 16 else (g.b_t[:, n - 16, :] if n < 24 else g.c_t[:, n - 24, :])
            bias = taps[:, 5, n:n + 1]
            a.activation(dst[:, 0:P], cv[:, n % 2, 0:P], ACT.Silu, bias=bias).then_inc(S["silu"], 1)
            a.activation(dst[:, P:NTOK], cv[:, n % 2, P + 4:NTOK + 4], ACT.Silu, bias=bias).then_inc(S["silu"], 1)

        def turned_out(n):
            act.wait_ge(S["tr_ps"], n + 1)
            dst = xs[:, :, n * P:(n + 1) * P] if n < 16 else g.b_n[:, :, n - 16, :]
            a.copy(dst, ps[:, 2 + n % 2, 0:NTOK].rearrange("p (t n) -> p t n", t=T)).then_inc(S["tr_ev"], 1)

        ring_wait(s, act, dt0)
        for k in range(0, KD, 2):
            a.copy(s.h_parts[0][:, k:k + 2, :], s.hT[:, k:k + 2, :]).then_inc(S["h_hi"], 1)
        for i in range(4):
            ws.make_hi(act, i)
        act.wait_ge(s.loads, s.loaded)
        a.activation(ea[:, :], alog[:, :], ACT.Exp).then_inc(S["dt_e"], 1)
        act.wait_ge(S["dt_x"], 1)
        a.activation(v2[:, :], v2[:, :], ACT.Exp, scale=-1.0).then_inc(S["dt_e"], 1)
        act.wait_ge(S["turn_ps"], 1)
        a.copy(taps[:, :, :].rearrange("p k c -> p (k c)"), ps[:, 4, 0:192]).then_inc(S["turn_ev"], 1)
        for q in range(4):
            act.wait_ge(S["turn_ps"], q + 2)
            a.copy(g.state[:, q // 2, (q % 2) * D:(q % 2 + 1) * D], ps[:, (2, 6)[q % 2]:(2, 6)[q % 2] + 2, :].rearrange("p b n -> p (b n)")).then_inc(S["turn_ev"], 1)
        act.wait_ge(S["zero"], 1)
        for n in range(NT + 3):
            if 1 <= n < NT - 1:
                for i in (2 * n + 2, 2 * n + 3):
                    ws.make_hi(act, i)
            if n < NT:
                act.wait_ge(ws.used, 2 * (n + 1))
                if n >= 2:
                    act.wait_ge(S["cv"], n - 1)
                a.copy(xp[:, n % 2, 2:P + 2], ps[:, n % 2, 0:P]).then_inc(S["xp"], 1)
                a.copy(xp[:, n % 2, P + 6:NTOK + 6], ps[:, n % 2, P:NTOK]).then_inc(S["xp"], 1)
            if 1 <= n <= NT:
                silu(n - 1)
            if n >= 3 and turned(n - 3):
                turned_out(n - 3)
            if n == 6:
                act.wait_ge(S["acs_x"], 1)
                a.activation(flat3(g.toend), flat3(g.toend), ACT.Exp).then_inc(S["acs_e"], 1)
                a.activation(flat3(g.eacs), flat3(g.nacs), ACT.Exp, scale=-1.0).then_inc(S["acs_e"], 1)
                a.activation(flat3(g.etot), flat3(g.etot), ACT.Exp).then_inc(S["acs_e"], 1)

    @block.vector
    def _(dve):
        v = nc.vector
        v.memset(xp[:, :, :], 0.0).then_inc(S["zero"], 1)
        dve.wait_ge(S["dt_ps"], 1)
        for k in range(0, KD, 2):
            dve.wait_ge(S["h_hi"], k // 2 + 1)
            v.tensor_tensor(s.h_parts[1][:, k:k + 2, :], s.hT[:, k:k + 2, :], s.h_parts[0][:, k:k + 2, :].bitcast(F32), ALU.subtract).then_inc(S["h_lo"], 1)
        dve.wait_ge(s.loads, s.loaded)
        dve.wait_ge(S["dt_ps"], 1)
        link(s, "dve", dve, v.tensor_tensor(v1[:, :].rearrange("p (t h) -> p t h", t=T), ps[:, 5, 0:T * 64].rearrange("p (t h) -> p t h", t=T),
                                            dtb[:, :].unsqueeze(1).broadcast_to([P, T, 64]), ALU.add))
        v.scalar_tensor_tensor(out=v2[:, :], in0=v1[:, :], scalar=-1.0, in1=v1[:, :], op0=ALU.mult, op1=ALU.max).then_inc(S["dt_x"], 1)
        dve.wait_ge(S["dt_e"], 2)
        link(s, "dve", dve, v.tensor_scalar(v3[:, :], v2[:, :], 2.0, None, ALU.add))
        link(s, "dve", dve, v.reciprocal(v3[:, :], v3[:, :]))
        link(s, "dve", dve, v.tensor_tensor(v2[:, :], v2[:, :], v3[:, :], ALU.mult))
        link(s, "dve", dve, v.tensor_tensor(v3[:, :], v2[:, :], v2[:, :], ALU.mult))
        link(s, "dve", dve, v.tensor_scalar(v4[:, :], v3[:, :], 1.0 / 13, None, ALU.mult))
        for odd in (11, 9, 7, 5, 3):
            link(s, "dve", dve, v.scalar_tensor_tensor(out=v4[:, :], in0=v4[:, :], scalar=1.0 / odd, in1=v3[:, :], op0=ALU.add, op1=ALU.mult))
        link(s, "dve", dve, v.scalar_tensor_tensor(out=v4[:, :], in0=v4[:, :], scalar=1.0, in1=v2[:, :], op0=ALU.add, op1=ALU.mult))
        link(s, "dve", dve, v.tensor_scalar(v4[:, :], v4[:, :], 2.0, None, ALU.mult))
        link(s, "dve", dve, v.scalar_tensor_tensor(out=flat3(g.dt), in0=v1[:, :], scalar=0.0, in1=v4[:, :], op0=ALU.max, op1=ALU.add))
        v.scalar_tensor_tensor(out=g.dta[:, :, :], in0=g.dt[:, :, :], scalar=-1.0, in1=ea[:, :].unsqueeze(1).broadcast_to([P, T, 64]),
                               op0=ALU.mult, op1=ALU.mult).then_inc(S["dta"], 1)
        dve.wait_ge(S["turn_ev"], 1)
        for n in range(NT):
            dve.wait_ge(S["xp"], 2 * (n + 1))
            if n >= 2:
                dve.wait_ge(S["silu"], 2 * (n - 1))
            o = cv[:, n % 2, :]
            link(s, "dve", dve, v.tensor_scalar(o, xp[:, n % 2, 0:PAD - 4], taps[:, 0, n:n + 1], None, ALU.mult))
            for k in range(1, 5):
                ins = v.scalar_tensor_tensor(out=o, in0=xp[:, n % 2, k:k + PAD - 4], scalar=taps[:, k, n:n + 1], in1=o,
                                             op0=ALU.mult, op1=ALU.add)
                if k < 4:
                    link(s, "dve", dve, ins)
            ins.then_inc(S["cv"], 1)
            if n == 4:
                dve.wait_ge(S["acs_ps"], 1)
                link(s, "dve", dve, v.tensor_scalar(flat3(g.nacs), ps[:, 6, 0:T * 64], -1.0, None, ALU.mult))
                link(s, "dve", dve, v.tensor_tensor(flat3(g.toend), flat3(g.nacs), ps[:, 7, 0:T * 64], ALU.add))
                v.tensor_copy(flat3(g.etot), ps[:, 7, 0:T * 64]).then_inc(S["acs_x"], 1)
            if n == 8:
                dve.wait_ge(S["acs_e"], 3)
                link(s, "dve", dve, v.tensor_tensor(flat3(g.toend), flat3(g.toend), flat3(g.dt), ALU.mult))


def flat3(t):
    return t[:, :, :].rearrange("p a b -> p (a b)")


def ssd_scan(s, st, xs, g):
    nc, w, ps, out = s.nc, s.w, s.ps, s.out
    sb = stage_buffers(s, st, "scan_")
    W = R_C * P_C
    e = sb("e", [P, 2, 2, R_C, P])
    cb = sb("cb", [P, T, P])
    xdt = sb("xdt", [P, T, 2, R_C, P_C])
    xe = sb("xe", [P, 4, R_C, P_C])
    inter = sb("inter", [P, 2, W])
    stage = sb("stage", [P, BANK])
    skip = sb("skip", [P, H_C])
    ident_h = sb("ident_h", [P, P], BF16)
    mask_h = sb("mask_h", [P, 2, P], BF16)
    names = ("cb_ps", "cb_ev", "a_ps", "exp", "m", "pool", "y_ps", "y_ev", "i_ps", "i_ev", "sp_ps", "sp_ev", "s1_ps", "upd", "init", "stage")
    S = {n: s.sem("scan_" + n) for n in names}
    EX = ((0, 0), (0, 1), (1, 0), (2, 1))
    block = st.enter_context(nc.Block())

    @block.sync
    def _(sp):
        sp.dma_start(skip[:, :], w["ssd_d"][0].partition_broadcast(P)).then_inc(s.loads, 16)
        s.loaded += 16
        for q in range(G_C):
            sp.wait_ge(S["sp_ev"], q + 1)
            for d in range(2):
                dst = out["new_state_bwd" if d else "new_state_fwd"][0, 0, 4 * q:4 * q + 4].rearrange("(a b) p n -> (b p) a n", a=2)
                sp.dma_start(dst, stage[:, d * 256:(d + 1) * 256].rearrange("p (a n) -> p a n", a=2)).then_inc(S["stage"], 16)
        sp.wait_ge(S["stage"], 32 * G_C)

    @block.gpsimd
    def _(pool):
        pool.wait_ge(s.loads, s.loaded)

        def scaled(dst, t, src, col):
            return nc.gpsimd.tensor_tensor(dst, xs[:, t, q * W:(q + 1) * W].rearrange("p (h d) -> p h d", h=R_C),
                                           src[:, col:col + R_C].unsqueeze(2).broadcast_to([P, R_C, P_C]), ALU.mult)
        for q in range(G_C):
            if q:
                pool.wait_ge(S["y_ps"], 3 * q)
                pool.wait_ge(S["y_ev"], 3 * q)
                pool.wait_ge(S["s1_ps"], q)
            for t in range(T):
                for d in range(2):
                    scaled(xdt[:, t, d], t, g.dt[:, t, :], 32 * d + 4 * q)
                for i, (tt, d) in enumerate(EX):
                    if tt == t:
                        scaled(xe[:, i], t, g.toend[:, t, :], 32 * d + 4 * q)
                scaled(xs[:, t, q * W:(q + 1) * W].rearrange("p (h d) -> p h d", h=R_C), t, skip, 4 * q).then_inc(S["pool"], 1)

    @block.tensor
    def _(pe):
        pe.wait_ge(S["init"], 3)

        def decay(q, t):
            u = 3 * q + t
            if u >= 2:
                pe.wait_ge(S["exp"], 8 * (u - 1))
            for d in range(2):
                b = 1 + 2 * (u % 2) + d
                for r in range(R_C):
                    c = 32 * d + 4 * q + r
                    pe.matmul(ps[:, b, r * P:(r + 1) * P], g.dta[:, t, c:c + 1].broadcast_to([P, P]),
                              s.cid("from_" if d else "upto"), start=(r == 0), stop=False, skip_group_check=True)
                mm = pe.matmul(ps[:, b, :].rearrange("p (r i) -> p r i", r=R_C), ident_h[:, :],
                               mask_h[:, d, :].unsqueeze(1).broadcast_to([P, R_C, P]), start=False, stop=True, skip_group_check=True)
            mm.then_inc(S["a_ps"], 1)

        def give(q, t):
            u = 3 * q + t
            pe.wait_ge(S["m"], u + 1)
            pe.wait_ge(S["pool"], u + 1)
            if u:
                pe.wait_ge(S["y_ev"], u)
            for r in range(R_C):
                for d in range(2):
                    mm = narrow_matmul(pe, ps[:, 5, r * P_C:(r + 1) * P_C], e[:, u % 2, d, r, :], xdt[:, t, d, r, :],
                                       start=(d == 0), stop=(d == 1))
            mm.then_inc(S["y_ps"], 1)

        def from_state(q, rnd):
            n = 2 * q + rnd
            if n:
                pe.wait_ge(S["i_ev"], n)
            if rnd:
                pe.wait_ge(S["upd"], 2 * (q + 1))
            for d in range(2):
                t = (1, 2)[d] if rnd == 0 else (2, 1)[d]
                mm = pe.matmul(ps[:, 7, d * W:(d + 1) * W], g.c_t[:, q, t * P:(t + 1) * P], g.state[:, d, q * W:(q + 1) * W],
                               start=True, stop=True)
            mm.then_inc(S["i_ps"], 1)

        def chunk_products(q):
            if q:
                pe.wait_ge(S["cb_ev"], q)
            for t in range(T):
                mm = pe.matmul(ps[:, 0, t * P:(t + 1) * P], g.b_t[:, q, t * P:(t + 1) * P], g.c_t[:, q, t * P:(t + 1) * P],
                               start=True, stop=True)
            mm.then_inc(S["cb_ps"], 1)

        chunk_products(0)
        decay(0, 0)
        for q in range(G_C):
            decay(q, 1)
            from_state(q, 0)
            pe.wait_ge(S["pool"], 3 * q + 1)
            if q:
                pe.wait_ge(S["upd"], 2 * q)
            for d in range(2):
                for a in range(2):
                    mm = pe.matmul(ps[:, 6, (2 * d + a) * P:(2 * d + a + 1) * P], xe[:, d, 2 * a:2 * a + 2, :].rearrange("p h d -> p (h d)"),
                                   g.b_n[:, 0, q, :], start=True, stop=True)
            mm.then_inc(S["sp_ps"], 1)
            give(q, 0)
            decay(q, 2)
            pe.wait_ge(S["pool"], 3 * q + 3)
            pe.wait_ge(S["sp_ev"], q + 1)
            for d in range(2):
                mm = pe.matmul(ps[:, 6, d * W:(d + 1) * W], g.b_n[:, 1 + d, q, :], xe[:, 2 + d, :, :].rearrange("p h d -> p (h d)"),
                               start=True, stop=True)
            mm.then_inc(S["s1_ps"], 1)
            give(q, 1)
            if q + 1 < G_C:
                chunk_products(q + 1)
                decay(q + 1, 0)
            from_state(q, 1)
            give(q, 2)

    @block.scalar
    def _(act):
        a = nc.scalar
        for u in range(3 * G_C):
            q, t = divmod(u, T)
            act.wait_ge(S["a_ps"], u + 1)
            if u >= 2:
                act.wait_ge(S["y_ps"], u - 1)
            for d in range(2):
                for r in range(R_C):
                    c = 32 * d + 4 * q + r
                    a.activation(e[:, u % 2, d, r, :], ps[:, 1 + 2 * (u % 2) + d, r * P:(r + 1) * P], ACT.Exp,
                                 bias=g.nacs[:, t, c:c + 1]).then_inc(S["exp"], 1)
            if t == 1:
                act.wait_ge(S["sp_ps"], q + 1)
                if q >= 1:
                    act.wait_ge(S["stage"], 32 * q)
                a.copy(stage[:, :], ps[:, 6, :]).then_inc(S["sp_ev"], 1)

    @block.vector
    def _(dve):
        v = nc.vector
        v.tensor_copy(ident_h[:, :], s.ident).then_inc(S["init"], 1)
        v.tensor_copy(mask_h[:, 0, :], s.cid("mask_high")).then_inc(S["init"], 1)
        v.tensor_copy(mask_h[:, 1, :], s.cid("mask_low")).then_inc(S["init"], 1)

        def weigh(q, t):
            u = 3 * q + t
            dve.wait_ge(S["exp"], 8 * (u + 1))
            m = e[:, u % 2].rearrange("p d r i -> p (d r) i")
            v.tensor_tensor(m, m, cb[:, t, :].unsqueeze(1).broadcast_to([P, 2 * R_C, P]), ALU.mult).then_inc(S["m"], 1)

        def take(q, t):
            u = 3 * q + t
            dve.wait_ge(S["y_ps"], u + 1)
            dve.wait_ge(S["pool"], u + 1)
            v.tensor_tensor(xs[:, t, q * W:(q + 1) * W], ps[:, 5, 0:W], xs[:, t, q * W:(q + 1) * W], ALU.add).then_inc(S["y_ev"], 1)
            dve.wait_ge(S["y_ev"], u + 1)

        def add_inter(q, rnd, d):
            t = (1, 2)[d] if rnd == 0 else (2, 1)[d]
            yq = xs[:, t, q * W:(q + 1) * W]
            link(s, "dve", dve, v.tensor_tensor(yq, yq, inter[:, d, :], ALU.add))

        def scale_inter(q, rnd):
            dve.wait_ge(S["i_ps"], 2 * q + rnd + 1)
            for d in range(2):
                t = (1, 2)[d] if rnd == 0 else (2, 1)[d]
                c = 32 * d + 4 * q
                ins = v.tensor_tensor(inter[:, d, :].rearrange("p (h d) -> p h d", h=R_C), ps[:, 7, d * W:(d + 1) * W].rearrange("p (h d) -> p h d", h=R_C),
                                      g.eacs[:, t, c:c + 4].unsqueeze(2).broadcast_to([P, R_C, P_C]), ALU.mult)
                if d == 0:
                    link(s, "dve", dve, ins)
            ins.then_inc(S["i_ev"], 1)
            dve.wait_ge(S["i_ev"], 2 * q + rnd + 1)

        for q in range(G_C):
            dve.wait_ge(S["cb_ps"], q + 1)
            v.tensor_copy(cb[:, :, :].rearrange("p t i -> p (t i)"), ps[:, 0, 0:NTOK]).then_inc(S["cb_ev"], 1)
            dve.wait_ge(S["cb_ev"], q + 1)
            weigh(q, 0)
            weigh(q, 1)
            scale_inter(q, 0)
            for d in range(2):
                c, tt = 32 * d + 4 * q, 1 + d
                sq = g.state[:, d, q * W:(q + 1) * W].rearrange("p (h d) -> p h d", h=R_C)
                link(s, "dve", dve, v.tensor_tensor(sq, sq, g.etot[:, tt, c:c + 4].unsqueeze(2).broadcast_to([P, R_C, P_C]), ALU.mult))
            take(q, 0)
            weigh(q, 2)
            dve.wait_ge(S["s1_ps"], q + 1)
            for d in range(2):
                sq = g.state[:, d, q * W:(q + 1) * W]
                v.tensor_tensor(sq, sq, ps[:, 6, d * W:(d + 1) * W], ALU.add).then_inc(S["upd"], 1)
            take(q, 1)
            add_inter(q, 0, 0)
            take(q, 2)
            add_inter(q, 0, 1)
            scale_inter(q, 1)
            add_inter(q, 1, 0)
            add_inter(q, 1, 1)


def ssd_gate(s, st, xs, y_t):
    nc, w, ps = s.nc, s.w, s.ps
    sb = stage_buffers(s, st, "gate_")
    z = sb("z", [P, 2, BANK])
    gw_in, gw = sb("gw_in", [16, P]), sb("gw", [P, 16])
    sq = sb("sq", [P, 256])
    ss, x, r, tmp = (sb(n, [P, 4, T * 2]) for n in ("ss", "x", "r", "tmp"))
    names = ("z_ps", "z", "y", "ss", "x", "r", "yn", "gw_ps", "gw", "t_ps", "t_ev")
    S = {n: s.sem("gate_" + n) for n in names}
    z0 = s.at["ssd_z", 0]
    ws = SplitWeights(s, sb, "gate_", 4, [BANK], [(z0 + j, lambda slot, k=k: slot[:, k, :]) for j in range(4) for k in range(KD)])
    block = st.enter_context(nc.Block())

    def z_bank(j, t):
        return 3 * (j % 2) + t

    @block.sync
    def _(sp):
        sp.dma_start(gw_in[:, :], w["ssd_norm"][0].rearrange("(k p) -> k p", p=P)).then_inc(s.loads, 16)
        s.loaded += 16
        ring_loads(s, sp, z0 + 4 + SLOT_RING)

    @block.tensor
    def _(pe):
        def turn(j):
            for t in range(T):
                n = 3 * j + t
                pe.wait_ge(S["yn"], n + 1)
                if n == 0:
                    pe.wait_ge(S["gw"], 1)
                if n >= 2:
                    pe.wait_ge(S["t_ev"], n - 1)
                for k in range(4):
                    mm = pe.transpose(ps[:, 6 + n % 2, k * P:(k + 1) * P], xs[:, t, (4 * j + k) * P:(4 * j + k + 1) * P], s.ident)
                mm.then_inc(S["t_ps"], 1)

        pe.wait_ge(s.loads, s.loaded)
        pe.transpose(ps[:, 7, 0:16], gw_in[:, :], s.ident[0:16, 0:16]).then_inc(S["gw_ps"], 1)
        for j in range(4):
            if j >= 2:
                pe.wait_ge(S["z"], 3 * (j - 1))
            for k in range(KD):
                i = KD * j + k
                pe.wait_ge(ws.lo_ready, i + 1)
                for t in range(T):
                    c = slice(t * P, (t + 1) * P)
                    mm = split_passes(pe, ps[:, z_bank(j, t), :], (s.h_parts[0][:, k, c], s.h_parts[1][:, k, c]), (ws.hi(i), ws.lo(i)),
                                      k == 0, k == KD - 1)
                mm.then_inc(ws.used, 1)
                ws.free(pe, i - 1)
            if j:
                turn(j - 1)
        ws.free(pe, 4 * KD - 1)
        pe.sem_inc(s.ring_free, 1)
        turn(3)

    @block.scalar
    def _(act):
        a = nc.scalar

        def silu(j, t):
            n = 3 * j + t
            if t == 0:
                act.wait_ge(ws.used, KD * (j + 1))
            if n >= 2:
                act.wait_ge(S["y"], n - 1)
            a.activation(z[:, n % 2, :], ps[:, z_bank(j, t), :], ACT.Silu).then_inc(S["z"], 1)

        def squares(j, t):
            act.wait_ge(S["y"], 3 * j + t + 1)
            for g in range(2):
                i = 6 * j + 2 * t + g
                if i:
                    act.wait_ge(S["ss"], i)
                c = j * BANK + g * 256
                a.activation(sq[:, :], xs[:, t, c:c + 256], ACT.Square, accum_out=ss[:, j, 2 * t + g:2 * t + g + 1]).then_inc(S["ss"], 1)

        for j in range(5):
            for k in range(KD):
                if j < 4:
                    ws.make_hi(act, KD * j + k)
                if j:
                    if 1 <= k <= 3:
                        silu(j - 1, k - 1)
                    if 3 <= k <= 5:
                        squares(j - 1, k - 3)
                    if k == 6:
                        rsqrt_act(s, act, x[:, j - 1, :], r[:, j - 1, :], S["x"], j, S["r"])

    @block.vector
    def _(dve):
        v = nc.vector

        def take_turned(j):
            for t in range(T):
                n = 3 * j + t
                dve.wait_ge(S["t_ps"], n + 1)
                v.tensor_tensor(y_t[:, 4 * j:4 * j + 4, t * P:(t + 1) * P], ps[:, 6 + n % 2, :].rearrange("p (k n) -> p k n", k=4),
                                gw[:, 4 * j:4 * j + 4].unsqueeze(2).broadcast_to([P, 4, P]), ALU.mult).then_inc(S["t_ev"], 1)

        def gated(j, t):
            n = 3 * j + t
            dve.wait_ge(S["z"], n + 1)
            yj = xs[:, t, j * BANK:(j + 1) * BANK]
            v.tensor_tensor(yj, yj, z[:, n % 2, :], ALU.mult).then_inc(S["y"], 1)

        def normalise(j):
            dve.wait_ge(S["ss"], 6 * (j + 1))
            v.tensor_scalar(x[:, j, :], ss[:, j, :], 1.0 / 256, EPS, ALU.mult, ALU.add).then_inc(S["x"], 1)
            rsqrt_dve(s, dve, x[:, j, :], r[:, j, :], tmp[:, j, :], S["r"], j + 1)
            for t in range(T):
                yj = xs[:, t, j * BANK:(j + 1) * BANK].rearrange("p (g c) -> p g c", g=2)
                v.tensor_tensor(yj, yj, r[:, j, 2 * t:2 * t + 2].unsqueeze(2).broadcast_to([P, 2, 256]), ALU.mult).then_inc(S["yn"], 1)

        for j in range(5):
            for k in range(KD):
                if j < 4:
                    ws.make_lo(dve, v, KD * j + k)
                if (j, k) == (0, 1):
                    dve.wait_ge(S["gw_ps"], 1)
                    v.tensor_copy(gw[:, :], ps[:, 7, 0:16]).then_inc(S["gw"], 1)
                    dve.wait_ge(S["gw"], 1)
                if j >= 2 and k == 1:
                    take_turned(j - 2)
                if j:
                    if 1 <= k <= 3:
                        gated(j - 1, k - 1)
                    if k == 6:
                        normalise(j - 1)
        take_turned(3)


def moe(s, l, st):
    sb = stage_buffers(s, st, f"moe{l}_")
    m = Shared()
    m.hp = [sb(n, [P, T, KD, P], F32R) for n in ("hp_hi", "hp_lo")]
    m.acc = s.hT[:, :, :].rearrange("p k n -> p (k n)").rearrange("p (t d) -> p t d", t=T)
    m.gates = sb("gates", [P, T, NE])
    m.code = sb("code", [P, T, NE])
    m.most = sb("most", [1, 1], I32)
    m.w2_ring = sb("w2_ring", [P, 4, 2, D])
    m.w2_full = [s.sem(f"ex{l}_w2_full{n}") for n in range(4)]
    with ExitStack() as routing:
        sb2 = stage_buffers(s, routing, f"moe{l}_")
        m.rw, m.rb = sb2("rw", [P, KD, NG + NE]), sb2("rb", [P, NG + NE])
        loads = [(m.rw[:, :, 0:NG], s.w["moe_wg"][l].rearrange("(p k) n -> p k n", k=KD)),
                 (m.rw[:, :, NG:NG + NE], s.w["moe_we"][l].rearrange("(p k) n -> p k n", k=KD)),
                 (m.rb[:, 0:NG], s.w["moe_bg"][l].partition_broadcast(P)),
                 (m.rb[:, NG:NG + NE], s.w["moe_be"][l].partition_broadcast(P))]
        with ExitStack() as st2:
            norm_stage(s, l, FFN, st2, hp=m.hp, loads=loads)
        with ExitStack() as st2:
            route(s, l, st2, m)
    with ExitStack() as st2:
        experts(s, l, st2, m)
    with ExitStack() as st2:
        add_moe(s, l, st2, m)


def route(s, l, st, m):
    nc, w, ps = s.nc, s.w, s.ps
    sb = stage_buffers(s, st, f"rt{l}_")
    rw, rb = m.rw, m.rb
    lg = sb("lg", [P, T, NG + NE])
    v4 = sb("v4", [P, T, NG])
    oh4 = sb("oh4", [P, T, NG])
    le, eq, oh1, oh2, sel = (sb(n, [P, T, NE]) for n in ("le", "eq", "oh1", "oh2", "sel"))
    mx, m1, m2, t1, ptop, w1, w2 = (sb(n, [P, T, 1]) for n in ("mx", "m1", "m2", "t1", "ptop", "w1", "w2"))
    top = sb("top", [P, 1])
    names = ("lg_ps", "x4", "e4", "x2", "e2", "sel", "rank_ps")
    S = {n: s.sem(f"rt{l}_" + n) for n in names}
    block = st.enter_context(nc.Block())

    @block.sync
    def _(sp):
        for e in range(4):
            sp.dma_start(m.w2_ring[:, e], w["moe_w2"][l, e].rearrange("(p c) d -> p c d", c=2)).then_inc(m.w2_full[e], 16)

    @block.tensor
    def _(pe):
        pe.wait_ge(s.loads, s.loaded)
        for t in range(T):
            for k in range(KD):
                mm = narrow_matmul(pe, ps[:, 0, t * 36:(t + 1) * 36], s.hT[:, k, t * P:(t + 1) * P], rw[:, k, :],
                                   start=(k == 0), stop=(k == KD - 1))
        mm.then_inc(S["lg_ps"], 1)
        pe.wait_ge(S["sel"], 1)
        for t in range(T):
            for b in range(t):
                narrow_matmul(pe, ps[:, 1, t * NE:(t + 1) * NE], s.cid("ones"), sel[:, b, :], start=(b == 0), stop=False)
            narrow_matmul(pe, ps[:, 1, t * NE:(t + 1) * NE], s.cid("before"), sel[:, t, :], start=(t == 0), stop=True)
        for t in range(T):
            mm = narrow_matmul(pe, ps[:, 1, T * NE:(T + 1) * NE], s.cid("ones"), sel[:, t, :], start=(t == 0), stop=(t == T - 1))
        mm.then_inc(S["rank_ps"], 1)

    @block.scalar
    def _(act):
        act.wait_ge(S["x4"], 1)
        nc.scalar.activation(v4[:, :, :], v4[:, :, :], ACT.Exp).then_inc(S["e4"], 1)
        act.wait_ge(S["x2"], 1)
        nc.scalar.activation(w2[:, :, :], w2[:, :, :], ACT.Exp).then_inc(S["e2"], 1)

    @block.vector
    def _(dve):
        v = nc.vector

        def do(ins):
            link(s, "dve", dve, ins)

        def wide(a, n):
            return a.broadcast_to([P, T, n])

        def first_of(dst, values, most, order, n):
            e = eq[:, :, 0:n]
            do(v.tensor_tensor(e, values, wide(most, n), ALU.is_equal))
            do(v.tensor_tensor(e, e, order.unsqueeze(1).broadcast_to([P, T, n]), ALU.mult))
            do(v.tensor_reduce(t1[:, :, :], e, AX.X, ALU.max))
            do(v.tensor_tensor(dst, e, wide(t1[:, :, :], n), ALU.is_equal))

        dve.wait_ge(s.loads, s.loaded)
        dve.wait_ge(S["lg_ps"], 1)
        do(v.tensor_tensor(lg[:, :, :], ps[:, 0, 0:T * 36].rearrange("p (t n) -> p t n", t=T), rb[:, :].unsqueeze(1).broadcast_to([P, T, 36]), ALU.add))
        grp = lg[:, :, 0:NG]
        do(v.tensor_reduce(mx[:, :, :], grp, AX.X, ALU.max))
        v.tensor_tensor(v4[:, :, :], grp, wide(mx[:, :, :], NG), ALU.subtract).then_inc(S["x4"], 1)
        first_of(oh4[:, :, :], grp, mx[:, :, :], s.cid("rank4"), NG)
        do(v.tensor_scalar(oh4[:, :, :], oh4[:, :, :], -1.0, BIG, ALU.add, ALU.mult))
        do(v.tensor_copy(le[:, :, :], lg[:, :, NG:]))
        for t in range(T):
            le_t = le[:, t, :].rearrange("p (g e) -> p g e", g=NG)
            do(v.tensor_tensor(le_t, le_t, oh4[:, t, :].unsqueeze(2).broadcast_to([P, NG, PER]), ALU.add))
        do(v.tensor_reduce(m1[:, :, :], le[:, :, :], AX.X, ALU.max))
        first_of(oh1[:, :, :], le[:, :, :], m1[:, :, :], s.cid("rank32"), NE)
        do(v.scalar_tensor_tensor(out=le[:, :, :], in0=oh1[:, :, :], scalar=-3 * BIG, in1=le[:, :, :], op0=ALU.mult, op1=ALU.add))
        do(v.tensor_reduce(m2[:, :, :], le[:, :, :], AX.X, ALU.max))
        first_of(oh2[:, :, :], le[:, :, :], m2[:, :, :], s.cid("rank32"), NE)
        v.tensor_tensor(w2[:, :, :], m2[:, :, :], m1[:, :, :], ALU.subtract).then_inc(S["x2"], 1)
        v.tensor_tensor(sel[:, :, :], oh1[:, :, :], oh2[:, :, :], ALU.add).then_inc(S["sel"], 1)
        dve.wait_ge(S["e4"], 1)
        do(v.tensor_reduce(ptop[:, :, :], v4[:, :, :], AX.X, ALU.add))
        dve.wait_ge(S["e2"], 1)
        do(v.tensor_scalar(w1[:, :, :], w2[:, :, :], 1.0, None, ALU.add))
        do(v.tensor_tensor(w1[:, :, :], w1[:, :, :], ptop[:, :, :], ALU.mult))
        do(v.reciprocal(w1[:, :, :], w1[:, :, :]))
        do(v.tensor_tensor(w2[:, :, :], w2[:, :, :], w1[:, :, :], ALU.mult))
        do(v.tensor_tensor(oh1[:, :, :], oh1[:, :, :], wide(w1[:, :, :], NE), ALU.mult))
        do(v.tensor_tensor(oh2[:, :, :], oh2[:, :, :], wide(w2[:, :, :], NE), ALU.mult))
        do(v.tensor_tensor(m.gates[:, :, :], oh1[:, :, :], oh2[:, :, :], ALU.add))
        dve.wait_ge(S["sel"], 1)
        dve.wait_ge(S["rank_ps"], 1)
        do(v.scalar_tensor_tensor(out=m.code[:, :, :], in0=ps[:, 1, 0:T * NE].rearrange("p (t n) -> p t n", t=T), scalar=1.0,
                                  in1=sel[:, :, :], op0=ALU.add, op1=ALU.mult))
        do(v.tensor_scalar(m.code[:, :, :], m.code[:, :, :], -1.0, None, ALU.add))
        do(v.tensor_reduce(top[:, :], ps[:, 1, T * NE:(T + 1) * NE], AX.X, ALU.max))
        do(v.tensor_copy(m.most[:, :], top[0:1, :]))


class PairSteps:

    NAMES = ("onehot", "gate_in", "gt_ps", "gt_ev", "hg_ps", "hg_ev", "h_ps", "silu", "hid", "ht_ps", "ht_ev", "o_ps", "o_ev", "lo_ev", "sc_ps", "sc_ev")

    def __init__(self, s, m, bufs, sems, deep, wide):
        self.s, self.m, self.b, self.S, self.deep, self.wide = s, m, bufs, sems, deep, wide

    def wait(self, eng, name, value, at_least=1):
        if at_least > 0:
            eng.wait_ge(self.S[name], value)

    def onehot(self, dve, i, n, g, j, n0):
        v, m = self.s.nc.vector, self.m
        back = self.deep * self.wide
        halves = 2 // self.wide
        self.wait(dve, "hg_ps", halves * (n - j + self.wide - back), n0 - j + self.wide - back)
        self.wait(dve, "gt_ps", n + 1 - back, n0 + 1 - back)
        for e in range(2):
            c = j * P + e * SLOTS
            v.tensor_tensor(self.b.onehot[:, g, :, c:c + SLOTS],
                            self.s.cid("slot_no")[:, 0:SLOTS].unsqueeze(1).broadcast_to([P, T, SLOTS]),
                            m.code[:, :, bass.ds(2 * i + e, 1)].broadcast_to([P, T, SLOTS]), ALU.is_equal).then_inc(self.S["onehot"], 1)

    def take_gates(self, dve, i, n, b, n0):
        self.wait(dve, "gt_ps", n + 1 - self.deep, n0 + 1 - self.deep)
        self.s.nc.vector.tensor_copy(self.b.turn[:, b, :, P:P + 2], self.m.gates[:, :, bass.ds(2 * i, 2)]).then_inc(self.S["gate_in"], 1)

    def take_turned(self, dve, n, b, n0):
        v = self.s.nc.vector
        dve.wait_ge(self.S["gt_ps"], n + 1)
        self.wait(dve, "sc_ps", 6 * (n + 1 - self.deep), n0 + 1 - self.deep)
        turned = self.s.ps[:, 3, 0:T * (P + 2)].rearrange("p (t c) -> p t c", t=T)
        v.tensor_copy(self.b.onehot_t[:, b, :].rearrange("p (t n) -> p t n", t=T), turned[:, :, 0:P]).then_inc(self.S["gt_ev"], 1)
        for e in range(2):
            q = slice(e * SLOTS, (e + 1) * SLOTS)
            v.tensor_reduce(self.b.slot_gate[q, b:b + 1], turned[q, :, P + e:P + e + 1].rearrange("p t c -> p c t"), AX.X, ALU.add).then_inc(self.S["gt_ev"], 1)

    def hidden(self, dve, n, b):
        dve.wait_ge(self.S["silu"], n + 1)
        dve.wait_ge(self.S["gt_ev"], 3 * (n + 1))
        self.s.nc.vector.scalar_tensor_tensor(out=self.b.hid[:, :], in0=self.s.ps[:, 2, FE:2 * FE], scalar=self.b.slot_gate[:, b:b + 1],
                                              in1=self.b.silu[:, :], op0=ALU.mult, op1=ALU.mult).then_inc(self.S["hid"], 1)

    def take_hidden(self, dve, n, n0):
        dve.wait_ge(self.S["ht_ps"], n + 1)
        self.wait(dve, "o_ps", 2 * n, n0)
        self.s.nc.vector.tensor_copy(self.b.hid_t[:, :], self.s.ps[:, 2, 0:2 * P]).then_inc(self.S["ht_ev"], 1)

    def out_low(self, dve, n, b, n0):
        self.wait(dve, "sc_ps", 6 * (n + 1 - self.deep), n0 + 1 - self.deep)
        for h in range(2):
            c = slice(h * BANK, (h + 1) * BANK)
            dve.wait_ge(self.S["o_ev"], 2 * n + h + 1)
            self.s.nc.vector.tensor_tensor(self.b.o_lo[:, b, c], self.s.ps[:, 5 + h, :], self.b.o_hi[:, b, c].bitcast(F32),
                                           ALU.subtract).then_inc(self.S["lo_ev"], 1)

    def add_tokens(self, dve, n):
        v, acc = self.s.nc.vector, self.m.acc
        for q in range(6):
            t, h = divmod(q, 2)
            dve.wait_ge(self.S["sc_ps"], 6 * n + q + 1)
            a = acc[:, t, h * BANK:(h + 1) * BANK]
            v.tensor_tensor(a, a, self.s.ps[:, 4 if q % 2 else 7, :], ALU.add).then_inc(self.S["sc_ev"], 1)

    def gathered(self, x):
        return self.s.ps[:, 0:2, :].rearrange("p b (k n) -> p (b k) n", k=2)[:, :, 0:x]

    def take_gathered(self, act, h, g, half, h0):
        act.wait_ge(self.S["hg_ps"], h + 1)
        self.wait(act, "h_ps", self.wide * (h - half) + 2 * self.wide * (1 - self.deep), h0 - half + 2 * (1 - self.deep))
        n = self.wide * P
        self.s.nc.scalar.copy(self.b.hg[:, g, 4 * half:4 * half + 4, 0:n], self.gathered(n)).then_inc(self.S["hg_ev"], 1)

    def silu(self, act, n, n0):
        act.wait_ge(self.S["h_ps"], 2 * (n + 1))
        self.wait(act, "hid", n, n0)
        self.s.nc.scalar.activation(self.b.silu[:, :], self.s.ps[:, 2, 0:FE], ACT.Silu).then_inc(self.S["silu"], 1)

    def take_out(self, act, n, b, n0):
        act.wait_ge(self.S["o_ps"], 2 * (n + 1))
        self.wait(act, "sc_ps", 6 * (n + 1 - self.deep), n0 + 1 - self.deep)
        for h in range(2):
            self.s.nc.scalar.copy(self.b.o_hi[:, b, h * BANK:(h + 1) * BANK], self.s.ps[:, 5 + h, :]).then_inc(self.S["o_ev"], 1)

    def turn_onehot(self, pe, n, b, g, j, n0):
        ps, oh = self.s.ps, self.b.onehot
        pe.wait_ge(self.S["onehot"], 2 * (n + 1))
        pe.wait_ge(self.S["gate_in"], n + 1)
        self.wait(pe, "gt_ev", 3 * n, n0)
        for t in range(T):
            mm = pe.matmul(ps[:, 3, t * (P + 2):(t + 1) * (P + 2)], oh[:, g, t, j * P:(j + 1) * P].bitcast(F32), self.b.turn[:, b, t, :], start=True, stop=True)
        mm.then_inc(self.S["gt_ps"], 1)

    def gather(self, pe, h, g, half, h0):
        pe.wait_ge(self.S["onehot"], self.wide * (h - half) + 2 * self.wide)
        self.wait(pe, "hg_ev", h, h0)
        n = self.wide * P
        for k in range(4):
            for t in range(T):
                for part in (0, 1):
                    mm = pe.matmul(self.gathered(n)[:, k, :], self.m.hp[part][:, t, 4 * half + k, :], self.b.onehot[:, g, t, 0:n],
                                   start=(t + part == 0), stop=(t + part == T))
        mm.then_inc(self.S["hg_ps"], 1)

    def hidden_products(self, pe, n, g, j, n0, w13, ready):
        ps = self.s.ps
        pe.wait_ge(self.S["hg_ev"], n - j + 2 if self.wide == 2 else 2 * n + 2)
        self.wait(pe, "ht_ev", n, n0)
        for e, k in self.order(pe, ready, range(KD)):
            c = j * P + e * SLOTS
            mm = pe.matmul(ps[e * SLOTS:(e + 1) * SLOTS, 2, :], self.b.hg[:, g, k, c:c + SLOTS],
                           w13(e)[:, k, :], start=(k == 0), stop=(k == KD - 1))
            if k == KD - 1:
                mm.then_inc(self.S["h_ps"], 1)

    def order(self, pe, ready, steps):
        if self.deep == 1:
            for e in range(2):
                ready(pe, e)
                for x in steps:
                    yield e, x
        else:
            ready(pe, 0)
            ready(pe, 1)
            for x in steps:
                yield 0, x
                yield 1, x

    def turn_hidden(self, pe, n):
        pe.wait_ge(self.S["hid"], n + 1)
        for c in range(2):
            mm = pe.transpose(self.s.ps[:, 2, c * P:(c + 1) * P], self.b.hid[:, c::2], self.s.ident)
        mm.then_inc(self.S["ht_ps"], 1)

    def out_products(self, pe, n, n0, w2, ready, halves=(0, 1)):
        pe.wait_ge(self.S["ht_ev"], n + 1)
        self.wait(pe, "lo_ev", 2 * n, n0)
        for e, (h, c) in self.order(pe, ready, [(h, c) for h in halves for c in range(2)]):
            mm = pe.matmul(self.s.ps[e * SLOTS:(e + 1) * SLOTS, 5 + h, :], self.b.hid_t[:, c * P + e * SLOTS:c * P + (e + 1) * SLOTS],
                           w2(e)[:, c, h * BANK:(h + 1) * BANK], start=(c == 0), stop=(c == 1))
            if (h, c) == (1, 1):
                mm.then_inc(self.S["o_ps"], 1)

    def scatter(self, pe, n, b, n0, parts=range(6)):
        pe.wait_ge(self.S["lo_ev"], 2 * (n + 1))
        pe.wait_ge(self.S["gt_ev"], 3 * (n + 1))
        for q in parts:
            t, h = divmod(q, 2)
            if q >= 2 or n0 > 0:
                pe.wait_ge(self.S["sc_ev"], 6 * n + q - 1)
            for part in (self.b.o_hi, self.b.o_lo):
                mm = pe.matmul(self.s.ps[:, 4 if q % 2 else 7, :], self.b.onehot_t[:, b, t * P:(t + 1) * P],
                               part[:, b, h * BANK:(h + 1) * BANK], start=(part is self.b.o_hi), stop=(part is self.b.o_lo))
            mm.then_inc(self.S["sc_ps"], 1)


def experts(s, l, st, m):
    nc, w = s.nc, s.w
    sb = stage_buffers(s, st, f"ex{l}_")

    def buffers(pre, deep):
        b = Shared()
        b.onehot = sb(pre + "onehot", [P, deep, T, 2 * P], F32R)
        b.turn = sb(pre + "turn", [P, deep, T, P + 2])
        b.onehot_t = sb(pre + "onehot_t", [P, deep, NTOK], F32R)
        b.slot_gate = sb(pre + "slot_gate", [P, deep])
        b.hg = sb(pre + "hg", [P, deep, KD, 2 * P])
        b.silu, b.hid = sb(pre + "silu", [P, FE]), sb(pre + "hid", [P, FE])
        b.hid_t = sb(pre + "hid_t", [P, 2 * P])
        b.o_hi, b.o_lo = (sb(pre + n, [P, deep, D], F32R) for n in ("o_hi", "o_lo"))
        return b

    w2_ring, w2_full = m.w2_ring, m.w2_full
    bufs = buffers("", 2)
    over_w = w2_ring[:, 2:4, :, :].rearrange("p e c (h n) -> p (e c h) n", n=BANK)
    S = {n: s.sem(f"ex{l}_" + n) for n in PairSteps.NAMES}
    V = {n: s.sem(f"ov{l}_" + n) for n in PairSteps.NAMES}
    zeroed, shifted, ov_w13, ov_w2 = (s.sem(f"ex{l}_" + n) for n in ("zeroed", "shifted", "ov_w13", "ov_w2"))
    base = s.at["moe", l]
    main = PairSteps(s, m, bufs, S, 2, 2)
    over = PairSteps(s, m, bufs, V, 1, 1)
    w1v = w["moe_w1"][l].rearrange("e (p k) f -> p e k f", k=KD)
    w3v = w["moe_w3"][l].rearrange("e (p k) f -> p e k f", k=KD)
    w2v = w["moe_w2"][l].rearrange("e (p c) d -> p e c d", c=2)
    block = st.enter_context(nc.Block())

    def engine_rounds(eng, steps, before):
        most = eng.value_load(m.most[0:1, 0:1], min_val=0, max_val=NTOK)
        with eng.If(most > SLOTS):
            eng.wait_ge(S["sc_ev"], 6 * PAIRS)
            for r in range(1, ROUNDS):
                before()
                first = PAIRS * (r - 1)
                steps(0, first, first)
                with eng.Fori(1, PAIRS) as i:
                    steps(i, first + i, first + 1)

    @block.gpsimd
    def _(pool):
        for b in range(2):
            for t in range(T):
                nc.gpsimd.tensor_copy(bufs.turn[:, b, t, 0:P], s.ident).then_inc(zeroed, 1)
        nc.gpsimd.memset(m.acc[:, :, :], 0.0).then_inc(zeroed, 1)

    @block.sync
    def _(sp):
        def w13_load(dst, ex, done):
            for src, c in ((w1v, 0), (w3v, FE)):
                sp.dma_start(dst[:, :, c:c + FE], src[:, bass.ds(ex, 1)].rearrange("p e k f -> p (e k) f")).then_inc(done, 16)

        def w2_load(dst, ex, done):
            sp.dma_start(dst, w2v[:, bass.ds(ex, 1)].rearrange("p e c d -> p (e c) d")).then_inc(done, 16)

        for e in range(4):
            slot = s.slot_of[base + e]
            if s.issued <= base + e:
                sp.wait_ge(s.ring_free, base + e - SLOT_RING + 1)
                w13_load(s.ring[:, slot], e, s.ring_full[slot])
        with sp.Fori(0, NE // 4 - 1) as q:
            for e in range(4):
                slot = s.slot_of[base + e]
                sp.wait_ge(S["h_ps"], 4 * q + e + 1)
                w13_load(s.ring[:, slot], 4 * q + 4 + e, s.ring_full[slot])
                sp.wait_ge(S["o_ps"], 4 * q + e + 1)
                w2_load(w2_ring[:, e], 4 * q + 4 + e, w2_full[e])
        s.issued = base + NE
        ring_loads(s, sp, base + NE + SLOT_RING)
        sp.wait_ge(S["o_ps"], NE)

        def steps(i, n, n0):
            for e in range(2):
                if n0 + e > 0:
                    sp.wait_ge(V["h_ps"], 2 * n + e)
                w13_load(over_w, 2 * i + e, ov_w13)
                if n0 + e > 0:
                    sp.wait_ge(V["o_ps"], 2 * n + e)
                w2_load(w2_ring[:, 0], 2 * i + e, ov_w2)

        engine_rounds(sp, steps, lambda: None)

    @block.tensor
    def _(pe):
        def step(i, p, j):
            n0, b = p, p % 2
            def w13_ready(eng, e):
                x = 2 * p + e
                eng.wait_ge(s.ring_full[s.slot_of[base + x]], s.fill_of[base + x] + 32 * j)

            def w2_ready(eng, e):
                x = 2 * p + e
                eng.wait_ge(w2_full[x % 4], 16 * (x // 4 + 1) + 16 * j)

            g, place = (p // 2) % 2, p % 2
            main.hidden_products(pe, i, g, place, n0, lambda e: s.ring[:, s.slot_of[base + 2 * p + e]], w13_ready)
            if p < PAIRS - 2:
                main.gather(pe, i + 2, 1 - g, place, n0 + 2)
            if p < PAIRS - 1:
                main.turn_onehot(pe, i + 1, 1 - b, ((p + 1) // 2) % 2, 1 - place, n0 + 1)
            main.turn_hidden(pe, i)
            for h in range(2):
                if p > 0:
                    main.scatter(pe, i - 1, 1 - b, n0 - 1, (2 * h, 2 * h + 1))
                main.out_products(pe, i, n0, lambda e: w2_ring[:, (2 * p + e) % 4], w2_ready, (h,))
            if p > 0:
                main.scatter(pe, i - 1, 1 - b, n0 - 1, (4, 5))

        pe.wait_ge(zeroed, 2 * T)
        main.gather(pe, 0, 0, 0, 0)
        main.gather(pe, 1, 0, 1, 1)
        main.turn_onehot(pe, 0, 0, 0, 0, 0)
        for p in range(TURN):
            step(p, p, 0)
        with pe.Fori(0, TURNS) as j:
            for p in range(TURN, 2 * TURN):
                step(TURN * j + p, p, 2 * j)
        for p in range(PAIRS - TURN, PAIRS):
            step(p, p, 0)
        main.scatter(pe, PAIRS - 1, (PAIRS - 1) % 2, PAIRS - 1)
        pe.wait_ge(S["h_ps"], NE)
        pe.sem_inc(s.ring_free, NE)

        def steps(i, n, n0):
            for half in range(2):
                over.gather(pe, 2 * n + half, 0, half, 2 * n0 + half)
            over.turn_onehot(pe, n, 0, 0, 0, n0)
            over.hidden_products(pe, n, 0, 0, n0, lambda e: over_w, lambda eng, e: eng.wait_ge(ov_w13, 64 * n + 32 * (e + 1)))
            over.turn_hidden(pe, n)
            over.out_products(pe, n, n0, lambda e: w2_ring[:, 0], lambda eng, e: eng.wait_ge(ov_w2, 32 * n + 16 * (e + 1)))
            over.scatter(pe, n, 0, n0)

        engine_rounds(pe, steps, lambda: None)

    @block.scalar
    def _(act):
        def step(i, p):
            main.silu(act, i, p)
            if p < PAIRS - 2:
                main.take_gathered(act, i + 2, (p // 2 + 1) % 2, p % 2, p + 2)
            main.take_out(act, i, p % 2, p)

        main.take_gathered(act, 0, 0, 0, 0)
        main.take_gathered(act, 1, 0, 1, 1)
        for p in range(TURN):
            step(p, p)
        with act.Fori(0, TURNS) as j:
            for p in range(TURN, 2 * TURN):
                step(TURN * j + p, p)
        for p in range(PAIRS - TURN, PAIRS):
            step(p, p)

        def steps(i, n, n0):
            for half in range(2):
                over.take_gathered(act, 2 * n + half, 0, half, 2 * n0 + half)
            over.silu(act, n, n0)
            over.take_out(act, n, 0, n0)

        engine_rounds(act, steps, lambda: None)

    @block.vector
    def _(dve):
        def step(i, p):
            if p > 0:
                main.out_low(dve, i - 1, (p - 1) % 2, p - 1)
            main.hidden(dve, i, p % 2)
            main.take_hidden(dve, i, p)
            if p > 0:
                main.add_tokens(dve, i - 1)
            if p < PAIRS - 1:
                main.take_turned(dve, i + 1, (p + 1) % 2, p + 1)
            if p < PAIRS - 2:
                main.take_gates(dve, i + 2, i + 2, p % 2, p + 2)
            if p < PAIRS - 4:
                main.onehot(dve, i + 4, i + 4, (p // 2) % 2, p % 2, p + 4)

        for p in range(4):
            main.onehot(dve, p, p, p // 2, p % 2, p)
        for p in range(2):
            main.take_gates(dve, p, p, p, p)
        main.take_turned(dve, 0, 0, 0)
        dve.wait_ge(zeroed, 2 * T + 1)
        for p in range(TURN):
            step(p, p)
        with dve.Fori(0, TURNS) as j:
            for p in range(TURN, 2 * TURN):
                step(TURN * j + p, p)
        for p in range(PAIRS - TURN, PAIRS):
            step(p, p)
        main.out_low(dve, PAIRS - 1, (PAIRS - 1) % 2, PAIRS - 1)
        main.add_tokens(dve, PAIRS - 1)

        rounds = [0]

        def next_round():
            rounds[0] += 1
            if rounds[0] > 1:
                dve.wait_ge(V["hg_ps"], 2 * PAIRS * (rounds[0] - 1))
            nc.vector.tensor_scalar(m.code[:, :, :], m.code[:, :, :], -float(SLOTS), None, ALU.add).then_inc(shifted, 1)
            dve.wait_ge(shifted, rounds[0])

        def steps(i, n, n0):
            over.onehot(dve, i, n, 0, 0, n0)
            over.take_gates(dve, i, n, 0, n0)
            over.take_turned(dve, n, 0, n0)
            over.hidden(dve, n, 0)
            over.take_hidden(dve, n, n0)
            over.out_low(dve, n, 0, n0)
            over.add_tokens(dve, n)

        engine_rounds(dve, steps, next_round)


TURN = 4
TURNS = PAIRS // TURN - 2


def add_moe(s, l, st, m):
    nc, ps = s.nc, s.ps
    g_ps, mul, added = (s.sem(f"am{l}_" + n) for n in ("g_ps", "mul", "added"))
    rows = slice(32 * l, 32 * l + 2)
    block = st.enter_context(nc.Block())

    @block.tensor
    def _(pe):
        for g in range(2):
            for h in range(2):
                mm = pe.matmul(ps[:, 2 * g + h, :], s.cid("pick")[rows, g * P:(g + 1) * P], s.gates[rows, FFN, h * BANK:(h + 1) * BANK],
                               start=True, stop=True)
            mm.then_inc(g_ps, 1)

    @block.vector
    def _(dve):
        v = nc.vector
        for t in range(T):
            g = min(t, 1)
            dve.wait_ge(g_ps, g + 1)
            for h in range(2):
                a = m.acc[:, t, h * BANK:(h + 1) * BANK]
                v.tensor_tensor(a, a, ps[:, 2 * g + h, :], ALU.mult).then_inc(mul, 1)
            for h in range(2):
                dve.wait_ge(mul, 2 * t + h + 1)
                ys = s.y[:, t, h * BANK:(h + 1) * BANK]
                v.tensor_tensor(ys, ys, m.acc[:, t, h * BANK:(h + 1) * BANK], ALU.add).then_inc(added, 1)

    @block.sync
    def _(sp):
        if l == 1:
            for t in range(T):
                dst = s.out["y_prompt"][0] if t == 0 else s.out["y_sample"][0, (t - 1) * P:t * P]
                sp.wait_ge(added, 2 * (t + 1))
                sp.dma_start(dst, s.y[:, t, :]).then_inc(s.stores, 16)
            s.stored += 16 * T
            sp.wait_ge(s.stores, s.stored)


_INS = ["x_prompt", "x_sample", "cache_a_k", "cache_a_v", "cache_b_ckv", "cache_b_krope", "state_c_fwd", "state_c_bwd",
        "c", "c_ctx", "ada_w", "ada_b", "norm_mix", "norm_ffn",
        "att_w_in", "att_a_qnorm", "att_a_knorm", "att_a_sink", "att_b_qa_norm", "att_b_wuq", "att_b_kva_norm",
        "att_b_wukv", "att_b_qnorm", "att_b_knorm", "att_w_out",
        "ssd_w_in", "ssd_conv_w", "ssd_conv_b", "ssd_alog_fwd", "ssd_alog_bwd", "ssd_dtb_fwd", "ssd_dtb_bwd", "ssd_d",
        "ssd_norm", "ssd_w_out", "moe_wg", "moe_bg", "moe_we", "moe_be", "moe_w1", "moe_w3", "moe_w2"]
_OUTS = [("y_prompt", (1, 128, 1024)), ("y_sample", (1, 256, 1024)), ("new_a_k", (1, 1, 128, 2, 64)),
         ("new_a_v", (1, 1, 128, 2, 64)), ("new_b_ckv", (1, 1, 128, 128)), ("new_b_krope", (1, 1, 128, 32)),
         ("new_state_fwd", (1, 1, 32, 64, 128)), ("new_state_bwd", (1, 1, 32, 64, 128))]


def kernel(**inputs):
    import concourse.bacc as _bacc
    from concourse.bass_utils import run_bass_kernel_spmd as _run

    nc = _bacc.Bacc("TRN2", target_bir_lowering=False, num_devices=1)
    arrays, ins, outs = {}, {}, {}
    given = {name: inputs[name] for name in _INS}
    given["consts"] = const_table()[0]
    for name, value in given.items():
        a = np.ascontiguousarray(value)
        arrays[f"in_{name}_dram"] = a
        ins[name] = nc.dram_tensor(f"in_{name}_dram", a.shape, mybir.dt.from_np(a.dtype), kind="ExternalInput").ap()
    for name, shape in _OUTS:
        outs[name] = nc.dram_tensor(f"out_{name}_dram", shape, F32, kind="ExternalOutput").ap()
    build(nc, ins, outs)
    r = _run(nc, [arrays], core_ids=[0])
    return tuple(r.results[0][f"out_{name}_dram"] for name, _ in _OUTS)
```
